# Optimizing a Trainium2 kernel written in Bass

```python
import math
import numpy as np
import jax
import jax.numpy as jnp
from jax import lax

D_MODEL = 1024
BATCH = 1
SEQ = 512
DEPTH = 2

CTX_LEN = 256
GRID_W = 64
N_EVEN = (DEPTH + 1) // 2
N_ODD = DEPTH // 2

SSD_HEADS = 16
SSD_HEAD_DIM = 64
SSD_WIDTH = SSD_HEADS * SSD_HEAD_DIM
SSD_GROUPS = 2
SSD_STATE = 128
SSD_CHUNK = 128
CONV_K = 5
CONV_CH = SSD_WIDTH + 2 * SSD_GROUPS * SSD_STATE

GLA_HEADS = 4
GLA_KEY_DIM = 128
GLA_VAL_DIM = 256
GLA_K = GLA_HEADS * GLA_KEY_DIM
GLA_V = GLA_HEADS * GLA_VAL_DIM
GLA_RANK = 16
GLA_GATE_NORMALIZER = 16.0
GLA_CHUNK = 64

E_SPLITS = (SSD_WIDTH, CONV_CH, 2 * SSD_HEADS, GLA_K, GLA_K, GLA_V, GLA_V, 2 * GLA_RANK)
E_IN = SSD_WIDTH + CONV_CH + 2 * SSD_HEADS + 2 * GLA_K + 2 * GLA_V + 2 * GLA_RANK
E_MIX = SSD_WIDTH + GLA_V

ATT_HEADS = 16
ATT_KV_HEADS = 4
ATT_GROUP = ATT_HEADS // ATT_KV_HEADS
ATT_HEAD_DIM = 128
ATT_W = ATT_HEADS * ATT_HEAD_DIM
ATT_KV_W = ATT_KV_HEADS * ATT_HEAD_DIM
WINDOW = 128
ATT_BLOCK = 128
ROPE_BASE = 10000.0
ROPE_FREQS = ATT_HEAD_DIM // 4
O_IN = 2 * ATT_KV_W + 2 * ATT_W
NORM_EPS = 1e-6

kernel_name = 'hybrid_ssd_gla_swa_ctxprefix'

def rms_norm(t, g):
    tf = t.astype(jnp.float32)
    y = tf * lax.rsqrt(jnp.mean(tf * tf, axis=-1, keepdims=True) + NORM_EPS)
    return (y * g.astype(jnp.float32)).astype(t.dtype)

def split_cols(t, sizes):
    idx = np.cumsum(np.array(sizes))[:-1].tolist()
    return jnp.split(t, idx, axis=-1)

def _flip(t):
    return jnp.flip(t, axis=1)

def adaln(cvec, w, b):
    mod = (jnp.dot(jax.nn.silu(cvec), w) + b)[:, None, :]
    return jnp.split(mod, 3, axis=-1)

def centered_dwconv(t, w, b):
    half = (w.shape[0] - 1) // 2
    out = lax.conv_general_dilated(t, w.astype(t.dtype)[:, None, :], window_strides=(1,), padding=[(half, half)],
                                   dimension_numbers=('NWC', 'WIO', 'NWC'), feature_group_count=t.shape[-1])
    return out + b.astype(t.dtype)

def ssd_scan(xs, dt, a, bm, cm, init):
    bsz, seq, _, hd = xs.shape
    T = SSD_CHUNK
    nc = seq // T
    G, R, N = SSD_GROUPS, SSD_HEADS // SSD_GROUPS, SSD_STATE
    xdt = (xs * dt[..., None]).reshape(bsz, nc, T, G, R, hd)
    cs = jnp.cumsum((dt * a).reshape(bsz, nc, T, G, R), axis=2)
    bm = bm.reshape(bsz, nc, T, G, N)
    cm = cm.reshape(bsz, nc, T, G, N)
    incl = jnp.tril(jnp.ones((T, T), bool))[:, :, None, None]
    seg = jnp.exp(jnp.where(incl, cs[:, :, :, None] - cs[:, :, None, :], -jnp.inf))
    cb = jnp.einsum('bcign,bcjgn->bcijg', cm, bm)
    y_diag = jnp.einsum('bcijg,bcijgr,bcjgrp->bcigrp', cb, seg, xdt)
    u = jnp.einsum('bctgn,bctgr,bctgrp->bcgrpn', bm, jnp.exp(cs[:, :, -1:] - cs), xdt)
    chunk_decay = jnp.exp(cs[:, :, -1])

    def step(state, inp):
        d, uc = inp
        return d[..., None, None] * state + uc, state

    final, starts = lax.scan(step, init, (jnp.moveaxis(chunk_decay, 1, 0), jnp.moveaxis(u, 1, 0)))
    starts = jnp.moveaxis(starts, 0, 1)
    y_off = jnp.einsum('bcign,bcigr,bcgrpn->bcigrp', cm, jnp.exp(cs), starts)
    return (y_diag + y_off).reshape(bsz, seq, SSD_HEADS, hd), final

def ssd_mixer(z, xbc, dt_raw, conv_w, conv_b, dt_bias, a_log, d_skip, norm_g, init):
    bsz, seq, _ = z.shape
    xbc = jax.nn.silu(centered_dwconv(xbc, conv_w, conv_b))
    xs, bm, cm = split_cols(xbc, (SSD_WIDTH, SSD_GROUPS * SSD_STATE, SSD_GROUPS * SSD_STATE))
    xs = xs.reshape(bsz, seq, SSD_HEADS, SSD_HEAD_DIM)
    bm = bm.reshape(bsz, seq, SSD_GROUPS, SSD_STATE)
    cm = cm.reshape(bsz, seq, SSD_GROUPS, SSD_STATE)
    dt = jax.nn.softplus(dt_raw.reshape(bsz, seq, 2, SSD_HEADS) + dt_bias.astype(jnp.float32))
    a = -jnp.exp(a_log.astype(jnp.float32))
    y_f, fin_f = ssd_scan(xs, dt[:, :, 0], a[0], bm, cm, init[0])
    y_b, fin_b = ssd_scan(_flip(xs), _flip(dt[:, :, 1]), a[1], _flip(bm), _flip(cm), init[1])
    y = y_f + _flip(y_b) + d_skip.astype(jnp.float32)[:, None] * xs
    gsz = SSD_WIDTH // SSD_GROUPS
    y = y.reshape(bsz, seq, SSD_GROUPS, gsz) * jax.nn.silu(z).reshape(bsz, seq, SSD_GROUPS, gsz)
    y = rms_norm(y, norm_g.reshape(SSD_GROUPS, gsz))
    return y.reshape(bsz, seq, SSD_WIDTH), (fin_f, fin_b)

def gla_scan(q, k, v, lg, init):
    bsz, seq, nh, dk = q.shape
    dv = v.shape[-1]
    T = GLA_CHUNK
    nc = seq // T
    q = q.reshape(bsz, nc, T, nh, dk) * (dk ** -0.5)
    k = k.reshape(bsz, nc, T, nh, dk)
    v = v.reshape(bsz, nc, T, nh, dv)
    cs = jnp.cumsum(lg.reshape(bsz, nc, T, nh, dk), axis=2)
    q_dec = q * jnp.exp(cs)
    att = jnp.einsum('bcihd,bcjhd->bchij', q_dec, k * jnp.exp(-cs))
    att = jnp.where(jnp.tril(jnp.ones((T, T), bool)), att, 0.0)
    o_intra = jnp.einsum('bchij,bcjhe->bcihe', att, v)
    u = jnp.einsum('bcthd,bcthe->bchde', k * jnp.exp(cs[:, :, -1:] - cs), v)
    chunk_decay = jnp.exp(cs[:, :, -1])

    def step(state, inp):
        d, uc = inp
        return d[..., None] * state + uc, state

    final, starts = lax.scan(step, init, (jnp.moveaxis(chunk_decay, 1, 0), jnp.moveaxis(u, 1, 0)))
    starts = jnp.moveaxis(starts, 0, 1)
    o_inter = jnp.einsum('bcthd,bchde->bcthe', q_dec, starts)
    return (o_intra + o_inter).reshape(bsz, seq, nh, dv), final

def gla_mixer(q, k, v, g, g_lr, gate_w, gate_b, norm_g, init):
    bsz, seq, _ = q.shape
    lr = g_lr.reshape(bsz, seq, 2, GLA_RANK)
    logits = jnp.einsum('bldr,drk->bldk', lr, gate_w.astype(jnp.float32)) + gate_b.astype(jnp.float32)
    lg = (jax.nn.log_sigmoid(logits) / GLA_GATE_NORMALIZER).reshape(bsz, seq, 2, GLA_HEADS, GLA_KEY_DIM)
    qh = q.reshape(bsz, seq, GLA_HEADS, GLA_KEY_DIM)
    kh = k.reshape(bsz, seq, GLA_HEADS, GLA_KEY_DIM)
    vh = v.reshape(bsz, seq, GLA_HEADS, GLA_VAL_DIM)
    o_f, fin_f = gla_scan(qh, kh, vh, lg[:, :, 0], init[0])
    o_b, fin_b = gla_scan(_flip(qh), _flip(kh), _flip(vh), _flip(lg[:, :, 1]), init[1])
    o = rms_norm(o_f + _flip(o_b), norm_g.reshape(GLA_HEADS, GLA_VAL_DIM)).reshape(bsz, seq, GLA_V)
    return o * jax.nn.silu(g), (fin_f, fin_b)

def even_layer(x, xc, c, c_ctx, norm_g, mod_w, mod_b, w_in, conv_w, conv_b, dt_bias, a_log, d_skip,
               ssd_norm, gla_gate_w, gla_gate_b, gla_norm, w_out, update_ctx):
    f32 = jnp.float32

    def branch_inputs(stream, cvec):
        shift, scale, gate = adaln(cvec, mod_w, mod_b)
        h = rms_norm(stream, norm_g) * (1 + scale) + shift
        return [p.astype(f32) for p in split_cols(jnp.dot(h, w_in), E_SPLITS)], gate

    def mixers(parts, ssd_init, gla_init):
        z, xbc, dt_raw, q, k, v, g, g_lr = parts
        y_ssd, ssd_fin = ssd_mixer(z, xbc, dt_raw, conv_w, conv_b, dt_bias, a_log, d_skip, ssd_norm, ssd_init)
        y_gla, gla_fin = gla_mixer(q, k, v, g, g_lr, gla_gate_w, gla_gate_b, gla_norm, gla_init)
        return jnp.concatenate([y_ssd, y_gla], axis=-1), ssd_fin, gla_fin

    bsz = x.shape[0]
    ssd0 = jnp.zeros((bsz, SSD_GROUPS, SSD_HEADS // SSD_GROUPS, SSD_HEAD_DIM, SSD_STATE), f32)
    gla0 = jnp.zeros((bsz, GLA_HEADS, GLA_KEY_DIM, GLA_VAL_DIM), f32)
    ctx_parts, ctx_gate = branch_inputs(xc, c_ctx[None])
    y_c, ssd_fin, gla_fin = mixers(ctx_parts, (ssd0, ssd0), (gla0, gla0))
    lat_parts, lat_gate = branch_inputs(x, c)
    y, _, _ = mixers(lat_parts, ssd_fin, gla_fin)
    x = x + (lat_gate * jnp.dot(y, w_out)).astype(x.dtype)
    if update_ctx:
        xc = xc + (ctx_gate * jnp.dot(y_c, w_out)).astype(xc.dtype)
    return x, xc

def axial_rope_tables(seq):
    rows = seq // GRID_W
    row = jnp.repeat(jnp.arange(rows, dtype=jnp.float32), GRID_W)
    col = jnp.tile(jnp.arange(GRID_W, dtype=jnp.float32), rows)
    inv = 1.0 / (ROPE_BASE ** (jnp.arange(ROPE_FREQS, dtype=jnp.float32) / ROPE_FREQS))
    ang = jnp.stack([row[:, None] * inv, col[:, None] * inv], axis=1)
    return jnp.cos(ang), jnp.sin(ang)

def apply_axial_rope(t, cos, sin):
    bsz, seq, nh, dh = t.shape
    t = t.reshape(bsz, seq, nh, 2, 2, ROPE_FREQS)
    t1, t2 = t[..., 0, :], t[..., 1, :]
    cs = cos[None, :, None]
    sn = sin[None, :, None]
    return jnp.stack([t1 * cs - t2 * sn, t2 * cs + t1 * sn], axis=-2).reshape(bsz, seq, nh, dh)

def _heads(t, n):
    return t.reshape(t.shape[0], t.shape[1], n, ATT_HEAD_DIM)

def band_blocks(t, nb):
    tp = jnp.pad(t, ((0, 0), (ATT_BLOCK, ATT_BLOCK), (0, 0), (0, 0)))
    tp = tp.reshape(t.shape[0], nb + 2, ATT_BLOCK, t.shape[2], t.shape[3])
    return jnp.concatenate([tp[:, :-2], tp[:, 1:-1], tp[:, 2:]], axis=2)

def band_mask(nb, seq):
    qpos = jnp.arange(nb)[:, None] * ATT_BLOCK + jnp.arange(ATT_BLOCK)[None]
    kpos = (jnp.arange(nb)[:, None] - 1) * ATT_BLOCK + jnp.arange(3 * ATT_BLOCK)[None]
    inside = (kpos >= 0) & (kpos < seq)
    return (jnp.abs(qpos[:, :, None] - kpos[:, None, :]) <= WINDOW) & inside[:, None, :]

def attend_with_sink(qb, key_sets, sink):
    scores = []
    for k, _, mask in key_sets:
        spec = 'bnqhgd,bnkhd->bnhgqk' if k.ndim == 5 else 'bnqhgd,bkhd->bnhgqk'
        s = jnp.einsum(spec, qb, k)
        if mask is not None:
            s = jnp.where(mask[None, :, None, None], s, -jnp.inf)
        scores.append(s)
    sink_l = sink.reshape(ATT_KV_HEADS, ATT_GROUP)[None, None, :, :, None, None]
    m = sink_l
    for s in scores:
        m = jnp.maximum(m, jnp.max(s, axis=-1, keepdims=True))
    denom = jnp.exp(sink_l - m)[..., 0]
    out = 0.0
    for s, (_, v, _) in zip(scores, key_sets):
        p = jnp.exp(s - m)
        denom = denom + jnp.sum(p, axis=-1)
        spec = 'bnhgqk,bnkhd->bnqhgd' if v.ndim == 5 else 'bnhgqk,bkhd->bnqhgd'
        out = out + jnp.einsum(spec, p, v)
    return out / jnp.moveaxis(denom, -1, 2)[..., None]

def odd_layer(x, xc, c, c_ctx, norm_g, mod_w, mod_b, w_in, q_norm, k_norm, sink, w_out, update_ctx):
    f32 = jnp.float32
    bsz, seq, _ = x.shape
    n_ctx = xc.shape[1]
    scale = ATT_HEAD_DIM ** -0.5
    sink = sink.astype(f32)
    c_shift, c_scale, c_gate = adaln(c_ctx[None], mod_w, mod_b)
    hc = rms_norm(xc, norm_g) * (1 + c_scale) + c_shift
    k_c, v_c = split_cols(jnp.dot(hc, w_in[:, :2 * ATT_KV_W]), (ATT_KV_W, ATT_KV_W))
    k_c = rms_norm(_heads(k_c, ATT_KV_HEADS), k_norm).astype(f32)
    v_c = _heads(v_c, ATT_KV_HEADS).astype(f32)
    shift, mscale, gate = adaln(c, mod_w, mod_b)
    h = rms_norm(x, norm_g) * (1 + mscale) + shift
    k, v, q, g = split_cols(jnp.dot(h, w_in), (ATT_KV_W, ATT_KV_W, ATT_W, ATT_W))
    cos, sin = axial_rope_tables(seq)
    q = apply_axial_rope(rms_norm(_heads(q, ATT_HEADS), q_norm).astype(f32), cos, sin)
    k = apply_axial_rope(rms_norm(_heads(k, ATT_KV_HEADS), k_norm).astype(f32), cos, sin)
    v = _heads(v, ATT_KV_HEADS).astype(f32)
    nb = seq // ATT_BLOCK
    qb = (q * scale).reshape(bsz, nb, ATT_BLOCK, ATT_KV_HEADS, ATT_GROUP, ATT_HEAD_DIM)
    o = attend_with_sink(qb, [(band_blocks(k, nb), band_blocks(v, nb), band_mask(nb, seq)), (k_c, v_c, None)], sink)
    o = o.reshape(bsz, seq, ATT_W) * jax.nn.silu(g.astype(f32))
    x = x + (gate * jnp.dot(o, w_out)).astype(x.dtype)
    if update_ctx:
        q_c, g_c = split_cols(jnp.dot(hc, w_in[:, 2 * ATT_KV_W:]), (ATT_W, ATT_W))
        q_c = rms_norm(_heads(q_c, ATT_HEADS), q_norm).astype(f32) * scale
        o_c = attend_with_sink(q_c.reshape(bsz, 1, n_ctx, ATT_KV_HEADS, ATT_GROUP, ATT_HEAD_DIM), [(k_c, v_c, None)], sink)
        o_c = o_c.reshape(bsz, n_ctx, ATT_W) * jax.nn.silu(g_c.astype(f32))
        xc = xc + (c_gate * jnp.dot(o_c, w_out)).astype(xc.dtype)
    return x, xc

def setup_inputs(seed: int = 0) -> dict:
    key = jax.random.key(seed)
    keys = list(jax.random.split(key, 32))
    f32 = jnp.float32

    def normal(shape, s):
        return jax.random.normal(keys.pop(), shape, f32) * s

    def gain(shape):
        return 1.0 + normal(shape, 0.02)

    E, O, D = N_EVEN, N_ODD, D_MODEL
    dt0 = jnp.exp(jax.random.uniform(keys.pop(), (E, 2, SSD_HEADS), f32, math.log(1e-3), math.log(1e-1)))
    a_log = jnp.log(jax.random.uniform(keys.pop(), (E, 2, SSD_HEADS), f32, 1.0, 16.0))
    return {
        'x': normal((BATCH, SEQ, D), 1.0),
        'c': normal((BATCH, D), 1.0),
        'ctx': normal((BATCH, CTX_LEN, D), 1.0),
        'c_ctx': normal((D,), 1.0),
        'e_norm': gain((E, D)),
        'e_mod_w': normal((E, D, 3 * D), 0.5 * D ** -0.5),
        'e_mod_b': normal((E, 3 * D), 0.02),
        'e_w_in': normal((E, D, E_IN), D ** -0.5),
        'e_conv_w': normal((E, CONV_K, CONV_CH), CONV_K ** -0.5),
        'e_conv_b': normal((E, CONV_CH), 0.02),
        'e_dt_bias': dt0 + jnp.log(-jnp.expm1(-dt0)),
        'e_a_log': a_log,
        'e_d_skip': gain((E, SSD_HEADS)),
        'e_ssd_norm': gain((E, SSD_WIDTH)),
        'e_gla_gate_w': normal((E, 2, GLA_RANK, GLA_K), GLA_RANK ** -0.5),
        'e_gla_gate_b': normal((E, 2, GLA_K), 0.1),
        'e_gla_norm': gain((E, GLA_V)),
        'e_w_out': normal((E, E_MIX, D), E_MIX ** -0.5),
        'o_norm': gain((O, D)),
        'o_mod_w': normal((O, D, 3 * D), 0.5 * D ** -0.5),
        'o_mod_b': normal((O, 3 * D), 0.02),
        'o_w_in': normal((O, D, O_IN), D ** -0.5),
        'o_q_norm': gain((O, ATT_HEAD_DIM)),
        'o_k_norm': gain((O, ATT_HEAD_DIM)),
        'o_sink': normal((O, ATT_HEADS), 0.5),
        'o_w_out': normal((O, ATT_W, D), ATT_W ** -0.5),
    }

def reference(x, c, ctx, c_ctx, e_norm, e_mod_w, e_mod_b, e_w_in, e_conv_w, e_conv_b, e_dt_bias, e_a_log,
              e_d_skip, e_ssd_norm, e_gla_gate_w, e_gla_gate_b, e_gla_norm, e_w_out, o_norm, o_mod_w, o_mod_b,
              o_w_in, o_q_norm, o_k_norm, o_sink, o_w_out):
    xc = ctx
    for i in range(DEPTH):
        update_ctx = i < DEPTH - 1
        j = i // 2
        if i % 2 == 0:
            x, xc = even_layer(x, xc, c, c_ctx, e_norm[j], e_mod_w[j], e_mod_b[j], e_w_in[j], e_conv_w[j],
                               e_conv_b[j], e_dt_bias[j], e_a_log[j], e_d_skip[j], e_ssd_norm[j],
                               e_gla_gate_w[j], e_gla_gate_b[j], e_gla_norm[j], e_w_out[j], update_ctx)
        else:
            x, xc = odd_layer(x, xc, c, c_ctx, o_norm[j], o_mod_w[j], o_mod_b[j], o_w_in[j], o_q_norm[j],
                              o_k_norm[j], o_sink[j], o_w_out[j], update_ctx)
    return x


_drawn_inputs = setup_inputs


def setup_inputs(seed=0):
    import zlib

    import numpy as np

    out = dict(_drawn_inputs(seed))
    spreads = {}
    factors = {'e_norm': 7.033,
     'e_conv_b': 8.0,
     'e_d_skip': 8.0,
     'e_ssd_norm': 8.0,
     'e_gla_gate_w': 2.702,
     'e_gla_gate_b': 8.0,
     'e_gla_norm': 8.0,
     'o_norm': 8.0,
     'o_mod_b': 8.0,
     'o_q_norm': 8.0,
     'o_k_norm': 8.0,
     'o_sink': 8.0}
    for name, (base, spread) in spreads.items():
        noise = np.random.default_rng([zlib.crc32(name.encode()), seed]).standard_normal(out[name].shape)
        drawn = base * np.exp(spread * noise) if base else spread * noise
        out[name] = jnp.asarray(drawn.astype(out[name].dtype))
    for name, factor in factors.items():
        out[name] = (out[name] * factor).astype(out[name].dtype)
    return out
```

```python
import concourse.bass as bass
from concourse import mybir
from contextlib import ExitStack

P = 128
DM = 1024
KT = DM // P
CTX, LAT = 256, 512
TOK = CTX + LAT
TT, CT = TOK // P, CTX // P
LT = TT - CT
SH, SD, SG, SN = 16, 64, 2, 128
SW = SH * SD
GW = SW // SG
CONV_K = 5
XB = (SW + 2 * SG * SN) // P
GH, GK, GV, RANK = 4, 128, 256, 16
HALF = 64
AH, AKV, AD = 16, 4, 128
GRP = AH // AKV
NB = 512
KH = 4
SLOTS = 4
EPS = 1e-6
NEG = -1e30
E_Z = 0
E_XBC = E_Z + SW
E_DT = E_XBC + XB * P
E_Q = E_DT + 2 * SH
E_K = E_Q + GH * GK
E_V = E_K + GH * GK
E_G = E_V + GH * GV
E_LR = E_G + GH * GV
KVW = AKV * AD
ORDER = [list(range(TT)), list(range(CT))[::-1] + list(range(CT, TT))[::-1]]

C_ID, C_LE, C_GT, C_GE, C_LT, C_ONE, C_GF, C_GB, C_SCAN = [i * P for i in range(9)]
C_COLS = C_SCAN + NB
M_COLS = (CTX + 2 * P) + (CTX + 3 * P)


def even_odd_layers(nc, x, c, ctx_in, c_ctx, e_norm, e_mod_w, e_mod_b, e_w_in, e_conv_w, e_conv_b, e_dt_bias,
                    e_a_log, e_d_skip, e_ssd_norm, e_gla_gate_w, e_gla_gate_b, e_gla_norm, e_w_out, o_norm,
                    o_mod_w, o_mod_b, o_w_in, o_q_norm, o_k_norm, o_sink, o_w_out, consts, masks, rope, out):
    f32, i32 = mybir.dt.float32, mybir.dt.int32
    ALU, ACT, AX = mybir.AluOpType, mybir.ActivationFunctionType, mybir.AxisListType
    es = ExitStack()

    def sb(name, shape):
        return es.enter_context(nc.sbuf_tensor(name, shape, f32))

    def sem(name):
        return es.enter_context(nc.semaphore(name))

    def spread(ap, axis, n):
        a = ap.unsqueeze(axis)
        shape = list(a.shape)
        shape[axis] = n
        return a.broadcast_to(shape)

    with es:
        SLAB = TT * DM
        arena = sb("arena", [P, 6 * SLAB])
        ring = sb("ring", [P, SLOTS, KH, NB])
        cst = sb("cst", [P, C_COLS])
        ident = cst[:, C_ID:C_ID + P]
        incl = [cst[:, C_LE:C_LE + P], cst[:, C_GE:C_GE + P]]
        strict = [cst[:, C_GT:C_GT + P], cst[:, C_LT:C_LT + P]]
        ones = cst[:, C_ONE:C_ONE + P]
        chunk_ok = [cst[:, C_GF:C_GF + P], cst[:, C_GB:C_GB + P]]
        scan_keep = cst[:, C_SCAN:C_SCAN + NB]
        vecs = sb("vecs", [P, 160])
        V_C, V_N, V_MB, V_CW, V_CB, V_GB, V_ON, V_OMB = 0, 16, 24, 48, 108, 120, 128, 136
        silu_c = sb("silu_c", [P, 16])
        mod = [sb("mod_e", [P, 24, 2]), sb("mod_o", [P, 24, 2])]
        small = sb("small", [P, 224])
        bc_small = sb("bc_small", [P, 96])
        dt_bias, a_log = bc_small[:, 0:32], bc_small[:, 32:64]
        d_skip, sink = bc_small[:, 64:80], bc_small[:, 80:96]
        dtv = sb("dtv", [P, TT, 32])
        dta = sb("dta", [P, TT, 32])
        gate_o = sb("gate_o", [P, DM])
        tail = sb("tail", [P, 3328])
        spare = sb("spare", [P, 1024])

        def slab(i, n=TT, w=DM):
            return arena[:, i * SLAB:i * SLAB + n * w].rearrange("p (n w) -> p n w", n=n)

        hT = [arena[:, s * SLAB:(s + 1) * SLAB].rearrange("p (t k c) -> p t k c", t=TT, k=KT) for s in (0, 2)]
        zs = slab(1)
        xT = arena[:, 2 * SLAB:2 * SLAB + 8 * TOK].rearrange("p (c t) -> p c t", c=8)
        y = slab(2)
        xs = slab(3)
        yT_ssd = arena[:, 3 * SLAB:4 * SLAB].rearrange("p (t k c) -> p t k c", t=TT, k=KT)
        bcT = arena[:, 4 * SLAB:4 * SLAB + 4 * TOK].rearrange("p (c t) -> p c t", c=4)
        b_tok = arena[:, 4 * SLAB + 3072:4 * SLAB + 4608].rearrange("p (t n) -> p t n", t=TT)
        s4 = 4 * SLAB + 4608
        xdt = [arena[:, s4:s4 + 512], spare[:, 0:512]]
        xw = [arena[:, s4 + 512:s4 + 1024], spare[:, 512:1024]]
        ytmp = arena[:, s4 + 1024:s4 + 1536]
        s5 = 5 * SLAB
        S_ssd = arena[:, s5:s5 + 2048].rearrange("p (d n) -> p d n", d=2)
        Edec = [arena[:, s5 + 2048 + 1024 * i:s5 + 3072 + 1024 * i].rearrange("p (h i) -> p h i", h=8) for i in (0, 1)]
        RD = [arena[:, s5 + 4096 + 1024 * i:s5 + 5120 + 1024 * i].rearrange("p (h i) -> p h i", h=8) for i in (0, 1)]
        RAW = TOK + 6
        raw = [arena[:, s5 + 2048 + RAW * i:s5 + 2048 + RAW * (i + 1)] for i in (0, 1)]
        cacc = [arena[:, s5 + 3600 + 772 * i:s5 + 3600 + 772 * i + TOK + 2] for i in (0, 1)]
        vrow1 = arena[:, s5:s5 + P]
        vrow2 = arena[0:32, s5 + P:s5 + 2 * P]
        junk = arena[:, 4 * SLAB:4 * SLAB + DM]
        w_small = tail[:, 0:512].rearrange("p (k n) -> p k n", k=KT)
        norm_bc = tail[:, 768:1792]
        lr_tok = tail[:, 512:704].rearrange("p (t n) -> p t n", t=TT)
        gate_w = tail[0:32, 1792:2816].rearrange("p (d n) -> p d n", d=2)
        cbm = tail[:, 2816:3328].rearrange("p (d g n) -> p d g n", d=2, g=2)
        lrT = tail[0:32, 0:TOK]
        vv = slab(1)
        yT_gla = arena[:, 1 * SLAB:2 * SLAB].rearrange("p (t k c) -> p t k c", t=TT, k=KT)
        gs = slab(2)
        qT_g = arena[:, 4 * SLAB:4 * SLAB + 4 * TOK].rearrange("p (c t) -> p c t", c=4)
        kT_g = arena[:, 4 * SLAB + 4 * TOK:5 * SLAB].rearrange("p (c t) -> p c t", c=4)
        og = slab(0)
        S_gla = arena[:, s5:s5 + 2048].rearrange("p (d h e) -> p d h e", d=2, h=GH)

        def five(i):
            return arena[:, s5 + 2048 + 512 * i:s5 + 2560 + 512 * i]

        def heads4(ap):
            return ap.rearrange("p (h n) -> p h n", h=4)

        attm = [heads4(five(0)), heads4(five(1))]
        qdec = [heads4(five(2)), heads4(five(3))]
        kutok = [heads4(five(4)), heads4(five(5))]
        gcs, gtmp = five(6), five(7)
        gex, kk = spare[:, 0:512], spare[:, 512:1024]
        x1 = slab(0)
        gate_e = arena[:, 4 * SLAB:4 * SLAB + 2 * DM].rearrange("p (s n) -> p s n", s=2)
        etmp = [five(0), five(1)]
        xn1 = slab(3)
        qT = arena[:, 3 * SLAB:3 * SLAB + 8192].rearrange("p (t h c) -> p t h c", t=LT, h=AH)
        sg = arena[:, 3 * SLAB + 8192:3 * SLAB + 16384].rearrange("p (t n) -> p t n", t=LT)
        tables = arena[:, 3 * SLAB + 16384:6 * SLAB].rearrange("p (a t n) -> p a t n", a=4, t=LT)
        kT = arena[:, SLAB:SLAB + AKV * TOK].rearrange("p (h t) -> p h t", h=AKV)
        va = arena[:, SLAB + 3072:2 * SLAB].rearrange("p (t n) -> p t n", t=TT)
        amask = arena[:, 0:M_COLS]
        s2 = 2 * SLAB
        prob = [arena[:, s2 + 640 * i:s2 + 640 * (i + 1)] for i in (0, 1)]
        probT = [arena[:, s2 + 1280 + 640 * i:s2 + 1920 + 640 * i].rearrange("p (b q) -> p b q", b=5) for i in (0, 1)]
        ogate = [arena[:, s2 + 2560 + 512 * i:s2 + 3072 + 512 * i] for i in (0, 1)]
        ftmp = [arena[:, s2 + 3584 + 512 * i:s2 + 4096 + 512 * i] for i in (0, 1)]
        rp = [[tail[:, 2048 * b + 512 * i:2048 * b + 512 * (i + 1)] for i in range(4 if b == 0 else 2)] for b in (0, 1)]
        rp[1] += [spare[:, 0:512], spare[:, 512:1024]]
        qk_gain = sb("qk_gain", [P, 2, AD])

        ps = es.enter_context(nc.psum_tensor("ps", [P, 8, NB], f32))

        def banks(b, n=1):
            return ps[:, b:b + n, :].rearrange("p b n -> p (b n)")

        def halves(w, c0):
            return [w[0, KH * P * k:KH * P * (k + 1), c0:c0 + NB].rearrange("(j p) n -> p j n", p=P)
                    for k in range(w.shape[1] // (KH * P))]

        chunks = []

        def plan(w, c0):
            first = len(chunks)
            chunks.extend(halves(w, c0))
            return list(range(first, len(chunks)))

        MB = 6
        mod_ch = [[plan(e_mod_w, NB * b) for b in range(4)], []]
        xbc_ch = [plan(e_w_in, E_XBC + NB * b) for b in range(XB // 4)]
        z_ch = [plan(e_w_in, E_Z + NB * b) for b in range(2)]
        qk_ch = [plan(e_w_in, E_Q), plan(e_w_in, E_K)]
        v_ch = [plan(e_w_in, E_V + NB * b) for b in range(2)]
        g_ch = [plan(e_w_in, E_G + NB * b) for b in range(2)]
        mod_ch[0] += [plan(e_mod_w, NB * b) for b in range(4, MB)]
        mod_ch[1] += [plan(o_mod_w, NB * b) for b in range(MB)]
        eo_ch = [plan(e_w_out, NB * n) for n in range(2)]
        oin_ch = [plan(o_w_in, NB * b) for b in range(10)]
        oo_ch = [plan(o_w_out, NB * n) for n in range(2)]

        jobs = [("sm", 0, t) for t in range(TT)]
        jobs += [("xbc", cc, part) for cc in range(XB) for part in (0, 1)]
        jobs += [("z", n, t) for n in range(2) for t in range(TT)]
        JOBS_SSD = len(jobs)
        jobs += [("qk", cc, part) for cc in range(2 * GH) for part in (0, 1)]
        JOBS_QK = len(jobs)
        jobs += [("v", n, t) for n in range(2) for t in range(TT)]
        jobs += [("g", n, t) for n in range(2) for t in range(TT)]
        JOBS_E = len(jobs)
        jobs += [("k", 0, t) for t in range(TT)] + [("va", 1, t) for t in range(TT)]
        jobs += [("q", 2 + n, t) for n in range(4) for t in range(CT, TT)]
        jobs += [("sg", 6 + n, t) for n in range(4) for t in range(CT, TT)]
        BY_DVE, BY_ACT = {"sm", "v", "va"}, {"xbc", "z", "qk", "g", "sg"}

        def emptied(j):
            d = jobs[j][0] in BY_DVE
            return d, sum(jobs[i][0] in (BY_DVE if d else BY_ACT) for i in range(j + 1))

        ropes = [j for j in range(len(jobs)) if jobs[j][0] in ("k", "q")]

        mod_mm = [sem("mod_mm_e"), sem("mod_mm_o")]
        proj_mm = sem("proj_mm")
        eo_mm, eo_w = sem("eo_mm"), sem("eo_w")
        oo_mm, oo_w = sem("oo_mm"), sem("oo_w")
        used = {}
        for l in (0, 1):
            for b, ch in enumerate(mod_ch[l]):
                used.update({n: (mod_mm[l], b + 1) for n in ch})
        for jj, (kind, n, t) in enumerate(jobs):
            ch = {"sm": [], "xbc": xbc_ch[n // 4 % 3], "z": z_ch[n % 2], "qk": qk_ch[n // GH % 2], "v": v_ch[n % 2], "g": g_ch[n % 2]}.get(kind, oin_ch[n % 10])
            used.update({m: (proj_mm, jj + 1) for m in ch})
        for n in range(2):
            for q in range(3):
                used[eo_ch[n][q]], used[oo_ch[n][q]] = (eo_w, 3 * n + q + 1), (oo_w, 3 * n + q + 1)
            used[eo_ch[n][3]], used[oo_ch[n][3]] = (eo_mm, TT * (n + 1)), (oo_mm, LT * (n + 1))
        ring_full = [sem(f"ring_full{i}") for i in range(SLOTS)]
        cst_in, vec_in, bc_in, wsm_in, gw_in, nb_in, nb2_in = [sem(n) for n in (
            "cst_in", "vec_in", "bc_in", "wsm_in", "gw_in", "ssd_norm_in", "gla_norm_in")]
        x_in = [sem(f"x_in{t}") for t in range(TT)]
        x1_in = [sem(f"x1_in{t}") for t in range(TT)]
        tab_in, mask_in, gain_in = sem("tab_in"), sem("mask_in"), sem("gain_in")
        gw_zero, conv_zero, S_zero = sem("gw_zero"), sem("conv_zero"), sem("S_zero")
        vec_T, vec_c, silu_done = sem("vec_T"), sem("vec_copied"), sem("silu_done")
        mod_done = [sem("mod_done_e"), sem("mod_done_o")]
        rstd_in, xn_done, ht_tr, ht_done = ([sem(f"{n}{l}") for l in (0, 1)] for n in ("rstd_in", "xn_done", "ht_tr", "ht_done"))
        proj_dve, proj_act = sem("proj_dve"), sem("proj_act")
        lr_tr, lr_done = sem("lr_tr"), sem("lr_done")
        conv_done, xbc_done = sem("conv_done"), sem("xbc_done")
        xs_tr, xs_done, b_done = sem("xs_tr"), sem("xs_done"), sem("b_done")
        dtraw, soft_in, ea_done, dta_done, y_init = (sem(n) for n in ("dtraw", "soft_in", "ea_done", "dta_done", "y_init"))
        cb_mm, d_mm, yo_mm, u_mm, yd_mm = (sem(n) for n in ("cb_mm", "d_mm", "yo_mm", "u_mm", "yd_mm"))
        ex_done, cbm_done, rd_done, dec_done, a_done = (sem(n) for n in ("ex_done", "cbm_done", "rd_done", "dec_done", "a_done"))
        xw_done, sscale, s_new, tmp_done, y_added = (sem(n) for n in ("xw_done", "s_scaled", "s_new", "tmp_done", "y_added"))
        yz_done, ssd_rstd, yn_done, yT_tr, yT_done = (sem(n) for n in ("yz_done", "ssd_rstd", "yn_done", "yT_tr", "yT_done"))
        g_zero = sem("gla_zero")
        lg_mm, lg_x, lg_sp, cs_done, e1_done, qd_done = (sem(n) for n in ("lg_mm", "lg_x", "lg_sp", "cs_done", "e1_done", "qd_done"))
        e2_done, ki_done, at_mm, am_done = (sem(n) for n in ("e2_done", "ki_done", "at_mm", "am_done"))
        tc_done, e3_done, ku_done, ku_tr, kut_done = (sem(n) for n in ("tc_done", "e3_done", "ku_done", "ku_tr", "kut_done"))
        inter_mm, gu_mm, gs_new, o_added = (sem(n) for n in ("inter_mm", "gla_u_mm", "gla_s_new", "o_added"))
        g_rstd, gn_done, gg_done, gT_tr, gT_done = (sem(n) for n in ("gla_rstd", "gla_normed", "gla_gated", "gT_tr", "gT_done"))
        gr_mm, gr_done = sem("gate_row_mm"), sem("gate_row_done")
        eo_done = sem("eo_done")
        gain_done, rk_rstd, rk_t0, rk_b, rk_a, rk_r, rk_tr, rk_done = (sem(n) for n in (
            "tables_done", "rk_rstd", "rk_t0", "rk_b", "rk_a", "rk_r", "rk_tr", "rk_done"))
        sink_done = sem("sink_done")
        s_mm, mx_done, p_done, p_tr, pt_a, pt_d, pv_mm = (sem(n) for n in ("s_mm", "mx_done", "p_done", "p_tr", "pt_act", "pt_dve", "pv_mm"))
        dk_done, ek_done, on_done, og_done, ot_tr, ot_done = (sem(n) for n in ("dk_done", "ek_done", "on_done", "og_done", "ot_tr", "ot_done"))
        fin_done, out_done = sem("fin_done"), sem("out_done")
        dve_own, act_own, pool_own = sem("dve_own"), sem("act_own"), sem("pool_own")

        def step(eng, own):
            n = [0]

            def do(ins):
                n[0] += 1
                ins.then_inc(own, 1)
                eng.wait_ge(own, n[0])
            return do

        block = es.enter_context(nc.Block())

        @block.sync
        def _(sp):
            def load(n):
                if n >= SLOTS:
                    sp.wait_ge(*used[n - SLOTS])
                sp.dma_start(ring[:, n % SLOTS, :, :], chunks[n]).then_inc(ring_full[n % SLOTS], 16)

            for n in range(eo_ch[0][0]):
                load(n)
            sp.wait_ge(gT_tr, TT)
            for t in range(TT):
                src = ctx_in[0, P * t:P * (t + 1), :] if t < CT else x[0, P * (t - CT):P * (t - CT + 1), :]
                sp.dma_start(x1[:, t, :], src).then_inc(x1_in[t], 16)
            for n in range(eo_ch[0][0], oin_ch[0][0]):
                load(n)
            sp.wait_ge(eo_done, 2 * TT)
            for a in range(4):
                sp.dma_start(tables[:, a, :, :], rope[a // 2, :, :].rearrange("(t p) n -> p t n", p=P)).then_inc(tab_in, 16)
            for n in range(oin_ch[0][0], oin_ch[2][0]):
                load(n)
            sp.wait_ge(ht_tr[1], 2 * KT)
            sp.wait_ge(xn_done[1], TT)
            sp.dma_start(amask, masks).then_inc(mask_in, 16)
            for n in range(oin_ch[2][0], len(chunks)):
                load(n)
            for n in range(2):
                for t in range(LT):
                    sp.wait_ge(fin_done, n * LT + t + 1)
                    sp.dma_start(out[0, P * t:P * (t + 1), NB * n:NB * (n + 1)],
                                 x1[:, CT + t, NB * n:NB * (n + 1)]).then_inc(out_done, 16)
            sp.wait_ge(out_done, 16 * 2 * LT)

        @block.gpsimd
        def _(pool):
            do = step(pool, pool_own)
            pool.memset(gate_w, 0.0).then_inc(gw_zero, 1)
            pool.memset(arena[:, s5 + 2048:s5 + 2048 + 2 * RAW], 0.0).then_inc(conv_zero, 1)
            pool.memset(cbm, 0.0).then_inc(conv_zero, 1)
            pool.dma_start(w_small[:, :, 0:32], e_w_in[0, :, E_DT:E_DT + 32].rearrange("(k p) n -> p k n", p=P)).then_inc(wsm_in, 16)
            pool.dma_start(w_small[:, :, 32:64], e_w_in[0, :, E_LR:E_LR + 32].rearrange("(k p) n -> p k n", p=P)).then_inc(wsm_in, 16)
            pool.dma_start(norm_bc, e_ssd_norm[0, :].partition_broadcast(P)).then_inc(nb_in, 16)
            pool.wait_ge(gw_zero, 1)
            for d in range(2):
                pool.dma_start(gate_w[RANK * d:RANK * (d + 1), d, :], e_gla_gate_w[0, d, :, :]).then_inc(gw_in, 16)
            pool.dma_start(qk_gain[:, 0, :], o_q_norm[0, :].partition_broadcast(P)).then_inc(gain_in, 16)
            pool.dma_start(qk_gain[:, 1, :], o_k_norm[0, :].partition_broadcast(P)).then_inc(gain_in, 16)
            pool.wait_ge(xs_tr, TT)
            pool.wait_ge(bc_in, 64)
            for t in range(TT):
                pool.wait_ge(xs_done, t + 1)
                pool.tensor_tensor(y[:, t, :].rearrange("p (h e) -> p h e", h=SH), xs[:, t, :].rearrange("p (h e) -> p h e", h=SH),
                                   spread(d_skip, 2, SD), ALU.mult).then_inc(y_init, 1)
            pool.memset(S_ssd, 0.0).then_inc(S_zero, 1)
            pool.wait_ge(S_zero, 1)
            pool.wait_ge(y_init, TT)
            pool.wait_ge(dta_done, 1)
            for u in range(4 * TT + 1):
                if u < 4 * TT:
                    s, g = u // 2, u % 2
                    d, t = s % 2, ORDER[s % 2][s // 2]
                    dts = dtv[:, t, SH * d + 8 * g:SH * d + 8 * g + 8]
                    xg = xs[:, t, GW * g:GW * (g + 1)].rearrange("p (h e) -> p h e", h=8)
                    ex = small[:, 48 * d:48 * d + 48]
                    if u >= 2:
                        pool.wait_ge(yd_mm, u - 1)
                        pool.wait_ge(u_mm, u - 1)
                    do(pool.tensor_tensor(xdt[u % 2].rearrange("p (h e) -> p h e", h=8), xg, spread(dts, 2, SD), ALU.mult))
                    pool.wait_ge(ex_done, s + 1)
                    pool.tensor_tensor(xw[u % 2].rearrange("p (h e) -> p h e", h=8), xdt[u % 2].rearrange("p (h e) -> p h e", h=8),
                                       spread(ex[:, 16 + 8 * g:24 + 8 * g], 2, SD), ALU.mult).then_inc(xw_done, 1)
                if u >= 1:
                    v = u - 1
                    s, g = v // 2, v % 2
                    d, t = s % 2, ORDER[s % 2][s // 2]
                    ex = small[:, 48 * d:48 * d + 48]
                    Sg = S_ssd[:, d, GW * g:GW * (g + 1)].rearrange("p (h e) -> p h e", h=8)
                    pool.wait_ge(yo_mm, v + 1)
                    if v >= 4:
                        pool.wait_ge(s_new, v - 3)
                    pool.tensor_tensor(Sg, Sg, spread(ex[:, 32 + 8 * g:40 + 8 * g], 2, SD), ALU.mult).then_inc(sscale, 1)
                    pool.wait_ge(tmp_done, v + 1)
                    if v >= 2:
                        pool.wait_ge(y_added, v - 1)
                    yg = y[:, t, GW * g:GW * (g + 1)]
                    pool.tensor_tensor(yg, yg, ytmp, ALU.add).then_inc(y_added, 1)
            pool.wait_ge(s_new, 4 * TT)
            pool.wait_ge(y_added, 4 * TT)
            pool.memset(arena[:, s5:s5 + 2048], 0.0).then_inc(g_zero, 1)
            pool.wait_ge(a_done, 4 * TT)
            pool.wait_ge(yd_mm, 4 * TT)
            pool.memset(arena[:, s5 + 2048:s5 + 3072], 0.0).then_inc(g_zero, 1)
            pool.wait_ge(yn_done, TT)
            pool.dma_start(norm_bc, e_gla_norm[0, :].partition_broadcast(P)).then_inc(nb2_in, 16)
            pool.wait_ge(proj_act, emptied(JOBS_QK - 1)[1])
            for i in range(2 * TT):
                d, t = i % 2, ORDER[i % 2][i // 2]
                kt_ = kT_g[:, :, P * t:P * (t + 1)]
                pool.wait_ge(e2_done, i + 1)
                if i >= 1:
                    pool.wait_ge(ku_tr, i)
                pool.tensor_tensor(heads4(kk), kt_, heads4(gtmp), ALU.mult).then_inc(ki_done, 1)
                pool.wait_ge(ki_done, i + 1)
                end = HALF - 1 if d == 0 else 0
                cs3 = gcs.rearrange("p (h n) -> p h n", n=HALF)
                pool.tensor_tensor(gtmp.rearrange("p (h n) -> p h n", n=HALF), spread(cs3[:, :, end], 2, HALF), cs3,
                                   ALU.subtract).then_inc(tc_done, 1)
                pool.wait_ge(e3_done, i + 1)
                pool.wait_ge(at_mm, i + 1)
                pool.tensor_tensor(heads4(kk), kt_, heads4(gex), ALU.mult).then_inc(ku_done, 1)
            pool.wait_ge(proj_act, emptied(JOBS_E - 1)[1])
            for t in range(TT):
                pool.wait_ge(gn_done, t + 1)
                pool.tensor_tensor(og[:, t, :], og[:, t, :], gs[:, t, :], ALU.mult).then_inc(gg_done, 1)
            for r, j in enumerate(ropes):
                kind, n, t = jobs[j]
                t0, A, B, R = rp[r % 2]
                if kind == "k" and t < CT:
                    continue
                rot = r - CT
                a = 2 if kind == "q" else 3
                pool.wait_ge(rk_t0, r + 1)
                pool.wait_ge(gain_done, 4)
                pool.tensor_tensor(heads4(B), heads4(t0), spread(tables[:, a, t - CT, :], 1, 4), ALU.mult).then_inc(rk_b, 1)
                pool.wait_ge(rk_b, rot + 1)
                pool.wait_ge(rk_a, rot + 1)
                if r >= 2:
                    pool.wait_ge(rk_tr, r - 1)
                A4, B4, R4 = (m.rearrange("p (a s f) -> p a s f", s=2, f=32) for m in (A, B, R))
                pool.tensor_tensor(R4[:, :, 0, :], A4[:, :, 0, :], B4[:, :, 1, :], ALU.add)
                pool.tensor_tensor(R4[:, :, 1, :], A4[:, :, 1, :], B4[:, :, 0, :], ALU.add).then_inc(rk_r, 1)
            for G in range(LT * AKV):
                pool.wait_ge(on_done, G + 1)
                t, g4 = G // AKV, G % AKV
                pool.wait_ge(proj_act, emptied(len(jobs) - 1)[1])
                og_ = ogate[G % 2]
                pool.tensor_tensor(og_, og_, sg[:, t, NB * g4:NB * (g4 + 1)], ALU.mult).then_inc(og_done, 1)

        @block.scalar
        def _(act):
            do = step(act, act_own)
            act.dma_start(cst[:, :], consts).then_inc(cst_in, 16)
            for r0, n, src in ((0, 8, c[0, :]), (8, 8, c_ctx[:]), (16, 8, e_norm[0, :]), (24, 24, e_mod_b[0, :]),
                               (48, 60, e_conv_w[0, :, :]), (108, 12, e_conv_b[0, :]), (120, 8, e_gla_gate_b[0, :, :])):
                src = src.rearrange("(r p) -> r p", p=P) if len(src.shape) == 1 else src.rearrange("k (r p) -> (k r) p", p=P)
                act.dma_start(vrow1[r0:r0 + n, :], src).then_inc(vec_in, 16)
            for r0, n, src in ((0, 8, o_norm[0, :]), (8, 24, o_mod_b[0, :])):
                act.dma_start(vrow2[r0:r0 + n, :], src.rearrange("(r p) -> r p", p=P)).then_inc(vec_in, 16)
            for t in range(TT):
                src = ctx_in[0, P * t:P * (t + 1), :] if t < CT else x[0, P * (t - CT):P * (t - CT + 1), :]
                act.dma_start(xs[:, t, :], src).then_inc(x_in[t], 16)
            for c0, src in ((0, e_dt_bias[0, :, :].rearrange("a b -> (a b)")), (32, e_a_log[0, :, :].rearrange("a b -> (a b)")),
                            (64, e_d_skip[0, :]), (80, o_sink[0, :])):
                act.dma_start(bc_small[:, c0:c0 + src.shape[0]], src.partition_broadcast(P)).then_inc(bc_in, 16)
            act.wait_ge(vec_c, 1)
            act.activation(silu_c[:, :], banks(3)[:, 0:16], ACT.Silu).then_inc(silu_done, 1)

            def inv_rms(ss, width):
                do(act.activation(ss, ss, ACT.Copy, scale=1.0 / width, bias=EPS))
                do(act.activation(ss, ss, ACT.Ln))
                return act.activation(ss, ss, ACT.Exp, scale=-0.5)

            def token_rstd(l):
                src = (xs, x1)[l]
                ss = small[:, 96:96 + TT]
                for t in range(TT):
                    if l == 0:
                        act.wait_ge(x_in[t], 16)
                    else:
                        act.wait_ge(eo_done, TT + t + 1)
                    do(act.activation(junk if l == 0 else arena[:, s5 + 3072:s5 + 4096], src[:, t, :], ACT.Square, accum_out=ss[:, t:t + 1]))
                inv_rms(ss, DM).then_inc(rstd_in[l], 1)

            token_rstd(0)

            def proj_evac(j):
                kind, n, t = jobs[j]
                act.wait_ge(proj_mm, j + 1)
                bank = banks(j % 2)
                if kind == "xbc":
                    if n >= 2:
                        act.wait_ge(conv_done, n - 1)
                    if n < 2:
                        act.wait_ge(conv_zero, 2)
                    o0, w = (2, CTX) if t == 0 else (CTX + 4, LAT)
                    ins = act.activation(raw[n % 2][:, o0:o0 + w], bank[:, 0:w], ACT.Copy)
                elif kind == "z":
                    ins = act.activation(zs[:, t, NB * n:NB * (n + 1)], bank, ACT.Silu)
                elif kind == "qk":
                    o0, w = (0, CTX) if t == 0 else (CTX, LAT)
                    dst = (qT_g if n < GH else kT_g)[:, n % GH, o0:o0 + w]
                    ins = act.activation(dst, bank[:, 0:w], ACT.Copy, scale=float(GK) ** -0.5 if n < GH else 1.0)
                elif kind == "g":
                    ins = act.activation(gs[:, t, NB * n:NB * (n + 1)], bank, ACT.Silu)
                else:
                    ins = act.activation(sg[:, t - CT, NB * (n - 6):NB * (n - 5)], bank, ACT.Silu)
                ins.then_inc(proj_act, 1)

            def conv_silu(cc):
                act.wait_ge(conv_done, cc + 1)
                dst = xT[:, cc, :] if cc < 8 else bcT[:, cc - 8, :]
                act.activation(dst[:, 0:CTX], cacc[cc % 2][:, 0:CTX], ACT.Silu)
                act.activation(dst[:, CTX:TOK], cacc[cc % 2][:, CTX + 2:TOK + 2], ACT.Silu).then_inc(xbc_done, 1)

            j = TT
            act.wait_ge(ht_tr[0], 2 * KT)
            for cc in range(XB):
                proj_evac(j)
                proj_evac(j + 1)
                j += 2
                if cc >= 1:
                    conv_silu(cc - 1)
            conv_silu(XB - 1)
            while j < JOBS_SSD:
                proj_evac(j)
                j += 1
            act.wait_ge(dtraw, TT)
            a3 = dta[:, :, :]
            do(act.activation(a3, dtv[:, :, :], ACT.Abs))
            do(act.activation(a3, a3, ACT.Exp, scale=-1.0))
            act.activation(a3, a3, ACT.Ln, bias=1.0).then_inc(soft_in, 1)
            act.wait_ge(bc_in, 64)
            act.activation(a_log, a_log, ACT.Exp).then_inc(ea_done, 1)
            for t in range(TT):
                act.wait_ge(xs_tr, t + 1)
                act.activation(xs[:, t, :], banks(2 + 3 * (t % 2), 2), ACT.Copy).then_inc(xs_done, 1)
            for u in range(4 * TT):
                s, g = u // 2, u % 2
                if g == 0:
                    d = s % 2
                    act.wait_ge(cb_mm, s + 1)
                    if s >= 2:
                        act.wait_ge(y_added, 2 * (s - 1))
                        act.wait_ge(sscale, 2 * (s - 1))
                    act.activation(small[:, 48 * d:48 * d + 48], banks(7)[:, 48 * d:48 * d + 48], ACT.Exp).then_inc(ex_done, 1)
                act.wait_ge(d_mm, u + 1)
                if u >= 2:
                    act.wait_ge(yd_mm, u - 1)
                act.activation(Edec[u % 2].rearrange("p h i -> p (h i)"), banks(2, 2), ACT.Exp).then_inc(dec_done, 1)
            ss = small[:, 104:104 + 2 * TT]
            for t in range(TT):
                act.wait_ge(yz_done, t + 1)
                for g in range(SG):
                    do(act.activation(junk[:, 0:GW], y[:, t, GW * g:GW * (g + 1)], ACT.Square, accum_out=ss[:, 2 * t + g:2 * t + g + 1]))
            inv_rms(ss, GW).then_inc(ssd_rstd, 1)
            while j < JOBS_QK:
                proj_evac(j)
                j += 1

            def out_T(dst, tr, done):
                for t in range(TT):
                    act.wait_ge(tr, t + 1)
                    act.activation(dst[:, t, :, :].rearrange("p k c -> p (k c)"), banks(2 + 2 * (t % 2), 2), ACT.Copy).then_inc(done, 1)

            out_T(yT_ssd, yT_tr, yT_done)
            while j < JOBS_E:
                if jobs[j][0] == "g":
                    proj_evac(j)
                j += 1
            for i in range(2 * TT):
                act.wait_ge(lg_x, i + 1)
                if i >= 1:
                    act.wait_ge(ku_done, i)
                do(act.activation(gex, gtmp, ACT.Abs))
                do(act.activation(gex, gex, ACT.Exp, scale=-1.0))
                act.activation(gex, gex, ACT.Ln, bias=1.0).then_inc(lg_sp, 1)
                act.wait_ge(cs_done, i + 1)
                act.activation(gex, gcs, ACT.Exp, scale=1.0 / 16).then_inc(e1_done, 1)
                act.activation(gtmp, gcs, ACT.Exp, scale=-1.0 / 16).then_inc(e2_done, 1)
                act.wait_ge(tc_done, i + 1)
                act.wait_ge(qd_done, i + 1)
                act.activation(gex, gtmp, ACT.Exp, scale=1.0 / 16).then_inc(e3_done, 1)
                act.wait_ge(ku_tr, i + 1)
                if i >= 2:
                    act.wait_ge(gu_mm, 4 * (i - 1))
                act.activation(kutok[i % 2].rearrange("p h n -> p (h n)"), banks(7), ACT.Copy).then_inc(kut_done, 1)
            ss = small[:, 116:116 + GH * TT]
            for t in range(TT):
                act.wait_ge(o_added, 2 * TT)
                for h in range(GH):
                    do(act.activation(five(6)[:, 0:GV], og[:, t, GV * h:GV * (h + 1)], ACT.Square, accum_out=ss[:, GH * t + h:GH * t + h + 1]))
            inv_rms(ss, GV).then_inc(g_rstd, 1)
            out_T(yT_gla, gT_tr, gT_done)
            for q in range(3):
                act.wait_ge(gr_mm, q + 1)
                dst = gate_e[:, q, :] if q < 2 else gate_o[:, :]
                act.activation(dst, banks(2 + 2 * (q % 2), 2), ACT.Copy).then_inc(gr_done, 1)
            token_rstd(1)

            def rope_rstd(r, j):
                ss = small[:, 140 + 4 * (r % 2):144 + 4 * (r % 2)]
                act.wait_ge(proj_mm, j + 1)
                if r >= 2:
                    act.wait_ge(rk_t0, r - 1)
                for h in range(4):
                    do(act.activation(vecs[:, 0:AD], banks(j % 2)[:, AD * h:AD * (h + 1)], ACT.Square, accum_out=ss[:, h:h + 1]))
                inv_rms(ss, AD).then_inc(rk_rstd, 1)

            def rope_T(r):
                kind, n, t = jobs[ropes[r]]
                act.wait_ge(rk_tr, r + 1)
                src = heads4(banks(2 + r % 2))
                if kind == "k":
                    dst = kT[:, :, P * t:P * (t + 1)]
                else:
                    dst = qT[:, t - CT, 4 * (n - 2):4 * (n - 1), :]
                act.activation(dst, src, ACT.Copy).then_inc(rk_done, 1)

            act.wait_ge(ht_tr[1], 2 * KT)
            r = 0
            for j in range(JOBS_E, len(jobs)):
                if jobs[j][0] in ("k", "q"):
                    rope_rstd(r, j)
                    r += 1
                elif jobs[j][0] == "sg":
                    proj_evac(j)
                if j - 2 in ropes:
                    rope_T(ropes.index(j - 2))
            def probs(a):
                t, h = a // AH, a % AH
                nk = CTX + P * (3 if 0 < t < LT - 1 else 2)
                act.wait_ge(mx_done, a + 1)
                if h % GRP == 0 and t >= 1:
                    act.wait_ge(on_done, a // GRP - AKV + 1)
                act.activation(prob[a % 2][:, 0:nk], prob[a % 2][:, 0:nk], ACT.Exp, scale=-1.0, bias=small[:, 160 + h:161 + h],
                               accum_out=small[:, 176 + h:177 + h]).then_inc(p_done, 1)

            def probs_T(a):
                act.wait_ge(p_tr, a + 1)
                if a >= 2:
                    act.wait_ge(pv_mm, a - 1)
                act.activation(probT[a % 2][:, 0:4, :].rearrange("p b q -> p (b q)"), banks(6), ACT.Copy).then_inc(pt_a, 1)

            NA = LT * AH
            for a in range(NA + 1):
                if a < NA:
                    probs(a)
                if a >= 1:
                    v = a - 1
                    probs_T(v)
                    if v % GRP == GRP - 1:
                        G = v // GRP
                        g4 = G % AKV
                        act.wait_ge(dk_done, G + 1)
                        act.activation(small[:, 192 + 4 * g4:196 + 4 * g4], small[:, 192 + 4 * g4:196 + 4 * g4], ACT.Exp).then_inc(ek_done, 1)
                    if v % GRP == 1 and v >= GRP:
                        G = v // GRP - 1
                        act.wait_ge(ot_tr, G + 1)
                        act.activation(qT[:, G // AKV, 4 * (G % AKV):4 * (G % AKV) + 4, :].rearrange("p h c -> p (h c)"), banks(1), ACT.Copy).then_inc(ot_done, 1)
            G = LT * AKV - 1
            act.wait_ge(ot_tr, G + 1)
            act.activation(qT[:, G // AKV, 4 * (G % AKV):4 * (G % AKV) + 4, :].rearrange("p h c -> p (h c)"), banks(1), ACT.Copy).then_inc(ot_done, 1)

        @block.vector
        def _(dve):
            do = step(dve, dve_own)
            dve.wait_ge(vec_T, 1)
            dve.tensor_copy(vecs[:, :], banks(3)[:, 0:160]).then_inc(vec_c, 1)
            dve.wait_ge(vec_c, 1)

            def shift_scale(l):
                mb = vecs[:, (V_MB, V_OMB)[l]:(V_MB, V_OMB)[l] + 24]
                g = vecs[:, (V_N, V_ON)[l]:(V_N, V_ON)[l] + KT]
                m3 = banks(2)[:, 48 * l:48 * l + 48].rearrange("p (m s) -> p m s", s=2)
                dve.wait_ge(mod_mm[l], 4 if l == 0 else MB)
                do(dve.tensor_tensor(mod[l][:, 0:16, :], m3[:, 0:16, :], spread(mb[:, 0:16], 2, 2), ALU.add))
                dve.scalar_tensor_tensor(mod[l][:, 8:16, :], mod[l][:, 8:16, :], 1.0, spread(g, 2, 2), ALU.add, ALU.mult).then_inc(mod_done[l], 1)

            def gates(l):
                mb = vecs[:, (V_MB, V_OMB)[l]:(V_MB, V_OMB)[l] + 24]
                m3 = banks(2)[:, 48 * l:48 * l + 48].rearrange("p (m s) -> p m s", s=2)
                dve.wait_ge(mod_mm[l], MB)
                dve.tensor_tensor(mod[l][:, 16:24, :], m3[:, 16:24, :], spread(mb[:, 16:24], 2, 2), ALU.add).then_inc(mod_done[l], 1)

            def normalise(l):
                dve.wait_ge(rstd_in[l], 1)
                src, dst = ((xs, xs), (x1, xn1))[l]
                for t in [2, 3, 4, 5, 0, 1]:
                    dve.tensor_scalar(dst[:, t, :], src[:, t, :], small[:, 96 + t:97 + t], None, ALU.mult).then_inc(xn_done[l], 1)
                dve.wait_ge(mod_done[l], 1)
                for q in range(2 * KT):
                    kt, s = q % KT, q // KT
                    t0, n = (CT, LT) if s == 0 else (0, CT)
                    dve.wait_ge(ht_tr[l], q + 1)
                    dve.tensor_scalar(hT[l][:, t0:t0 + n, kt, :], banks(4 + q % 2)[:, 0:n * P].rearrange("p (t c) -> p t c", t=n),
                                      mod[l][:, 8 + kt, s:s + 1], mod[l][:, kt, s:s + 1], ALU.mult, ALU.add).then_inc(ht_done[l], 1)

            shift_scale(0)
            normalise(0)

            dve.wait_ge(bc_in, 64)
            for t in range(TT):
                dve.wait_ge(proj_mm, t + 1)
                dve.tensor_tensor(dtv[:, t, :], banks(t % 2)[:, 0:32], dt_bias, ALU.add).then_inc(dtraw, 1)
                dve.tensor_copy(lr_tok[:, t, :], banks(t % 2)[:, 32:64]).then_inc(proj_dve, 1)
            dve.wait_ge(lr_tr, 1)
            dve.tensor_copy(lrT[:, 0:NB], banks(6)[0:32, :])
            dve.tensor_copy(lrT[:, NB:TOK], banks(7)[0:32, 0:TOK - NB]).then_inc(lr_done, 1)
            for cc in range(XB):
                dve.wait_ge(proj_act, 2 * cc + 2)
                if cc >= 2:
                    dve.wait_ge(xbc_done, cc - 1)
                acc = cacc[cc % 2]
                for k in range(CONV_K):
                    w = vecs[:, V_CW + XB * k + cc:V_CW + XB * k + cc + 1]
                    src = raw[cc % 2][:, k:k + TOK + 2]
                    if k == 0:
                        do(dve.tensor_scalar(acc, src, w, vecs[:, V_CB + cc:V_CB + cc + 1], ALU.mult, ALU.add))
                    elif k < CONV_K - 1:
                        do(dve.scalar_tensor_tensor(acc, src, w, acc, ALU.mult, ALU.add))
                    else:
                        dve.scalar_tensor_tensor(acc, src, w, acc, ALU.mult, ALU.add).then_inc(conv_done, 1)
            dve.wait_ge(soft_in, 1)
            dve.wait_ge(dtraw, TT)
            do(dve.scalar_tensor_tensor(dtv[:, :, :], dtv[:, :, :], 0.0, dta[:, :, :], ALU.max, ALU.add))
            dve.wait_ge(ea_done, 1)
            dve.scalar_tensor_tensor(dta[:, :, :], dtv[:, :, :], -1.0, spread(a_log, 1, TT), ALU.mult, ALU.mult).then_inc(dta_done, 1)
            for t in range(TT):
                dve.wait_ge(xs_tr, t + 1)
                dve.tensor_copy(b_tok[:, t, :], banks(4 + 3 * (t % 2))[:, 0:2 * P]).then_inc(b_done, 1)
            dve.wait_ge(dta_done, 1)

            def decay_rhs(u):
                s, g = u // 2, u % 2
                d, t = s % 2, ORDER[s % 2][s // 2]
                if u >= 2:
                    dve.wait_ge(d_mm, u - 1)
                dve.tensor_tensor(RD[u % 2], spread(dta[:, t, SH * d + 8 * g:SH * d + 8 * g + 8], 2, P), spread(incl[d], 1, 8),
                                  ALU.mult).then_inc(rd_done, 1)

            def mask_cb(s):
                dve.wait_ge(cb_mm, s + 1)
                dve.wait_ge(ex_done, s + 1)
                if s >= 2:
                    dve.wait_ge(a_done, 2 * (s - 1))
                dve.copy_predicated(cbm[:, s % 2, :, :], spread(incl[s % 2].bitcast(i32), 1, 2),
                                    banks(7)[:, 128:384].rearrange("p (g n) -> p g n", g=2)).then_inc(cbm_done, 1)

            dve.wait_ge(conv_zero, 2)
            decay_rhs(0)
            mask_cb(0)
            for u in range(4 * TT):
                s, g = u // 2, u % 2
                d = s % 2
                ex = small[:, 48 * d:48 * d + 48]
                if u + 1 < 4 * TT:
                    decay_rhs(u + 1)
                dve.wait_ge(dec_done, u + 1)
                dve.wait_ge(cbm_done, s + 1)
                dve.tensor_tensor(Edec[u % 2], Edec[u % 2], spread(cbm[:, d, g, :], 1, 8), ALU.mult).then_inc(a_done, 1)
                if g == 1 and s + 1 < 2 * TT:
                    mask_cb(s + 1)
                dve.wait_ge(yo_mm, u + 1)
                dve.wait_ge(ex_done, s + 1)
                if u >= 1:
                    dve.wait_ge(y_added, u)
                do(dve.tensor_tensor(ytmp.rearrange("p (h e) -> p h e", h=8), banks(5).rearrange("p (h e) -> p h e", h=8),
                                     spread(ex[:, 8 * g:8 * g + 8], 2, SD), ALU.mult))
                dve.wait_ge(yd_mm, u + 1)
                dve.tensor_tensor(ytmp, ytmp, banks(4), ALU.add).then_inc(tmp_done, 1)
                dve.wait_ge(u_mm, u + 1)
                dve.wait_ge(sscale, u + 1)
                Sg = S_ssd[:, d, GW * g:GW * (g + 1)]
                dve.tensor_tensor(Sg, Sg, banks(6), ALU.add).then_inc(s_new, 1)
            dve.wait_ge(y_added, 4 * TT)
            dve.wait_ge(proj_act, emptied(JOBS_SSD - 1)[1])
            for t in range(TT):
                dve.tensor_tensor(y[:, t, :], y[:, t, :], zs[:, t, :], ALU.mult).then_inc(yz_done, 1)
            dve.wait_ge(ssd_rstd, 1)
            dve.wait_ge(nb_in, 16)
            dve.wait_ge(yz_done, TT)
            for t in range(TT):
                for g in range(SG):
                    yg = y[:, t, GW * g:GW * (g + 1)]
                    ins = dve.scalar_tensor_tensor(yg, yg, small[:, 104 + 2 * t + g:105 + 2 * t + g], norm_bc[:, GW * g:GW * (g + 1)],
                                                   ALU.mult, ALU.mult)
                ins.then_inc(yn_done, 1)
            for j in range(JOBS_QK, JOBS_E):
                kind, n, t = jobs[j]
                if kind == "v":
                    dve.wait_ge(proj_mm, j + 1)
                    dve.tensor_copy(vv[:, t, NB * n:NB * (n + 1)], banks(j % 2)).then_inc(proj_dve, 1)
            dve.wait_ge(mod_mm[1], MB)
            gates(0)
            shift_scale(1)
            gates(1)

            def log_gates(i):
                d = i % 2
                dve.wait_ge(lg_mm, i + 1)
                if i >= 1:
                    dve.wait_ge(e3_done, i)
                dve.tensor_tensor(heads4(gtmp), heads4(banks(7)), spread(vecs[:, V_GB + 4 * d:V_GB + 4 * d + 4], 2, P), ALU.add).then_inc(lg_x, 1)
                dve.wait_ge(lg_x, i + 1)

            def decays(i):
                d, t = i % 2, ORDER[i % 2][i // 2]
                dve.wait_ge(lg_sp, i + 1)
                do(dve.scalar_tensor_tensor(gtmp, gtmp, 0.0, gex, ALU.min, ALU.subtract))
                o_, i_ = (gcs, gtmp) if d == 0 else (gcs[:, ::-1], gtmp[:, ::-1])
                dve.tensor_tensor_scan(o_, scan_keep, i_, 0.0, ALU.mult, ALU.add).then_inc(cs_done, 1)

            def dec_queries(i):
                d, t = i % 2, ORDER[i % 2][i // 2]
                dve.wait_ge(e1_done, i + 1)
                end = HALF - 1 if d == 0 else 0
                dve.tensor_copy(small[:, 208 + 8 * d:216 + 8 * d], gex.rearrange("p (h n) -> p h n", n=HALF)[:, :, end])
                dve.tensor_tensor(qdec[d], qT_g[:, :, P * t:P * (t + 1)], heads4(gex), ALU.mult).then_inc(qd_done, 1)

            def mask_att(i):
                dve.wait_ge(at_mm, i + 1)
                if i >= 2:
                    dve.wait_ge(inter_mm, 2 * (i - 1))
                dve.copy_predicated(attm[i % 2], spread(chunk_ok[i % 2].bitcast(i32), 1, 4), heads4(banks(6))).then_inc(am_done, 1)

            def states(i, a):
                d = i % 2
                half = a if d == 0 else 1 - a
                dve.wait_ge(inter_mm, 2 * i + a + 1)
                dve.wait_ge(qd_done, i + 1)
                for h in range(GH):
                    if h % 2 == 0:
                        dve.wait_ge(gu_mm, 2 * (2 * i + a) + h // 2 + 1)
                    Sh = S_gla[:, d, h, :]
                    ins = dve.scalar_tensor_tensor(Sh, Sh, small[:, 208 + 8 * d + 2 * h + half:209 + 8 * d + 2 * h + half],
                                                   banks(2 + h // 2)[:, GV * (h % 2):GV * (h % 2 + 1)], ALU.mult, ALU.add)
                    if h % 2 == 1:
                        ins.then_inc(gs_new, 1)

            dve.wait_ge(g_zero, 2)
            dve.wait_ge(xw_done, 4 * TT)
            dve.wait_ge(u_mm, 4 * TT)
            dve.wait_ge(proj_act, emptied(JOBS_QK - 1)[1])
            log_gates(0)
            decays(0)
            dec_queries(0)
            mask_att(0)
            seen = set()
            for i in range(2 * TT):
                d, t = i % 2, ORDER[i % 2][i // 2]
                nxt = i + 1 < 2 * TT
                if nxt:
                    log_gates(i + 1)
                states(i, 0)
                if nxt:
                    decays(i + 1)
                states(i, 1)
                dve.wait_ge(inter_mm, 2 * i + 2)
                ob = banks(4, 2) if d == 0 else banks(0, 2)
                if t in seen:
                    dve.wait_ge(o_added, i)
                    dve.tensor_tensor(og[:, t, :], og[:, t, :], ob, ALU.add).then_inc(o_added, 1)
                else:
                    dve.tensor_copy(og[:, t, :], ob).then_inc(o_added, 1)
                seen.add(t)
                if nxt:
                    dve.wait_ge(gs_new, 4 * (i + 1))
                    dec_queries(i + 1)
                    mask_att(i + 1)
            dve.wait_ge(g_rstd, 1)
            dve.wait_ge(nb2_in, 16)
            dve.wait_ge(o_added, 2 * TT)
            for t in range(TT):
                for h in range(GH):
                    oh = og[:, t, GV * h:GV * (h + 1)]
                    ins = dve.scalar_tensor_tensor(oh, oh, small[:, 116 + GH * t + h:117 + GH * t + h], norm_bc[:, GV * h:GV * (h + 1)],
                                                   ALU.mult, ALU.mult)
                ins.then_inc(gn_done, 1)
            dve.wait_ge(gr_done, 2)
            for n in range(2):
                for t in range(TT):
                    dve.wait_ge(eo_mm, n * TT + t + 1)
                    e = etmp[t % 2]
                    do(dve.tensor_tensor(e, banks(t), gate_e[:, 1 if t < CT else 0, NB * n:NB * (n + 1)], ALU.mult))
                    if n == 0:
                        dve.wait_ge(x1_in[t], 16)
                    xp = x1[:, t, NB * n:NB * (n + 1)]
                    dve.tensor_tensor(xp, xp, e, ALU.add).then_inc(eo_done, 1)
            dve.wait_ge(eo_done, 2 * TT)
            normalise(1)
            dve.wait_ge(tab_in, 64)
            dve.wait_ge(gain_in, 32)
            for a in range(4):
                qk = a % 2
                g3 = spread(qk_gain[:, qk, :], 1, LT)
                sc = -float(AD) ** -0.5 if qk == 0 else 1.0
                dve.scalar_tensor_tensor(tables[:, a, :, :], tables[:, a, :, :], sc, g3, ALU.mult, ALU.mult).then_inc(gain_done, 1)
            dve.tensor_scalar(sink, sink, -1.0, None, ALU.mult).then_inc(sink_done, 1)
            dve.wait_ge(gain_done, 4)
            r = 0
            for j in range(JOBS_E, len(jobs)):
                kind, n, t = jobs[j]
                if kind == "va":
                    dve.wait_ge(proj_mm, j + 1)
                    dve.tensor_copy(va[:, t, :], banks(j % 2)).then_inc(proj_dve, 1)
                elif kind in ("k", "q"):
                    t0, A, B, R = rp[r % 2]
                    dve.wait_ge(rk_rstd, r + 1)
                    if r > CT + 1:
                        dve.wait_ge(rk_b, r - 1 - CT)
                    ss = small[:, 140 + 4 * (r % 2):144 + 4 * (r % 2)]
                    ins = dve.tensor_tensor(heads4(t0), heads4(banks(j % 2)), spread(ss, 2, AD), ALU.mult)
                    ins.then_inc(rk_t0, 1)
                    dve.wait_ge(rk_t0, r + 1)
                    if kind == "k" and t < CT:
                        dve.tensor_tensor(heads4(R), heads4(t0), spread(qk_gain[:, 1, :], 1, 4), ALU.mult).then_inc(rk_r, 1)
                    else:
                        if r > CT + 1:
                            dve.wait_ge(rk_r, r - 1)
                        dve.tensor_tensor(heads4(A), heads4(t0), spread(tables[:, 0 if kind == "q" else 1, t - CT, :], 1, 4),
                                          ALU.mult).then_inc(rk_a, 1)
                    r += 1
            dve.wait_ge(mask_in, 16)
            dve.wait_ge(sink_done, 1)
            NA = LT * AH

            def row_min(a):
                t, h = a // AH, a % AH
                nk = CTX + P * (3 if 0 < t < LT - 1 else 2)
                m = amask[:, 0:nk] if t == 0 else amask[:, CTX + 2 * P:CTX + 2 * P + nk]
                dve.wait_ge(s_mm, a + 1)
                if a >= 2:
                    dve.wait_ge(p_tr, a - 1)
                dve.tensor_tensor_reduce(out=prob[a % 2][:, 0:nk], in0=banks(2 + 2 * (a % 2), 2)[:, 0:nk], in1=m, scale=1.0,
                                         scalar=sink[:, h:h + 1], op0=ALU.add, op1=ALU.min,
                                         accum_out=small[:, 160 + h:161 + h]).then_inc(mx_done, 1)

            for a in range(NA + 2):
                if a < NA:
                    if a % GRP == 0 and a >= AH:
                        dve.wait_ge(ek_done, (a - AH) // GRP + 1)
                    row_min(a)
                if 1 <= a <= NA:
                    v = a - 1
                    t = v // AH
                    if 0 < t < LT - 1:
                        dve.wait_ge(p_tr, v + 1)
                        if v >= 2:
                            dve.wait_ge(pv_mm, v - 1)
                        dve.tensor_copy(probT[v % 2][:, 4, :], banks(7)[:, 0:P]).then_inc(pt_d, 1)
                    if v % GRP == GRP - 1:
                        G = v // GRP
                        g4 = G % AKV
                        dk = small[:, 192 + 4 * g4:196 + 4 * g4]
                        dve.wait_ge(mx_done, v + 1)
                        dve.tensor_tensor(dk, small[:, 160 + 4 * g4:164 + 4 * g4], sink[:, 4 * g4:4 * g4 + 4], ALU.subtract).then_inc(dk_done, 1)
                if a >= 2 and (a - 2) % GRP == GRP - 1:
                    v = a - 2
                    G = v // GRP
                    g4 = G % AKV
                    dk = small[:, 192 + 4 * g4:196 + 4 * g4]
                    dve.wait_ge(ek_done, G + 1)
                    do(dve.tensor_tensor(dk, dk, small[:, 176 + 4 * g4:180 + 4 * g4], ALU.add))
                    do(dve.reciprocal(dk, dk))
                    dve.wait_ge(pv_mm, v + 1)
                    if G >= 2:
                        dve.wait_ge(ot_tr, G - 1)
                    dve.tensor_tensor(heads4(ogate[G % 2]), heads4(banks(0)), spread(dk, 2, AD), ALU.mult).then_inc(on_done, 1)
            dve.wait_ge(gr_done, 3)
            for n in range(2):
                for t in range(LT):
                    q = n * LT + t
                    dve.wait_ge(oo_mm, q + 1)
                    f = ftmp[q % 2]
                    do(dve.tensor_tensor(f, banks(q), gate_o[:, NB * n:NB * (n + 1)], ALU.mult))
                    xp = x1[:, CT + t, NB * n:NB * (n + 1)]
                    dve.tensor_tensor(xp, xp, f, ALU.add).then_inc(fin_done, 1)

        @block.tensor
        def _(pe):
            mm = pe.matmul

            def arrived(n):
                pe.wait_ge(ring_full[n % SLOTS], 16 * (n // SLOTS + 1))
                return ring[:, n % SLOTS, :, :]

            pe.wait_ge(cst_in, 16)
            pe.wait_ge(vec_in, 16 * 9)
            pe.transpose(banks(3)[:, 0:P], vrow1, ident)
            pe.transpose(banks(3)[:, P:P + 32], vrow2, ident[0:32, 0:32]).then_inc(vec_T, 1)

            def modulation(l, b):
                w = [arrived(n) for n in mod_ch[l][b]]
                for m in range(4):
                    o0 = 48 * l + 2 * (4 * b + m)
                    for k in range(KT):
                        ins = mm(banks(2)[:, o0:o0 + 2], w[k // KH][:, k % KH, P * m:P * (m + 1)], silu_c[:, k:16:8],
                                 start=(k == 0), stop=(k == KT - 1))
                ins.then_inc(mod_mm[l], 1)

            def transpose_h(l):
                src = (xs, xn1)[l]
                pe.wait_ge(xn_done[l], TT)
                for q in range(2 * KT):
                    kt, s = q % KT, q // KT
                    t0, n = (CT, LT) if s == 0 else (0, CT)
                    if q >= 2:
                        pe.wait_ge(ht_done[l], q - 1)
                    for t in range(n):
                        ins = pe.transpose(banks(4 + q % 2)[:, P * t:P * (t + 1)], src[:, t0 + t, P * kt:P * (kt + 1)], ident)
                    ins.then_inc(ht_tr[l], 1)

            pe.wait_ge(silu_done, 1)
            for b in range(4):
                modulation(0, b)
            transpose_h(0)
            pe.wait_ge(ht_done[0], 2 * KT)
            pe.wait_ge(wsm_in, 32)

            def free_bank(j):
                if j >= 2:
                    d, n = emptied(j - 2)
                    pe.wait_ge(proj_dve if d else proj_act, n)

            def token_job(j, l, ch):
                t = jobs[j][2]
                w = [arrived(n) for n in ch]
                for k in range(KT):
                    ins = mm(banks(j % 2), hT[l][:, t, k, :], w[k // KH][:, k % KH, :], start=(k == 0), stop=(k == KT - 1))
                ins.then_inc(proj_mm, 1)

            def feature_job(j, ch, m, part):
                w = [arrived(n) for n in ch]
                t0, n = (0, CT) if part == 0 else (CT, LT)
                for k in range(KT):
                    ins = mm(banks(j % 2)[:, 0:n * P], w[k // KH][:, k % KH, P * m:P * (m + 1)], hT[0][:, t0:t0 + n, k, :],
                             start=(k == 0), stop=(k == KT - 1))
                ins.then_inc(proj_mm, 1)

            j = 0
            for t in range(TT):
                free_bank(j)
                for k in range(KT):
                    ins = mm(banks(j % 2)[:, 0:64], hT[0][:, t, k, :], w_small[:, k, :], start=(k == 0), stop=(k == KT - 1))
                ins.then_inc(proj_mm, 1)
                j += 1
            while j < JOBS_SSD:
                kind, n, t = jobs[j]
                free_bank(j)
                if kind == "xbc":
                    feature_job(j, xbc_ch[n // 4], n % 4, t)
                else:
                    token_job(j, 0, z_ch[n])
                j += 1
                if j == TT + 2:
                    pe.wait_ge(proj_dve, TT)
                    for t in range(TT):
                        b, o0 = (6, P * t) if t < 4 else (7, P * (t - 4))
                        ins = pe.transpose(banks(b)[0:32, o0:o0 + P], lr_tok[:, t, :], ident)
                    ins.then_inc(lr_tr, 1)
            pe.wait_ge(xbc_done, XB)
            for t in range(TT):
                b = 2 + 3 * (t % 2)
                if t == 0:
                    pe.wait_ge(lr_done, 1)
                if t >= 2:
                    pe.wait_ge(xs_done, t - 1)
                    pe.wait_ge(b_done, t - 1)
                for cc in range(8):
                    pe.transpose(banks(b, 2)[:, P * cc:P * (cc + 1)], xT[:, cc, P * t:P * (t + 1)], ident)
                for cc in range(2):
                    ins = pe.transpose(banks(b + 2)[:, P * cc:P * (cc + 1)], bcT[:, cc, P * t:P * (t + 1)], ident)
                ins.then_inc(xs_tr, 1)

            def ssd_ahead(u):
                s, g = u // 2, u % 2
                d, t = s % 2, ORDER[s % 2][s // 2]
                if g == 0:
                    if s >= 1:
                        pe.wait_ge(cbm_done, s)
                    r = dta[:, t, SH * d:SH * (d + 1)]
                    for q, lhsT in enumerate((incl[d], strict[d], ones)):
                        mm(banks(7)[:, 48 * d + 16 * q:48 * d + 16 * q + 16], lhsT, r, start=True, stop=True)
                    for q in range(SG):
                        ins = mm(banks(7)[:, 128 + 128 * q:256 + 128 * q], bcT[:, q, P * t:P * (t + 1)], bcT[:, 2 + q, P * t:P * (t + 1)],
                                 start=True, stop=True)
                    ins.then_inc(cb_mm, 1)
                pe.wait_ge(rd_done, u + 1)
                if u >= 1:
                    pe.wait_ge(dec_done, u)
                for q in range(2):
                    ins = mm(banks(2 + q), strict[d], RD[u % 2][:, 4 * q:4 * q + 4, :], start=True, stop=True)
                ins.then_inc(d_mm, 1)

            pe.wait_ge(dta_done, 1)
            pe.wait_ge(xs_done, TT)
            pe.wait_ge(b_done, TT)
            pe.wait_ge(S_zero, 1)
            ssd_ahead(0)
            for u in range(4 * TT):
                s, g = u // 2, u % 2
                d, t = s % 2, ORDER[s % 2][s // 2]
                if u + 1 < 4 * TT:
                    ssd_ahead(u + 1)
                if u >= 4:
                    pe.wait_ge(s_new, u - 3)
                if u >= 1:
                    pe.wait_ge(tmp_done, u)
                mm(banks(5), bcT[:, 2 + g, P * t:P * (t + 1)], S_ssd[:, d, GW * g:GW * (g + 1)], start=True, stop=True).then_inc(yo_mm, 1)
                pe.wait_ge(xw_done, u + 1)
                if u >= 1:
                    pe.wait_ge(s_new, u)
                mm(banks(6), b_tok[:, t, P * g:P * (g + 1)], xw[u % 2], start=True, stop=True).then_inc(u_mm, 1)
                pe.wait_ge(a_done, u + 1)
                for h in range(8):
                    ins = mm(banks(4)[:, SD * h:SD * (h + 1)], Edec[u % 2][:, h, :], xdt[u % 2][:, SD * h:SD * (h + 1)], start=True, stop=True)
                ins.then_inc(yd_mm, 1)

            while j < JOBS_E:
                kind, n, t = jobs[j]
                if j == JOBS_QK:
                    for tt in range(TT):
                        pe.wait_ge(yn_done, tt + 1)
                        if tt >= 2:
                            pe.wait_ge(yT_done, tt - 1)
                        else:
                            pe.wait_ge(tmp_done, 4 * TT)
                        for k in range(KT):
                            ins = pe.transpose(banks(2 + 2 * (tt % 2), 2)[:, P * k:P * (k + 1)], y[:, tt, P * k:P * (k + 1)], ident)
                        ins.then_inc(yT_tr, 1)
                free_bank(j)
                if kind == "qk":
                    feature_job(j, qk_ch[n // GH], n % GH, t)
                else:
                    token_job(j, 0, (v_ch if kind == "v" else g_ch)[n])
                j += 1
            pe.wait_ge(yT_done, TT)
            for b in range(4, MB):
                modulation(0, b)
            for b in range(MB):
                modulation(1, b)

            def gla_logits(i):
                d, t = i % 2, ORDER[i % 2][i // 2]
                if i >= 1:
                    pe.wait_ge(kut_done, i)
                for h in range(GH):
                    ins = mm(banks(7)[:, P * h:P * (h + 1)], gate_w[:, d, GK * h:GK * (h + 1)], lrT[:, P * t:P * (t + 1)], start=True, stop=True)
                ins.then_inc(lg_mm, 1)

            def gla_scores(i):
                d = i % 2
                pe.wait_ge(ki_done, i + 1)
                pe.wait_ge(qd_done, i + 1)
                if i >= 1:
                    pe.wait_ge(am_done, i)
                for h in range(GH):
                    ins = mm(banks(6)[:, P * h:P * (h + 1)], heads4(kk)[:, h, :], qdec[d][:, h, :], start=True, stop=True)
                ins.then_inc(at_mm, 1)

            def gla_keys(i):
                pe.wait_ge(ku_done, i + 1)
                for h in range(GH):
                    ins = pe.transpose(banks(7)[:, P * h:P * (h + 1)], heads4(kk)[:, h, :], ident)
                ins.then_inc(ku_tr, 1)

            def gla_main(i):
                d, t = i % 2, ORDER[i % 2][i // 2]
                ob = 4 if d == 0 else 0
                o3 = banks(ob, 2).rearrange("p (h e) -> p h e", h=GH)
                if i >= 2:
                    pe.wait_ge(o_added, i - 1)
                elif i == 1:
                    pe.wait_ge(proj_act, emptied(JOBS_E - 1)[1])
                pe.wait_ge(am_done, i + 1)
                pe.wait_ge(kut_done, i + 1)
                for h in range(GH):
                    mm(o3[:, h, :], attm[d][:, h, :], vv[:, t, GV * h:GV * (h + 1)], start=(h % 2 == 0), stop=True, skip_group_check=True)
                for a in range(2):
                    half = a if d == 0 else 1 - a
                    r0 = HALF * half
                    if a == 1:
                        pe.wait_ge(gs_new, 2 * (2 * i + 1))
                    elif i >= 2:
                        pe.wait_ge(gs_new, 4 * (i - 1))
                    for h in range(GH):
                        ins = mm(o3[r0:r0 + HALF, h, :], qdec[d][:, h, r0:r0 + HALF], S_gla[:, d, h, :], start=False, stop=True,
                                 skip_group_check=True)
                    ins.then_inc(inter_mm, 1)
                    for h in range(GH):
                        hf = 2 * i + a
                        if h % 2 == 0 and 2 * hf - 1 + h // 2 > 0:
                            pe.wait_ge(gs_new, 2 * hf - 1 + h // 2)
                        ins = mm(banks(2 + h // 2)[:, GV * (h % 2):GV * (h % 2 + 1)], kutok[d][r0:r0 + HALF, h, :],
                                 vv[r0:r0 + HALF, t, GV * h:GV * (h + 1)], start=True, stop=True)
                        if h % 2 == 1:
                            ins.then_inc(gu_mm, 1)

            pe.wait_ge(gw_in, 32)
            pe.wait_ge(mod_done[1], 2)
            pe.wait_ge(g_zero, 2)
            gla_logits(0)
            gla_scores(0)
            gla_keys(0)
            for i in range(2 * TT):
                if i + 1 < 2 * TT:
                    gla_logits(i + 1)
                gla_main(i)
                if i + 1 < 2 * TT:
                    gla_scores(i + 1)
                    gla_keys(i + 1)
            for t in range(TT):
                pe.wait_ge(gg_done, t + 1)
                if t >= 2:
                    pe.wait_ge(gT_done, t - 1)
                else:
                    pe.wait_ge(o_added, 2 * TT)
                for k in range(KT):
                    ins = pe.transpose(banks(2 + 2 * (t % 2), 2)[:, P * k:P * (k + 1)], og[:, t, P * k:P * (k + 1)], ident)
                ins.then_inc(gT_tr, 1)
            for q in range(3):
                l, s = (0, q) if q < 2 else (1, 0)
                if q < 2:
                    pe.wait_ge(gT_done, TT - 1 + q)
                else:
                    pe.wait_ge(gr_done, 1)
                for k in range(KT):
                    ins = mm(banks(2 + 2 * (q % 2), 2)[:, P * k:P * (k + 1)], spread(mod[l][:, 16 + k, s], 1, P), ident, start=True, stop=True)
                ins.then_inc(gr_mm, 1)
            pe.wait_ge(gr_done, 3)
            for n in range(2):
                for q, ch in enumerate(eo_ch[n]):
                    w = arrived(ch)
                    src = yT_ssd if q < 2 else yT_gla
                    for t in range(TT):
                        if n == 1 and q == 0:
                            pe.wait_ge(eo_done, t + 1)
                        for k in range(KH):
                            ins = mm(banks(t), src[:, t, KH * (q % 2) + k, :], w[:, k, :], start=(q == 0 and k == 0), stop=(q == 3 and k == KH - 1))
                        if q == 3:
                            ins.then_inc(eo_mm, 1)
                    if q < 3:
                        ins.then_inc(eo_w, 1)
            transpose_h(1)
            pe.wait_ge(ht_done[1], 2 * KT)

            def rope_transpose(r):
                pe.wait_ge(rk_r, r + 1)
                if r >= 2:
                    pe.wait_ge(rk_done, r - 1)
                R = rp[r % 2][3]
                for h in range(4):
                    ins = pe.transpose(banks(2 + r % 2)[:, P * h:P * (h + 1)], heads4(R)[:, h, :], ident)
                ins.then_inc(rk_tr, 1)

            first = JOBS_E
            for j in range(JOBS_E, len(jobs)):
                kind, n, t = jobs[j]
                if j - 2 >= first:
                    if jobs[j - 2][0] in ("k", "q"):
                        r = ropes.index(j - 2)
                        pe.wait_ge(rk_t0, r + 1)
                    else:
                        d, m = emptied(j - 2)
                        pe.wait_ge(proj_dve if d else proj_act, m)
                token_job(j, 1, oin_ch[n])
                if j - 2 in ropes:
                    rope_transpose(ropes.index(j - 2))
            pe.wait_ge(rk_done, len(ropes))

            NA = LT * AH

            def scores(a):
                t, h = a // AH, a % AH
                kv = h // GRP
                lo, hi = max(t - 1, 0), min(t + 1, LT - 1)
                k0 = CTX + P * lo
                if a >= 2:
                    pe.wait_ge(mx_done, a - 1)
                b = banks(2 + 2 * (a % 2), 2)
                lhsT = qT[:, t, h, :]
                mm(b[:, 0:CTX], lhsT, kT[:, kv, 0:CTX], start=True, stop=True)
                ins = mm(b[:, CTX:CTX + 2 * P], lhsT, kT[:, kv, k0:k0 + 2 * P], start=True, stop=True)
                if hi - lo == 2:
                    ins = mm(b[:, CTX + 2 * P:CTX + 3 * P], lhsT, kT[:, kv, k0 + 2 * P:k0 + 3 * P], start=True, stop=True)
                ins.then_inc(s_mm, 1)

            def out_transpose(G):
                pe.wait_ge(og_done, G + 1)
                if G >= 1:
                    pe.wait_ge(ot_done, G)
                for h in range(GRP):
                    ins = pe.transpose(banks(1)[:, P * h:P * (h + 1)], heads4(ogate[G % 2])[:, h, :], ident)
                ins.then_inc(ot_tr, 1)

            scores(0)
            for a in range(NA + 1):
                if a + 1 < NA:
                    scores(a + 1)
                if a >= 1:
                    v = a - 1
                    t, h = v // AH, v % AH
                    kv = h // GRP
                    lo, hi = max(t - 1, 0), min(t + 1, LT - 1)
                    tiles = list(range(CT)) + [CT + b for b in range(lo, hi + 1)]
                    pe.wait_ge(pt_a, v + 1)
                    if len(tiles) == 5:
                        pe.wait_ge(pt_d, v + 1 - AH)
                    if v % GRP == 0 and v >= GRP:
                        pe.wait_ge(on_done, v // GRP)
                    for b, kt in enumerate(tiles):
                        ins = mm(banks(0)[:, AD * (v % GRP):AD * (v % GRP + 1)], probT[v % 2][:, b, :], va[:, kt, AD * kv:AD * (kv + 1)],
                                 start=(b == 0), stop=(b == len(tiles) - 1))
                    ins.then_inc(pv_mm, 1)
                if a < NA:
                    t = a // AH
                    nb = 5 if 0 < t < LT - 1 else 4
                    pe.wait_ge(p_done, a + 1)
                    for b in range(nb):
                        ins = pe.transpose(banks(6, 2)[:, P * b:P * (b + 1)], prob[a % 2][:, P * b:P * (b + 1)], ident)
                    ins.then_inc(p_tr, 1)
                if a >= 1 and (a - 1) % GRP == 1 and a - 1 >= GRP:
                    out_transpose((a - 1) // GRP - 1)
            out_transpose(LT * AKV - 1)
            pe.wait_ge(ot_done, LT * AKV)
            for n in range(2):
                for q, ch in enumerate(oo_ch[n]):
                    w = arrived(ch)
                    for t in range(LT):
                        for k in range(KH):
                            ins = mm(banks(n * LT + t), qT[:, t, KH * q + k, :], w[:, k, :], start=(q == 0 and k == 0), stop=(q == 3 and k == KH - 1))
                        if q == 3:
                            ins.then_inc(oo_mm, 1)
                    if q < 3:
                        ins.then_inc(oo_w, 1)


def constants():
    import numpy as np
    k = np.arange(P)
    a, b = k[:, None], k[None, :]
    same = a // HALF == b // HALF
    tiles = [a == b, a <= b, a > b, a >= b, a < b, np.ones((P, P)), same & (a <= b), same & (a >= b)]
    keep = np.ones((P, NB))
    keep[:, ::HALF] = 0
    consts = np.concatenate([np.asarray(m, np.float32) for m in tiles] + [keep.astype(np.float32)], axis=1)
    zero = np.zeros((P, P), np.float32)
    before = np.where(b >= a, 0, -NEG).astype(np.float32)
    after = np.where(b <= a, 0, -NEG).astype(np.float32)
    masks = np.concatenate([zero, zero, zero, after, zero, zero, before, zero, after], axis=1)
    grid, freqs, base = 64, AD // 4, 10000.0
    rows = LAT // grid
    row = np.repeat(np.arange(rows, dtype=np.float32), grid)
    col = np.tile(np.arange(grid, dtype=np.float32), rows)
    inv = (np.float32(1.0) / (np.float32(base) ** (np.arange(freqs, dtype=np.float32) / np.float32(freqs)))).astype(np.float32)
    ang = np.stack([row[:, None] * inv, col[:, None] * inv], axis=1).astype(np.float32)
    cos, sin = np.cos(ang), np.sin(ang)
    cc = np.stack([cos, cos], axis=2).reshape(LAT, AD)
    ss = np.stack([sin, -sin], axis=2).reshape(LAT, AD)
    return consts, masks, np.stack([cc, ss]).astype(np.float32)


_INS = ['x', 'c', 'ctx', 'c_ctx', 'e_norm', 'e_mod_w', 'e_mod_b', 'e_w_in', 'e_conv_w', 'e_conv_b', 'e_dt_bias', 'e_a_log',
        'e_d_skip', 'e_ssd_norm', 'e_gla_gate_w', 'e_gla_gate_b', 'e_gla_norm', 'e_w_out', 'o_norm', 'o_mod_w', 'o_mod_b',
        'o_w_in', 'o_q_norm', 'o_k_norm', 'o_sink', 'o_w_out']


def kernel(**inputs):
    import numpy as np
    import concourse.bacc as bacc
    from concourse.bass_utils import run_bass_kernel_spmd

    nc = bacc.Bacc("TRN2", target_bir_lowering=False, num_devices=1)
    arrays, args = {}, []
    extra = dict(zip(("consts", "masks", "rope"), constants()))
    for name in _INS + list(extra):
        a = np.ascontiguousarray(extra[name] if name in extra else inputs[name])
        arrays[f"in_{name}"] = a
        args.append(nc.dram_tensor(f"in_{name}", a.shape, mybir.dt.from_np(a.dtype), kind="ExternalInput").ap())
    args.append(nc.dram_tensor("out_x", (1, LAT, DM), mybir.dt.float32, kind="ExternalOutput").ap())
    even_odd_layers(nc, *args)
    r = run_bass_kernel_spmd(nc, [arrays], core_ids=[0])
    return r.results[0]["out_x"]
```

```python
import concourse.bass as bass
from concourse import mybir
from contextlib import ExitStack

P = 128
DM = 1024
KT = DM // P
CTX, LAT = 256, 512
TOK = CTX + LAT
TT, CT = TOK // P, CTX // P
LT = TT - CT
SH, SD, SG, SN = 16, 64, 2, 128
SW = SH * SD
GW = SW // SG
CONV_K = 5
XB = (SW + 2 * SG * SN) // P
GH, GK, GV, RANK = 4, 128, 256, 16
HALF = 64
AH, AKV, AD = 16, 4, 128
GRP = AH // AKV
NB = 512
KH = 4
HB = 256
SLOTS = 4
EPS = 1e-6
NEG = -1e30
E_Z = 0
E_XBC = E_Z + SW
E_DT = E_XBC + XB * P
E_Q = E_DT + 2 * SH
E_K = E_Q + GH * GK
E_V = E_K + GH * GK
E_G = E_V + GH * GV
E_LR = E_G + GH * GV
KVW = AKV * AD
ORDER = [list(range(TT)), list(range(CT))[::-1] + list(range(CT, TT))[::-1]]

C_ID, C_LE, C_GT, C_GE, C_LT, C_ONE, C_GF, C_GB, C_SCAN = [i * P for i in range(9)]
C_COLS = C_SCAN + NB
M_COLS = (CTX + 2 * P) + (CTX + 3 * P)


def even_odd_layers(nc, x, c, ctx_in, c_ctx, e_norm, e_mod_w, e_mod_b, e_w_in, e_conv_w, e_conv_b, e_dt_bias,
                    e_a_log, e_d_skip, e_ssd_norm, e_gla_gate_w, e_gla_gate_b, e_gla_norm, e_w_out, o_norm,
                    o_mod_w, o_mod_b, o_w_in, o_q_norm, o_k_norm, o_sink, o_w_out, consts, masks, rope, out):
    f32, i32 = mybir.dt.float32, mybir.dt.int32
    ALU, ACT, AX = mybir.AluOpType, mybir.ActivationFunctionType, mybir.AxisListType
    es = ExitStack()

    def sb(name, shape):
        return es.enter_context(nc.sbuf_tensor(name, shape, f32))

    def sem(name):
        return es.enter_context(nc.semaphore(name))

    def spread(ap, axis, n):
        a = ap.unsqueeze(axis)
        shape = list(a.shape)
        shape[axis] = n
        return a.broadcast_to(shape)

    with es:
        SLAB = TT * DM
        f32r = mybir.dt.float32r
        base = (nc.sbuf_base + 31) // 32 * 32
        arena = sb("arena", [P, 6 * SLAB])
        ring = sb("ring", [P, SLOTS, KH, NB])
        slab_r = [nc.alloc_sbuf_tensor_at(f"slab_parts{i}", [P, SLAB], f32r, offset=base + 4 * SLAB * i) for i in range(6)]
        ring_r = nc.alloc_sbuf_tensor_at("ring_parts", [P, SLOTS, KT, HB], f32r, offset=base + 4 * 6 * SLAB)
        cst = sb("cst", [P, C_COLS])
        ident = cst[:, C_ID:C_ID + P]
        incl = [cst[:, C_LE:C_LE + P], cst[:, C_GE:C_GE + P]]
        strict = [cst[:, C_GT:C_GT + P], cst[:, C_LT:C_LT + P]]
        ones = cst[:, C_ONE:C_ONE + P]
        chunk_ok = [cst[:, C_GF:C_GF + P], cst[:, C_GB:C_GB + P]]
        scan_keep = cst[:, C_SCAN:C_SCAN + NB]
        vecs = sb("vecs", [P, 160])
        V_C, V_N, V_MB, V_CW, V_CB, V_GB, V_ON, V_OMB = 0, 16, 24, 48, 108, 120, 128, 136
        silu_c = sb("silu_c", [P, 16])
        mod = [sb("mod_e", [P, 24, 2]), sb("mod_o", [P, 24, 2])]
        small = sb("small", [P, 224])
        bc_small = sb("bc_small", [P, 96])
        dt_bias, a_log = bc_small[:, 0:32], bc_small[:, 32:64]
        d_skip, sink = bc_small[:, 64:80], bc_small[:, 80:96]
        dtv = sb("dtv", [P, TT, 32])
        dta = sb("dta", [P, TT, 32])
        gate_o = sb("gate_o", [P, DM])
        tail = sb("tail", [P, 3328])
        spare = sb("spare", [P, 1024])

        def slab(i, n=TT, w=DM):
            return arena[:, i * SLAB:i * SLAB + n * w].rearrange("p (n w) -> p n w", n=n)

        def parts(i):
            return slab_r[i][:, :].rearrange("p (t k c) -> p t k c", t=TT, k=KT)

        h_hi, h_lo = parts(5), parts(0)
        ys_hi, ys_lo = parts(2), parts(3)
        yg_hi, yg_lo = parts(5), parts(1)
        hT = [arena[:, s * SLAB:(s + 1) * SLAB].rearrange("p (t k c) -> p t k c", t=TT, k=KT) for s in (0, 2)]
        zs = slab(1)
        xT = arena[:, 2 * SLAB:2 * SLAB + 8 * TOK].rearrange("p (c t) -> p c t", c=8)
        y = slab(2)
        xs = slab(3)
        yT_ssd = arena[:, 3 * SLAB:4 * SLAB].rearrange("p (t k c) -> p t k c", t=TT, k=KT)
        bcT = arena[:, 4 * SLAB:4 * SLAB + 4 * TOK].rearrange("p (c t) -> p c t", c=4)
        b_tok = arena[:, 4 * SLAB + 3072:4 * SLAB + 4608].rearrange("p (t n) -> p t n", t=TT)
        s4 = 4 * SLAB + 4608
        xdt = [arena[:, s4:s4 + 512], spare[:, 0:512]]
        xw = [arena[:, s4 + 512:s4 + 1024], spare[:, 512:1024]]
        ytmp = arena[:, s4 + 1024:s4 + 1536]
        s5 = 5 * SLAB
        S_ssd = arena[:, s5:s5 + 2048].rearrange("p (d n) -> p d n", d=2)
        Edec = [arena[:, s5 + 2048 + 1024 * i:s5 + 3072 + 1024 * i].rearrange("p (h i) -> p h i", h=8) for i in (0, 1)]
        RD = [arena[:, s5 + 4096 + 1024 * i:s5 + 5120 + 1024 * i].rearrange("p (h i) -> p h i", h=8) for i in (0, 1)]
        RAW = TOK + 6
        raw = [arena[:, s5 + 2048 + RAW * i:s5 + 2048 + RAW * (i + 1)] for i in (0, 1)]
        cacc = [arena[:, s5 + 3600 + 772 * i:s5 + 3600 + 772 * i + TOK + 2] for i in (0, 1)]
        vrow1 = arena[:, s5:s5 + P]
        vrow2 = arena[0:32, s5 + P:s5 + 2 * P]
        junk = arena[:, 4 * SLAB:4 * SLAB + DM]
        w_small = tail[:, 0:512].rearrange("p (k n) -> p k n", k=KT)
        norm_bc = tail[:, 768:1792]
        lr_tok = tail[:, 512:704].rearrange("p (t n) -> p t n", t=TT)
        gate_w = tail[0:32, 1792:2816].rearrange("p (d n) -> p d n", d=2)
        cbm = tail[:, 2816:3328].rearrange("p (d g n) -> p d g n", d=2, g=2)
        lrT = tail[0:32, 0:TOK]
        vv = slab(1)
        gs = slab(2)
        qT_g = arena[:, 4 * SLAB:4 * SLAB + 4 * TOK].rearrange("p (c t) -> p c t", c=4)
        kT_g = arena[:, 4 * SLAB + 4 * TOK:5 * SLAB].rearrange("p (c t) -> p c t", c=4)
        og = slab(0)
        S_gla = arena[:, s5:s5 + 2048].rearrange("p (d h e) -> p d h e", d=2, h=GH)

        def five(i):
            return arena[:, s5 + 2048 + 512 * i:s5 + 2560 + 512 * i]

        def heads4(ap):
            return ap.rearrange("p (h n) -> p h n", h=4)

        attm = [heads4(five(0)), heads4(five(1))]
        qdec = [heads4(five(2)), heads4(five(3))]
        kutok = [heads4(five(4)), heads4(five(5))]
        gcs, gx = five(6), five(7)
        gl = tail[:, 2816:3328]
        grow, kk = spare[:, 0:512], spare[:, 512:1024]
        gshrink, ku = gate_o[:, 0:512], gate_o[:, 512:1024]
        mrow = tail[:, 1280:1792]
        sq_junk = dtv.rearrange("p t n -> p (t n)").bitcast(mybir.dt.bfloat16)[:, 0:GV]
        x1 = slab(0)
        gate_e = arena[:, 4 * SLAB:4 * SLAB + 2 * DM].rearrange("p (s n) -> p s n", s=2)
        etmp = [arena[:, 4 * SLAB + 2048 + HB * i:4 * SLAB + 2048 + HB * (i + 1)] for i in (0, 1)]
        junk_o = arena[:, 4 * SLAB + 3072:4 * SLAB + 3072 + DM]
        xn1 = slab(3)
        qT = arena[:, 3 * SLAB:3 * SLAB + 8192].rearrange("p (t h c) -> p t h c", t=LT, h=AH)
        sg = arena[:, 3 * SLAB + 8192:3 * SLAB + 16384].rearrange("p (t n) -> p t n", t=LT)
        tables = arena[:, 3 * SLAB + 16384:6 * SLAB].rearrange("p (a t n) -> p a t n", a=4, t=LT)
        kT = arena[:, SLAB:SLAB + AKV * TOK].rearrange("p (h t) -> p h t", h=AKV)
        va = arena[:, SLAB + 3072:2 * SLAB].rearrange("p (t n) -> p t n", t=TT)
        amask = arena[:, 0:M_COLS]
        s2 = 2 * SLAB
        prob = [arena[:, s2 + 640 * i:s2 + 640 * (i + 1)] for i in (0, 1)]
        probT = [arena[:, s2 + 1280 + 640 * i:s2 + 1920 + 640 * i].rearrange("p (b q) -> p b q", b=5) for i in (0, 1)]
        ogate = [arena[:, s2 + 2560 + 512 * i:s2 + 3072 + 512 * i] for i in (0, 1)]
        ftmp = [arena[:, s2 + 3584 + 512 * i:s2 + 4096 + 512 * i] for i in (0, 1)]
        rp = [[tail[:, 2048 * b + 512 * i:2048 * b + 512 * (i + 1)] for i in range(4 if b == 0 else 2)] for b in (0, 1)]
        rp[1] += [spare[:, 0:512], spare[:, 512:1024]]
        qk_gain = sb("qk_gain", [P, 2, AD])

        ps = es.enter_context(nc.psum_tensor("ps", [P, 8, NB], f32))

        def banks(b, n=1):
            return ps[:, b:b + n, :].rearrange("p b n -> p (b n)")

        def eo_out(n, t):
            return ps[:, 3 * (n % 2) + t // 2, HB * (t % 2):HB * (t % 2 + 1)]

        chunks, slot_of, arrivals, before, split = [], [], [], [], []
        owner, loads = [None] * SLOTS, [0] * SLOTS

        def add_chunk(src, slot, two):
            n = len(chunks)
            chunks.append(src)
            slot_of.append(slot)
            loads[slot] += 1
            arrivals.append(loads[slot])
            before.append((owner[slot], owner[slot + 2] if two else None))
            split.append(two)
            owner[slot] = n
            if two:
                owner[slot + 2] = n
            return n

        def plan(w, c0):
            return [add_chunk(w[0, KH * P * k:KH * P * (k + 1), c0:c0 + NB].rearrange("(j p) n -> p j n", p=P),
                              len(chunks) % SLOTS, False) for k in range(w.shape[1] // (KH * P))]

        def plan_split(w, c0, k0=0):
            return add_chunk(w[0, P * k0:P * (k0 + KT), c0:c0 + HB].rearrange("(j p) n -> p j n", p=P), sum(split) % 2, True)

        complete = [max(i for i in range(2 * TT) if ORDER[i % 2][i // 2] == t) for t in range(TT)]
        FIN = sorted(range(TT), key=lambda t: complete[t])
        norm_at = {9: [0], 10: [1, 2], 11: [3]}
        MB = 6
        mod_ch = [[plan(e_mod_w, NB * b) for b in range(4)], []]
        xbc_ch = [plan(e_w_in, E_XBC + NB * b) for b in range(XB // 4)]
        z_ch = [plan(e_w_in, E_Z + NB * b) for b in range(2)]
        qk_ch = [plan_split(e_w_in, E_Q + HB * b) for b in range(4)]
        v_ch = [plan_split(e_w_in, E_V + HB * b) for b in range(4)]
        g_ch = [plan_split(e_w_in, E_G + HB * b) for b in range(4)]
        mod_ch[0] += [plan(e_mod_w, NB * b) for b in range(4, MB)]
        mod_ch[1] += [plan(o_mod_w, NB * b) for b in range(MB)]
        eo_ch = [plan_split(e_w_out, HB * (q // 2), KT * (q % 2)) for q in range(8)]
        oin_ch = [plan(o_w_in, NB * b) for b in range(10)]
        oo_ch = [plan(o_w_out, NB * n) for n in range(2)]

        jobs = [("sm", 0, t) for t in range(TT)]
        jobs += [("xbc", cc, part) for cc in range(XB) for part in (0, 1)]
        jobs += [("z", n, t) for n in range(2) for t in range(TT)]
        JOBS_SSD = len(jobs)
        jobs += [("qk", cc, part) for cc in range(2 * GH) for part in (0, 1)]
        JOBS_QK = len(jobs)
        jobs += [("v", n, t) for n in range(4) for t in range(TT)]
        JOBS_V = len(jobs)
        jobs += [("g", n, t) for n in range(4) for t in range(TT)]
        JOBS_E = len(jobs)
        late = qk_ch + v_ch + g_ch
        first_job = {}
        for jj in range(JOBS_SSD, JOBS_E):
            kind, n, t = jobs[jj]
            first_job.setdefault({"qk": qk_ch[n // 2 % 4], "v": v_ch[n % 4], "g": g_ch[n % 4]}[kind], jj)
        ready_at = {first_job[late[q - 1]] + (2 if q <= 4 else 3): late[q] for q in range(2, len(late))}
        jobs += [("k", 0, t) for t in range(TT)] + [("va", 1, t) for t in range(TT)]
        jobs += [("q", 2 + n, t) for n in range(4) for t in range(CT, TT)]
        jobs += [("sg", 6 + n, t) for n in range(4) for t in range(CT, TT)]
        BY_DVE, BY_ACT = {"sm", "v", "va"}, {"xbc", "z", "qk", "g", "sg"}

        def emptied(j):
            d = jobs[j][0] in BY_DVE
            return d, sum(jobs[i][0] in (BY_DVE if d else BY_ACT) for i in range(j + 1))

        ropes = [j for j in range(len(jobs)) if jobs[j][0] in ("k", "q")]

        mod_mm = [sem("mod_mm_e"), sem("mod_mm_o")]
        proj_mm = sem("proj_mm")
        eo_mm, eo_w = sem("eo_mm"), sem("eo_w")
        oo_mm, oo_w = sem("oo_mm"), sem("oo_w")
        used = {}
        for l in (0, 1):
            for b, ch in enumerate(mod_ch[l]):
                used.update({n: (mod_mm[l], b + 1) for n in ch})
        for jj, (kind, n, t) in enumerate(jobs):
            ch = {"sm": [], "xbc": xbc_ch[n // 4 % 3], "z": z_ch[n % 2], "qk": [qk_ch[n // 2 % 4]], "v": [v_ch[n % 4]],
                  "g": [g_ch[n % 4]]}.get(kind, oin_ch[n % 10])
            used.update({m: (proj_mm, jj + 1) for m in ch})
        for n in range(2):
            for q in range(3):
                used[oo_ch[n][q]] = (oo_w, 3 * n + q + 1)
            used[oo_ch[n][3]] = (oo_mm, LT * (n + 1))
        for q in range(8):
            used[eo_ch[q]] = (eo_w, q // 2 + 1) if q % 2 == 0 else (eo_mm, q // 2 + 1)
        w_hi, w_lo = sem("w_hi"), sem("w_lo")
        h_hi_done, h_lo_done, ys_hi_done, ys_lo_done, gT_hi_done = (sem(n) for n in (
            "h_hi_done", "h_lo_done", "ys_hi_done", "ys_lo_done", "gT_hi_done"))
        ring_full = [sem(f"ring_full{i}") for i in range(SLOTS)]
        cst_in, vec_in, bc_in, wsm_in, gw_in, nb_in, nb2_in = [sem(n) for n in (
            "cst_in", "vec_in", "bc_in", "wsm_in", "gw_in", "ssd_norm_in", "gla_norm_in")]
        x_in = [sem(f"x_in{t}") for t in range(TT)]
        x1_in = [sem(f"x1_in{t}") for t in range(TT)]
        tab_in, mask_in, gain_in = sem("tab_in"), sem("mask_in"), sem("gain_in")
        gw_zero, conv_zero, S_zero = sem("gw_zero"), sem("conv_zero"), sem("S_zero")
        vec_T, vec_c, silu_done = sem("vec_T"), sem("vec_copied"), sem("silu_done")
        mod_done = [sem("mod_done_e"), sem("mod_done_o")]
        mod_row, mod_tr, mod_add = sem("mod_row"), sem("mod_tr"), sem("mod_add")
        late_mods = [(0, b) for b in range(4, MB)] + [(1, b) for b in range(MB)]
        rstd_in, xn_done, ht_tr, ht_done = ([sem(f"{n}{l}") for l in (0, 1)] for n in ("rstd_in", "xn_done", "ht_tr", "ht_done"))
        proj_dve, proj_act = sem("proj_dve"), sem("proj_act")
        lr_tr, lr_done = sem("lr_tr"), sem("lr_done")
        conv_done, xbc_done = sem("conv_done"), sem("xbc_done")
        xs_tr, xs_done, b_done = sem("xs_tr"), sem("xs_done"), sem("b_done")
        dtraw, soft_in, ea_done, dta_done, y_init = (sem(n) for n in ("dtraw", "soft_in", "ea_done", "dta_done", "y_init"))
        cb_mm, d_mm, yo_mm, u_mm, yd_mm = (sem(n) for n in ("cb_mm", "d_mm", "yo_mm", "u_mm", "yd_mm"))
        ex_done, cbm_done, rd_done, dec_done, a_done = (sem(n) for n in ("ex_done", "cbm_done", "rd_done", "dec_done", "a_done"))
        xw_done, sscale, s_new, tmp_done, y_added = (sem(n) for n in ("xw_done", "s_scaled", "s_new", "tmp_done", "y_added"))
        yz_done, ssd_rstd, yn_done, yT_tr, yT_done = (sem(n) for n in ("yz_done", "ssd_rstd", "yn_done", "yT_tr", "yT_done"))
        g_zero = sem("gla_zero")
        lg_mm, lg_x, lg_sp, cs_done, e1_done, qd_done = (sem(n) for n in ("lg_mm", "lg_x", "lg_sp", "cs_done", "e1_done", "qd_done"))
        e2_done, ki_done, at_mm, am_done = (sem(n) for n in ("e2_done", "ki_done", "at_mm", "am_done"))
        ku_done, ku_tr, kut_done = (sem(n) for n in ("ku_done", "ku_tr", "kut_done"))
        inter_mm, gu_mm, gs_new, o_added = (sem(n) for n in ("inter_mm", "gla_u_mm", "gla_s_new", "o_added"))
        g_rstd, gn_done, gg_done, gT_tr, gT_done = (sem(n) for n in ("gla_rstd", "gla_normed", "gla_gated", "gT_tr", "gT_done"))
        gr_mm, gr_done = sem("gate_row_mm"), sem("gate_row_done")
        eo_done = sem("eo_done")
        gain_done, rk_rstd, rk_t0, rk_b, rk_a, rk_r, rk_tr, rk_done = (sem(n) for n in (
            "tables_done", "rk_rstd", "rk_t0", "rk_b", "rk_a", "rk_r", "rk_tr", "rk_done"))
        sink_done = sem("sink_done")
        s_mm, mx_done, p_done, p_tr, pt_a, pt_d, pv_mm = (sem(n) for n in ("s_mm", "mx_done", "p_done", "p_tr", "pt_act", "pt_dve", "pv_mm"))
        dk_done, ek_done, on_done, og_done, ot_tr, ot_done = (sem(n) for n in ("dk_done", "ek_done", "on_done", "og_done", "ot_tr", "ot_done"))
        fin_done, out_done = sem("fin_done"), sem("out_done")
        dve_own, act_own, pool_own = sem("dve_own"), sem("act_own"), sem("pool_own")

        def part_hi(eng, op, n):
            eng.wait_ge(ring_full[slot_of[n]], 16 * arrivals[n])
            if before[n][1] is not None:
                eng.wait_ge(*used[before[n][1]])
            a = ring[:, slot_of[n], :, :].rearrange("p j n -> p (j n)")
            op(ring_r[:, slot_of[n] + 2, :, :].rearrange("p j n -> p (j n)"), a).then_inc(w_hi, 1)

        def part_lo(eng, n):
            eng.wait_ge(w_hi, sum(split[:n]) + 1)
            a, lo, hi = (r[:, q, :, :].rearrange("p j n -> p (j n)") for r, q in (
                (ring, slot_of[n]), (ring_r, slot_of[n]), (ring_r, slot_of[n] + 2)))
            eng.tensor_tensor(lo, a, hi.bitcast(f32), ALU.subtract).then_inc(w_lo, 1)

        def step(eng, own):
            n = [0]

            def do(ins):
                n[0] += 1
                ins.then_inc(own, 1)
                eng.wait_ge(own, n[0])
            return do

        block = es.enter_context(nc.Block())

        @block.sync
        def _(sp):
            def load(n):
                if before[n][0] is not None:
                    sp.wait_ge(*used[before[n][0]])
                place = ring[:, slot_of[n], :, :]
                if split[n]:
                    place = place.rearrange("p j (s n) -> p (j s) n", n=HB)
                sp.dma_start(place, chunks[n]).then_inc(ring_full[slot_of[n]], 16)

            for n in range(eo_ch[2]):
                load(n)
            sp.wait_ge(gT_tr, TT)
            for t in range(TT):
                src = ctx_in[0, P * t:P * (t + 1), :] if t < CT else x[0, P * (t - CT):P * (t - CT + 1), :]
                sp.dma_start(x1[:, t, :], src).then_inc(x1_in[t], 16)
            for n in range(eo_ch[2], oin_ch[0][0]):
                load(n)
            sp.wait_ge(eo_done, 4 * TT)
            for a in range(4):
                sp.dma_start(tables[:, a, :, :], rope[a // 2, :, :].rearrange("(t p) n -> p t n", p=P)).then_inc(tab_in, 16)
            for n in range(oin_ch[0][0], oin_ch[2][0]):
                load(n)
            sp.wait_ge(ht_tr[1], 2 * KT)
            sp.wait_ge(xn_done[1], TT)
            sp.dma_start(amask, masks).then_inc(mask_in, 16)
            for n in range(oin_ch[2][0], len(chunks)):
                load(n)
            for n in range(2):
                for t in range(LT):
                    sp.wait_ge(fin_done, n * LT + t + 1)
                    sp.dma_start(out[0, P * t:P * (t + 1), NB * n:NB * (n + 1)],
                                 x1[:, CT + t, NB * n:NB * (n + 1)]).then_inc(out_done, 16)
            sp.wait_ge(out_done, 16 * 2 * LT)

        @block.gpsimd
        def _(pool):
            do = step(pool, pool_own)
            pool.memset(gate_w, 0.0).then_inc(gw_zero, 1)
            pool.memset(arena[:, s5 + 2048:s5 + 2048 + 2 * RAW], 0.0).then_inc(conv_zero, 1)
            pool.memset(cbm, 0.0).then_inc(conv_zero, 1)
            pool.dma_start(w_small[:, :, 0:32], e_w_in[0, :, E_DT:E_DT + 32].rearrange("(k p) n -> p k n", p=P)).then_inc(wsm_in, 16)
            pool.dma_start(w_small[:, :, 32:64], e_w_in[0, :, E_LR:E_LR + 32].rearrange("(k p) n -> p k n", p=P)).then_inc(wsm_in, 16)
            pool.wait_ge(gw_zero, 1)
            for d in range(2):
                pool.dma_start(gate_w[RANK * d:RANK * (d + 1), d, :], e_gla_gate_w[0, d, :, :]).then_inc(gw_in, 16)
            pool.dma_start(qk_gain[:, 0, :], o_q_norm[0, :].partition_broadcast(P)).then_inc(gain_in, 16)
            pool.dma_start(qk_gain[:, 1, :], o_k_norm[0, :].partition_broadcast(P)).then_inc(gain_in, 16)
            pool.wait_ge(mod_tr, 4)
            pool.dma_start(norm_bc, e_ssd_norm[0, :].partition_broadcast(P)).then_inc(nb_in, 16)
            pool.wait_ge(xs_tr, TT)
            pool.wait_ge(bc_in, 64)
            for t in range(TT):
                pool.wait_ge(xs_done, t + 1)
                pool.tensor_tensor(y[:, t, :].rearrange("p (h e) -> p h e", h=SH), xs[:, t, :].rearrange("p (h e) -> p h e", h=SH),
                                   spread(d_skip, 2, SD), ALU.mult).then_inc(y_init, 1)
            pool.memset(S_ssd, 0.0).then_inc(S_zero, 1)
            pool.wait_ge(S_zero, 1)
            pool.wait_ge(y_init, TT)
            pool.wait_ge(dta_done, 1)
            for u in range(4 * TT + 1):
                if u < 4 * TT:
                    s, g = u // 2, u % 2
                    d, t = s % 2, ORDER[s % 2][s // 2]
                    dts = dtv[:, t, SH * d + 8 * g:SH * d + 8 * g + 8]
                    xg = xs[:, t, GW * g:GW * (g + 1)].rearrange("p (h e) -> p h e", h=8)
                    ex = small[:, 48 * d:48 * d + 48]
                    if u >= 2:
                        pool.wait_ge(yd_mm, u - 1)
                        pool.wait_ge(u_mm, u - 1)
                    do(pool.tensor_tensor(xdt[u % 2].rearrange("p (h e) -> p h e", h=8), xg, spread(dts, 2, SD), ALU.mult))
                    pool.wait_ge(ex_done, s + 1)
                    pool.tensor_tensor(xw[u % 2].rearrange("p (h e) -> p h e", h=8), xdt[u % 2].rearrange("p (h e) -> p h e", h=8),
                                       spread(ex[:, 16 + 8 * g:24 + 8 * g], 2, SD), ALU.mult).then_inc(xw_done, 1)
                if u >= 1:
                    v = u - 1
                    s, g = v // 2, v % 2
                    d, t = s % 2, ORDER[s % 2][s // 2]
                    ex = small[:, 48 * d:48 * d + 48]
                    Sg = S_ssd[:, d, GW * g:GW * (g + 1)].rearrange("p (h e) -> p h e", h=8)
                    pool.wait_ge(yo_mm, v + 1)
                    if v >= 4:
                        pool.wait_ge(s_new, v - 3)
                    pool.tensor_tensor(Sg, Sg, spread(ex[:, 32 + 8 * g:40 + 8 * g], 2, SD), ALU.mult).then_inc(sscale, 1)
                    pool.wait_ge(tmp_done, v + 1)
                    if v >= 2:
                        pool.wait_ge(y_added, v - 1)
                    yg = y[:, t, GW * g:GW * (g + 1)]
                    pool.tensor_tensor(yg, yg, ytmp, ALU.add).then_inc(y_added, 1)
            pool.wait_ge(proj_mm, JOBS_E)
            pool.memset(arena[:, s5:s5 + 2048], 0.0).then_inc(g_zero, 1)
            pool.memset(arena[:, s5 + 2048:s5 + 3072], 0.0).then_inc(g_zero, 1)
            pool.wait_ge(proj_act, emptied(JOBS_QK - 1)[1])
            pool.wait_ge(u_mm, 4 * TT)

            def keys(i):
                d, t = i % 2, ORDER[i % 2][i // 2]
                end = HALF - 1 if d == 0 else 0
                pool.wait_ge(e2_done, i + 1)
                if i >= 1:
                    pool.wait_ge(at_mm, i)
                pool.tensor_tensor(heads4(kk), kT_g[:, :, P * t:P * (t + 1)], heads4(gshrink), ALU.mult).then_inc(ki_done, 1)
                pool.wait_ge(ki_done, i + 1)
                if i >= 1:
                    pool.wait_ge(ku_tr, i)
                pool.tensor_tensor(ku.rearrange("p (h n) -> p h n", n=HALF), kk.rearrange("p (h n) -> p h n", n=HALF),
                                   spread(grow.rearrange("p (h n) -> p h n", n=HALF)[:, :, end], 2, HALF), ALU.mult).then_inc(ku_done, 1)

            def gate_tile(n):
                t = FIN[n]
                pool.wait_ge(proj_act, emptied(JOBS_E - 1)[1])
                pool.wait_ge(gn_done, n + 1)
                pool.tensor_tensor(og[:, t, :], og[:, t, :], gs[:, t, :], ALU.mult).then_inc(gg_done, 1)

            keys(0)
            for i in range(2 * TT):
                if i + 1 < 2 * TT:
                    keys(i + 1)
                if i == len(late_mods) - 1:
                    pool.wait_ge(mod_tr, 4 + len(late_mods))
                    pool.dma_start(norm_bc, e_gla_norm[0, :].partition_broadcast(P)).then_inc(nb2_in, 16)
                for n in norm_at.get(i, []):
                    gate_tile(n)
            for n in range(sum(len(v) for v in norm_at.values()), TT):
                gate_tile(n)
            for r, j in enumerate(ropes):
                kind, n, t = jobs[j]
                t0, A, B, R = rp[r % 2]
                if kind == "k" and t < CT:
                    continue
                rot = r - CT
                a = 2 if kind == "q" else 3
                pool.wait_ge(rk_t0, r + 1)
                pool.wait_ge(gain_done, 4)
                pool.tensor_tensor(heads4(B), heads4(t0), spread(tables[:, a, t - CT, :], 1, 4), ALU.mult).then_inc(rk_b, 1)
                pool.wait_ge(rk_b, rot + 1)
                pool.wait_ge(rk_a, rot + 1)
                if r >= 2:
                    pool.wait_ge(rk_tr, r - 1)
                A4, B4, R4 = (m.rearrange("p (a s f) -> p a s f", s=2, f=32) for m in (A, B, R))
                pool.tensor_tensor(R4[:, :, 0, :], A4[:, :, 0, :], B4[:, :, 1, :], ALU.add)
                pool.tensor_tensor(R4[:, :, 1, :], A4[:, :, 1, :], B4[:, :, 0, :], ALU.add).then_inc(rk_r, 1)
            for G in range(LT * AKV):
                pool.wait_ge(on_done, G + 1)
                t, g4 = G // AKV, G % AKV
                pool.wait_ge(proj_act, emptied(len(jobs) - 1)[1])
                og_ = ogate[G % 2]
                pool.tensor_tensor(og_, og_, sg[:, t, NB * g4:NB * (g4 + 1)], ALU.mult).then_inc(og_done, 1)

        @block.scalar
        def _(act):
            do = step(act, act_own)
            act.dma_start(cst[:, :], consts).then_inc(cst_in, 16)
            for r0, n, src in ((0, 8, c[0, :]), (8, 8, c_ctx[:]), (16, 8, e_norm[0, :]), (24, 24, e_mod_b[0, :]),
                               (48, 60, e_conv_w[0, :, :]), (108, 12, e_conv_b[0, :]), (120, 8, e_gla_gate_b[0, :, :])):
                src = src.rearrange("(r p) -> r p", p=P) if len(src.shape) == 1 else src.rearrange("k (r p) -> (k r) p", p=P)
                act.dma_start(vrow1[r0:r0 + n, :], src).then_inc(vec_in, 16)
            for r0, n, src in ((0, 8, o_norm[0, :]), (8, 24, o_mod_b[0, :])):
                act.dma_start(vrow2[r0:r0 + n, :], src.rearrange("(r p) -> r p", p=P)).then_inc(vec_in, 16)
            for t in range(TT):
                src = ctx_in[0, P * t:P * (t + 1), :] if t < CT else x[0, P * (t - CT):P * (t - CT + 1), :]
                act.dma_start(xs[:, t, :], src).then_inc(x_in[t], 16)
            for c0, src in ((0, e_dt_bias[0, :, :].rearrange("a b -> (a b)")), (32, e_a_log[0, :, :].rearrange("a b -> (a b)")),
                            (64, e_d_skip[0, :]), (80, o_sink[0, :])):
                act.dma_start(bc_small[:, c0:c0 + src.shape[0]], src.partition_broadcast(P)).then_inc(bc_in, 16)
            act.wait_ge(vec_c, 1)
            act.activation(silu_c[:, :], banks(3)[:, 0:16], ACT.Silu).then_inc(silu_done, 1)

            def inv_rms(ss, width):
                do(act.activation(ss, ss, ACT.Copy, scale=1.0 / width, bias=EPS))
                do(act.activation(ss, ss, ACT.Ln))
                return act.activation(ss, ss, ACT.Exp, scale=-0.5)

            def token_rstd(l):
                src = (xs, x1)[l]
                ss = small[:, 96:96 + TT]
                for t in range(TT):
                    if l == 0:
                        act.wait_ge(x_in[t], 16)
                    else:
                        act.wait_ge(eo_done, 3 * TT + t + 1)
                    do(act.activation((junk, junk_o)[l], src[:, t, :], ACT.Square, accum_out=ss[:, t:t + 1]))
                inv_rms(ss, DM).then_inc(rstd_in[l], 1)

            token_rstd(0)

            def mod_rows(n, l, b, bank):
                act.wait_ge(mod_mm[l], b + 1)
                if n >= 1:
                    act.wait_ge(mod_tr, n)
                act.activation(mrow[0:2, :], banks(bank)[0:2, :], ACT.Copy).then_inc(mod_row, 1)

            for b in range(4):
                mod_rows(b, 0, b, b % 2)

            def hi_of(out_, in_):
                return act.activation(out_, in_, ACT.Copy)

            def proj_evac(j):
                kind, n, t = jobs[j]
                act.wait_ge(proj_mm, j + 1)
                bank = banks(j % 2)
                if kind == "xbc":
                    if n >= 2:
                        act.wait_ge(conv_done, n - 1)
                    if n < 2:
                        act.wait_ge(conv_zero, 2)
                    o0, w = (2, CTX) if t == 0 else (CTX + 4, LAT)
                    ins = act.activation(raw[n % 2][:, o0:o0 + w], bank[:, 0:w], ACT.Copy)
                elif kind == "z":
                    ins = act.activation(zs[:, t, NB * n:NB * (n + 1)], bank, ACT.Silu)
                elif kind == "qk":
                    o0, w = (0, CTX) if t == 0 else (CTX, LAT)
                    dst = (qT_g if n < GH else kT_g)[:, n % GH, o0:o0 + w]
                    ins = act.activation(dst, bank[:, 0:w], ACT.Copy, scale=float(GK) ** -0.5 if n < GH else 1.0)
                elif kind == "g":
                    ins = act.activation(gs[:, t, HB * n:HB * (n + 1)], bank[:, 0:HB], ACT.Silu)
                else:
                    ins = act.activation(sg[:, t - CT, NB * (n - 6):NB * (n - 5)], bank, ACT.Silu)
                ins.then_inc(proj_act, 1)

            def conv_silu(cc):
                act.wait_ge(conv_done, cc + 1)
                dst = xT[:, cc, :] if cc < 8 else bcT[:, cc - 8, :]
                act.activation(dst[:, 0:CTX], cacc[cc % 2][:, 0:CTX], ACT.Silu)
                act.activation(dst[:, CTX:TOK], cacc[cc % 2][:, CTX + 2:TOK + 2], ACT.Silu).then_inc(xbc_done, 1)

            j = TT
            act.wait_ge(ht_tr[0], 2 * KT)
            for cc in range(XB):
                proj_evac(j)
                proj_evac(j + 1)
                j += 2
                if cc >= 1:
                    conv_silu(cc - 1)
            conv_silu(XB - 1)
            while j < JOBS_SSD:
                proj_evac(j)
                j += 1
            act.wait_ge(dtraw, TT)
            a3 = dta[:, :, :]
            do(act.activation(a3, dtv[:, :, :], ACT.Abs))
            do(act.activation(a3, a3, ACT.Exp, scale=-1.0))
            act.activation(a3, a3, ACT.Ln, bias=1.0).then_inc(soft_in, 1)
            act.wait_ge(bc_in, 64)
            act.activation(a_log, a_log, ACT.Exp).then_inc(ea_done, 1)
            for t in range(TT):
                act.wait_ge(xs_tr, t + 1)
                act.activation(xs[:, t, :], banks(2 + 3 * (t % 2), 2), ACT.Copy).then_inc(xs_done, 1)
            for u in range(4 * TT):
                s, g = u // 2, u % 2
                if g == 0:
                    d = s % 2
                    act.wait_ge(cb_mm, s + 1)
                    if s >= 2:
                        act.wait_ge(y_added, 2 * (s - 1))
                        act.wait_ge(sscale, 2 * (s - 1))
                    act.activation(small[:, 48 * d:48 * d + 48], banks(7)[:, 48 * d:48 * d + 48], ACT.Exp).then_inc(ex_done, 1)
                if u in (14, 16):
                    part_hi(act, hi_of, late[(u - 14) // 2])
                act.wait_ge(d_mm, u + 1)
                if u >= 2:
                    act.wait_ge(yd_mm, u - 1)
                act.activation(Edec[u % 2].rearrange("p h i -> p (h i)"), banks(2, 2), ACT.Exp).then_inc(dec_done, 1)
            act.wait_ge(s_new, 4 * TT)
            act.wait_ge(a_done, 4 * TT)
            act.wait_ge(yd_mm, 4 * TT)
            for t in range(TT):
                act.activation(h_hi[:, t, :, :], hT[0][:, t, :, :], ACT.Copy).then_inc(h_hi_done, 1)
            ss = small[:, 104:104 + 2 * TT]
            for t in range(TT):
                act.wait_ge(yz_done, t + 1)
                for g in range(SG):
                    do(act.activation(junk[:, 0:GW], y[:, t, GW * g:GW * (g + 1)], ACT.Square, accum_out=ss[:, 2 * t + g:2 * t + g + 1]))
            inv_rms(ss, GW).then_inc(ssd_rstd, 1)
            while j < JOBS_QK:
                if j in ready_at:
                    part_hi(act, hi_of, ready_at[j])
                proj_evac(j)
                j += 1

            def out_T(dst, tr, done):
                for t in range(TT):
                    act.wait_ge(tr, t + 1)
                    act.activation(dst[:, t, :, :].rearrange("p k c -> p (k c)"), banks(2 + 2 * (t % 2), 2), ACT.Copy).then_inc(done, 1)

            out_T(yT_ssd, yT_tr, yT_done)
            while j < JOBS_E:
                if j in ready_at:
                    part_hi(act, hi_of, ready_at[j])
                if jobs[j][0] == "g":
                    proj_evac(j)
                j += 1
            act.preload_act_table_set("natural_log_exp_and_others")
            act.wait_ge(a_done, 4 * TT)
            act.wait_ge(yd_mm, 4 * TT)
            act.wait_ge(u_mm, 4 * TT)
            act.wait_ge(yn_done, TT)

            def soft(i):
                act.wait_ge(lg_x, i + 1)
                if i >= 1:
                    act.wait_ge(cs_done, i)
                do(act.activation(gl, gx, ACT.Abs))
                do(act.activation(gl, gl, ACT.Exp, scale=-1.0))
                act.activation(gl, gl, ACT.Ln, bias=1.0).then_inc(lg_sp, 1)

            def exps(i):
                act.wait_ge(cs_done, i + 1)
                if i >= 1:
                    act.wait_ge(qd_done, i)
                    act.wait_ge(ku_done, i)
                act.activation(grow, gcs, ACT.Exp, scale=1.0 / 16).then_inc(e1_done, 1)
                act.activation(gshrink, gcs, ACT.Exp, scale=-1.0 / 16).then_inc(e2_done, 1)

            def key_rows(i):
                act.wait_ge(ku_tr, i + 1)
                if i >= 2:
                    act.wait_ge(gu_mm, 4 * (i - 1))
                act.activation(kutok[i % 2].rearrange("p h n -> p (h n)"), banks(7), ACT.Copy).then_inc(kut_done, 1)

            def tile_rstd(n):
                t = FIN[n]
                ss = small[:, 116 + GH * t:116 + GH * (t + 1)]
                act.wait_ge(o_added, complete[t] + 1)
                for h in range(GH):
                    do(act.activation(sq_junk, og[:, t, GV * h:GV * (h + 1)], ACT.Square, accum_out=ss[:, h:h + 1]))
                inv_rms(ss, GV).then_inc(g_rstd, 1)

            soft(0)
            mod_rows(4, *late_mods[0], 0)
            exps(0)
            soft(1)
            key_rows(0)
            exps(1)
            for i in range(2 * TT):
                if i + 1 < len(late_mods):
                    mod_rows(5 + i, *late_mods[i + 1], 0)
                if i + 2 < 2 * TT:
                    soft(i + 2)
                if i + 1 < 2 * TT:
                    key_rows(i + 1)
                if i + 2 < 2 * TT:
                    exps(i + 2)
                for n in range(TT):
                    if complete[FIN[n]] == i - 1:
                        tile_rstd(n)
                if i in (8, 9):
                    part_hi(act, hi_of, eo_ch[i - 8])
            tile_rstd(TT - 1)
            for n, t in enumerate(FIN):
                act.wait_ge(gg_done, n + 1)
                act.activation(ys_hi[:, t, :, :], yT_ssd[:, t, :, :], ACT.Copy).then_inc(ys_hi_done, 1)
                act.wait_ge(gT_tr, n + 1)
                act.activation(yg_hi[:, t, :, :].rearrange("p k c -> p (k c)"), banks(2 + 2 * (n % 2), 2), ACT.Copy).then_inc(gT_hi_done, 1)
            for q in range(3):
                act.wait_ge(gr_mm, q + 1)
                dst = gate_e[:, q, :] if q < 2 else gate_o[:, :]
                act.activation(dst, banks(2 + 2 * (q % 2), 2), ACT.Copy).then_inc(gr_done, 1)
            for q in range(2, 8):
                part_hi(act, hi_of, eo_ch[q])
            token_rstd(1)

            def rope_rstd(r, j):
                ss = small[:, 140 + 4 * (r % 2):144 + 4 * (r % 2)]
                act.wait_ge(proj_mm, j + 1)
                if r >= 2:
                    act.wait_ge(rk_t0, r - 1)
                for h in range(4):
                    do(act.activation(vecs[:, 0:AD], banks(j % 2)[:, AD * h:AD * (h + 1)], ACT.Square, accum_out=ss[:, h:h + 1]))
                inv_rms(ss, AD).then_inc(rk_rstd, 1)

            def rope_T(r):
                kind, n, t = jobs[ropes[r]]
                act.wait_ge(rk_tr, r + 1)
                src = heads4(banks(2 + r % 2))
                if kind == "k":
                    dst = kT[:, :, P * t:P * (t + 1)]
                else:
                    dst = qT[:, t - CT, 4 * (n - 2):4 * (n - 1), :]
                act.activation(dst, src, ACT.Copy).then_inc(rk_done, 1)

            act.wait_ge(ht_tr[1], 2 * KT)
            r = 0
            for j in range(JOBS_E, len(jobs)):
                if jobs[j][0] in ("k", "q"):
                    rope_rstd(r, j)
                    r += 1
                elif jobs[j][0] == "sg":
                    proj_evac(j)
                if j - 2 in ropes:
                    rope_T(ropes.index(j - 2))
            def probs(a):
                t, h = a // AH, a % AH
                nk = CTX + P * (3 if 0 < t < LT - 1 else 2)
                act.wait_ge(mx_done, a + 1)
                if h % GRP == 0 and t >= 1:
                    act.wait_ge(on_done, a // GRP - AKV + 1)
                act.activation(prob[a % 2][:, 0:nk], prob[a % 2][:, 0:nk], ACT.Exp, scale=-1.0, bias=small[:, 160 + h:161 + h],
                               accum_out=small[:, 176 + h:177 + h]).then_inc(p_done, 1)

            def probs_T(a):
                act.wait_ge(p_tr, a + 1)
                if a >= 2:
                    act.wait_ge(pv_mm, a - 1)
                act.activation(probT[a % 2][:, 0:4, :].rearrange("p b q -> p (b q)"), banks(6), ACT.Copy).then_inc(pt_a, 1)

            NA = LT * AH
            for a in range(NA + 1):
                if a < NA:
                    probs(a)
                if a >= 1:
                    v = a - 1
                    probs_T(v)
                    if v % GRP == GRP - 1:
                        G = v // GRP
                        g4 = G % AKV
                        act.wait_ge(dk_done, G + 1)
                        act.activation(small[:, 192 + 4 * g4:196 + 4 * g4], small[:, 192 + 4 * g4:196 + 4 * g4], ACT.Exp).then_inc(ek_done, 1)
                    if v % GRP == 1 and v >= GRP:
                        G = v // GRP - 1
                        act.wait_ge(ot_tr, G + 1)
                        act.activation(qT[:, G // AKV, 4 * (G % AKV):4 * (G % AKV) + 4, :].rearrange("p h c -> p (h c)"), banks(1), ACT.Copy).then_inc(ot_done, 1)
            G = LT * AKV - 1
            act.wait_ge(ot_tr, G + 1)
            act.activation(qT[:, G // AKV, 4 * (G % AKV):4 * (G % AKV) + 4, :].rearrange("p h c -> p (h c)"), banks(1), ACT.Copy).then_inc(ot_done, 1)

        @block.vector
        def _(dve):
            do = step(dve, dve_own)
            dve.wait_ge(vec_T, 1)
            dve.tensor_copy(vecs[:, :], banks(3)[:, 0:160]).then_inc(vec_c, 1)
            dve.wait_ge(vec_c, 1)

            def mod_block(n, l, b, bank):
                mb = vecs[:, (V_MB, V_OMB)[l] + 4 * b:(V_MB, V_OMB)[l] + 4 * b + 4]
                dve.wait_ge(mod_tr, n + 1)
                dve.tensor_tensor(mod[l][:, 4 * b:4 * b + 4, :], banks(bank)[:, 0:8].rearrange("p (m s) -> p m s", s=2),
                                  spread(mb, 2, 2), ALU.add).then_inc(mod_add, 1)

            def scale_gain(l, n):
                g = vecs[:, (V_N, V_ON)[l]:(V_N, V_ON)[l] + KT]
                dve.wait_ge(mod_add, n)
                dve.scalar_tensor_tensor(mod[l][:, 8:16, :], mod[l][:, 8:16, :], 1.0, spread(g, 2, 2), ALU.add, ALU.mult).then_inc(mod_done[l], 1)

            def normalise(l):
                dve.wait_ge(rstd_in[l], 1)
                src, dst = ((xs, xs), (x1, xn1))[l]
                for t in [2, 3, 4, 5, 0, 1]:
                    dve.tensor_scalar(dst[:, t, :], src[:, t, :], small[:, 96 + t:97 + t], None, ALU.mult).then_inc(xn_done[l], 1)
                dve.wait_ge(mod_done[l], 1)
                for q in range(2 * KT):
                    kt, s = q % KT, q // KT
                    t0, n = (CT, LT) if s == 0 else (0, CT)
                    dve.wait_ge(ht_tr[l], q + 1)
                    dve.tensor_scalar(hT[l][:, t0:t0 + n, kt, :], banks(4 + q % 2)[:, 0:n * P].rearrange("p (t c) -> p t c", t=n),
                                      mod[l][:, 8 + kt, s:s + 1], mod[l][:, kt, s:s + 1], ALU.mult, ALU.add).then_inc(ht_done[l], 1)

            for b in range(4):
                mod_block(b, 0, b, 2)
            scale_gain(0, 4)
            normalise(0)

            dve.wait_ge(bc_in, 64)
            for t in range(TT):
                dve.wait_ge(proj_mm, t + 1)
                dve.tensor_tensor(dtv[:, t, :], banks(t % 2)[:, 0:32], dt_bias, ALU.add).then_inc(dtraw, 1)
                dve.tensor_copy(lr_tok[:, t, :], banks(t % 2)[:, 32:64]).then_inc(proj_dve, 1)
            dve.wait_ge(lr_tr, 1)
            dve.tensor_copy(lrT[:, 0:NB], banks(6)[0:32, :])
            dve.tensor_copy(lrT[:, NB:TOK], banks(7)[0:32, 0:TOK - NB]).then_inc(lr_done, 1)
            for cc in range(XB):
                dve.wait_ge(proj_act, 2 * cc + 2)
                if cc >= 2:
                    dve.wait_ge(xbc_done, cc - 1)
                acc = cacc[cc % 2]
                for k in range(CONV_K):
                    w = vecs[:, V_CW + XB * k + cc:V_CW + XB * k + cc + 1]
                    src = raw[cc % 2][:, k:k + TOK + 2]
                    if k == 0:
                        do(dve.tensor_scalar(acc, src, w, vecs[:, V_CB + cc:V_CB + cc + 1], ALU.mult, ALU.add))
                    elif k < CONV_K - 1:
                        do(dve.scalar_tensor_tensor(acc, src, w, acc, ALU.mult, ALU.add))
                    else:
                        dve.scalar_tensor_tensor(acc, src, w, acc, ALU.mult, ALU.add).then_inc(conv_done, 1)
            dve.wait_ge(soft_in, 1)
            dve.wait_ge(dtraw, TT)
            do(dve.scalar_tensor_tensor(dtv[:, :, :], dtv[:, :, :], 0.0, dta[:, :, :], ALU.max, ALU.add))
            dve.wait_ge(ea_done, 1)
            dve.scalar_tensor_tensor(dta[:, :, :], dtv[:, :, :], -1.0, spread(a_log, 1, TT), ALU.mult, ALU.mult).then_inc(dta_done, 1)
            for t in range(TT):
                dve.wait_ge(xs_tr, t + 1)
                dve.tensor_copy(b_tok[:, t, :], banks(4 + 3 * (t % 2))[:, 0:2 * P]).then_inc(b_done, 1)
            dve.wait_ge(dta_done, 1)

            def decay_rhs(u):
                s, g = u // 2, u % 2
                d, t = s % 2, ORDER[s % 2][s // 2]
                if u >= 2:
                    dve.wait_ge(d_mm, u - 1)
                dve.tensor_tensor(RD[u % 2], spread(dta[:, t, SH * d + 8 * g:SH * d + 8 * g + 8], 2, P), spread(incl[d], 1, 8),
                                  ALU.mult).then_inc(rd_done, 1)

            def mask_cb(s):
                dve.wait_ge(cb_mm, s + 1)
                dve.wait_ge(ex_done, s + 1)
                if s >= 2:
                    dve.wait_ge(a_done, 2 * (s - 1))
                dve.copy_predicated(cbm[:, s % 2, :, :], spread(incl[s % 2].bitcast(i32), 1, 2),
                                    banks(7)[:, 128:384].rearrange("p (g n) -> p g n", g=2)).then_inc(cbm_done, 1)

            dve.wait_ge(conv_zero, 2)
            decay_rhs(0)
            mask_cb(0)
            for u in range(4 * TT):
                s, g = u // 2, u % 2
                d = s % 2
                ex = small[:, 48 * d:48 * d + 48]
                if u in (15, 17):
                    part_lo(dve, late[(u - 15) // 2])
                if u + 1 < 4 * TT:
                    decay_rhs(u + 1)
                dve.wait_ge(dec_done, u + 1)
                dve.wait_ge(cbm_done, s + 1)
                dve.tensor_tensor(Edec[u % 2], Edec[u % 2], spread(cbm[:, d, g, :], 1, 8), ALU.mult).then_inc(a_done, 1)
                if g == 1 and s + 1 < 2 * TT:
                    mask_cb(s + 1)
                dve.wait_ge(yo_mm, u + 1)
                dve.wait_ge(ex_done, s + 1)
                if u >= 1:
                    dve.wait_ge(y_added, u)
                do(dve.tensor_tensor(ytmp.rearrange("p (h e) -> p h e", h=8), banks(5).rearrange("p (h e) -> p h e", h=8),
                                     spread(ex[:, 8 * g:8 * g + 8], 2, SD), ALU.mult))
                dve.wait_ge(yd_mm, u + 1)
                dve.tensor_tensor(ytmp, ytmp, banks(4), ALU.add).then_inc(tmp_done, 1)
                dve.wait_ge(u_mm, u + 1)
                dve.wait_ge(sscale, u + 1)
                Sg = S_ssd[:, d, GW * g:GW * (g + 1)]
                dve.tensor_tensor(Sg, Sg, banks(6), ALU.add).then_inc(s_new, 1)
            for t in range(TT):
                dve.wait_ge(h_hi_done, t + 1)
                dve.tensor_tensor(h_lo[:, t, :, :], hT[0][:, t, :, :], h_hi[:, t, :, :].bitcast(f32), ALU.subtract).then_inc(h_lo_done, 1)
            dve.wait_ge(y_added, 4 * TT)
            dve.wait_ge(proj_act, emptied(JOBS_SSD - 1)[1])
            for t in range(TT):
                dve.tensor_tensor(y[:, t, :], y[:, t, :], zs[:, t, :], ALU.mult).then_inc(yz_done, 1)
            dve.wait_ge(ssd_rstd, 1)
            dve.wait_ge(nb_in, 16)
            dve.wait_ge(yz_done, TT)
            for t in range(TT):
                for g in range(SG):
                    yg = y[:, t, GW * g:GW * (g + 1)]
                    ins = dve.scalar_tensor_tensor(yg, yg, small[:, 104 + 2 * t + g:105 + 2 * t + g], norm_bc[:, GW * g:GW * (g + 1)],
                                                   ALU.mult, ALU.mult)
                ins.then_inc(yn_done, 1)
            for j in range(JOBS_SSD, JOBS_E):
                kind, n, t = jobs[j]
                if j in ready_at:
                    part_lo(dve, ready_at[j])
                if kind == "v":
                    dve.wait_ge(proj_mm, j + 1)
                    dve.tensor_copy(vv[:, t, HB * n:HB * (n + 1)], banks(j % 2)[:, 0:HB]).then_inc(proj_dve, 1)

            def log_gates(i):
                d = i % 2
                dve.wait_ge(lg_mm, i + 1)
                if i >= 1:
                    dve.wait_ge(cs_done, i)
                dve.tensor_tensor(heads4(gx), heads4(banks(1)), spread(vecs[:, V_GB + 4 * d:V_GB + 4 * d + 4], 2, P), ALU.add).then_inc(lg_x, 1)

            def decays(i):
                d = i % 2
                dve.wait_ge(lg_sp, i + 1)
                dve.wait_ge(lg_x, i + 1)
                do(dve.scalar_tensor_tensor(gx, gx, 0.0, gl, ALU.min, ALU.subtract))
                if i >= 1:
                    dve.wait_ge(e2_done, i)
                o_, i_ = (gcs, gx) if d == 0 else (gcs[:, ::-1], gx[:, ::-1])
                dve.tensor_tensor_scan(o_, scan_keep, i_, 0.0, ALU.mult, ALU.add).then_inc(cs_done, 1)

            def dec_queries(i):
                d, t = i % 2, ORDER[i % 2][i // 2]
                end = HALF - 1 if d == 0 else 0
                dve.wait_ge(e1_done, i + 1)
                if i >= 2:
                    dve.wait_ge(inter_mm, 2 * (i - 1))
                    dve.wait_ge(gs_new, 4 * (i - 1))
                dve.tensor_copy(small[:, 208 + 8 * d:216 + 8 * d], grow.rearrange("p (h n) -> p h n", n=HALF)[:, :, end])
                dve.tensor_tensor(qdec[d], qT_g[:, :, P * t:P * (t + 1)], heads4(grow), ALU.mult).then_inc(qd_done, 1)

            def mask_att(i):
                dve.wait_ge(at_mm, i + 1)
                if i >= 2:
                    dve.wait_ge(inter_mm, 2 * (i - 1))
                dve.copy_predicated(attm[i % 2], spread(chunk_ok[i % 2].bitcast(i32), 1, 4), heads4(banks(6))).then_inc(am_done, 1)

            def states(i, a):
                d = i % 2
                half = a if d == 0 else 1 - a
                dve.wait_ge(inter_mm, 2 * i + a + 1)
                dve.wait_ge(qd_done, i + 1)
                for h in range(GH):
                    if h % 2 == 0:
                        dve.wait_ge(gu_mm, 2 * (2 * i + a) + h // 2 + 1)
                    Sh = S_gla[:, d, h, :]
                    ins = dve.scalar_tensor_tensor(Sh, Sh, small[:, 208 + 8 * d + 2 * h + half:209 + 8 * d + 2 * h + half],
                                                   banks(2 + h // 2)[:, GV * (h % 2):GV * (h % 2 + 1)], ALU.mult, ALU.add)
                    if h % 2 == 1:
                        ins.then_inc(gs_new, 1)

            dve.wait_ge(g_zero, 2)
            dve.wait_ge(xw_done, 4 * TT)
            dve.wait_ge(u_mm, 4 * TT)
            dve.wait_ge(proj_act, emptied(JOBS_QK - 1)[1])
            def norm_tile(n):
                t = FIN[n]
                dve.wait_ge(nb2_in, 16)
                dve.wait_ge(g_rstd, n + 1)
                for h in range(GH):
                    oh = og[:, t, GV * h:GV * (h + 1)]
                    ins = dve.scalar_tensor_tensor(oh, oh, small[:, 116 + GH * t + h:117 + GH * t + h], norm_bc[:, GV * h:GV * (h + 1)],
                                                   ALU.mult, ALU.mult)
                ins.then_inc(gn_done, 1)

            log_gates(0)
            decays(0)
            log_gates(1)
            dec_queries(0)
            mod_block(4, *late_mods[0], 0)
            decays(1)
            mask_att(0)
            seen = set()
            for i in range(2 * TT):
                t = ORDER[i % 2][i // 2]
                if i + 2 < 2 * TT:
                    log_gates(i + 2)
                if i + 1 < 2 * TT:
                    dec_queries(i + 1)
                states(i, 0)
                if i + 2 < 2 * TT:
                    decays(i + 2)
                if i + 1 < len(late_mods):
                    mod_block(5 + i, *late_mods[i + 1], 0)
                if i + 1 < 2 * TT:
                    mask_att(i + 1)
                dve.wait_ge(inter_mm, 2 * i + 2)
                if t in seen:
                    dve.wait_ge(o_added, i)
                    dve.tensor_tensor(og[:, t, :], og[:, t, :], banks(4, 2), ALU.add).then_inc(o_added, 1)
                else:
                    dve.tensor_copy(og[:, t, :], banks(4, 2)).then_inc(o_added, 1)
                seen.add(t)
                states(i, 1)
                if i + 1 == len(late_mods):
                    scale_gain(1, 4 + len(late_mods))
                for n in norm_at.get(i, []):
                    norm_tile(n)
                if i in (9, 10):
                    part_lo(dve, eo_ch[i - 9])
            for n in range(sum(len(v) for v in norm_at.values()), TT):
                norm_tile(n)
            for n, t in enumerate(FIN):
                dve.wait_ge(ys_hi_done, n + 1)
                dve.tensor_tensor(ys_lo[:, t, :, :], yT_ssd[:, t, :, :], ys_hi[:, t, :, :].bitcast(f32), ALU.subtract).then_inc(ys_lo_done, 1)
                dve.wait_ge(gT_hi_done, n + 1)
                dve.tensor_tensor(yg_lo[:, t, :, :].rearrange("p k c -> p (k c)"), banks(2 + 2 * (n % 2), 2),
                                  yg_hi[:, t, :, :].rearrange("p k c -> p (k c)").bitcast(f32), ALU.subtract).then_inc(gT_done, 1)
            part_lo(dve, eo_ch[2])
            dve.wait_ge(gr_done, 2)
            for n in range(4):
                dve.wait_ge(eo_mm, n + 1)
                for t in range(TT):
                    e = etmp[t % 2]
                    do(dve.tensor_tensor(e, eo_out(n, t), gate_e[:, 1 if t < CT else 0, HB * n:HB * (n + 1)], ALU.mult))
                    if n == 0:
                        dve.wait_ge(x1_in[t], 16)
                    xp = x1[:, t, HB * n:HB * (n + 1)]
                    dve.tensor_tensor(xp, xp, e, ALU.add).then_inc(eo_done, 1)
                if n < 3:
                    part_lo(dve, eo_ch[2 * n + 3])
                if n < 2:
                    part_lo(dve, eo_ch[2 * n + 4])
            dve.wait_ge(eo_done, 4 * TT)
            normalise(1)
            dve.wait_ge(tab_in, 64)
            dve.wait_ge(gain_in, 32)
            for a in range(4):
                qk = a % 2
                g3 = spread(qk_gain[:, qk, :], 1, LT)
                sc = -float(AD) ** -0.5 if qk == 0 else 1.0
                dve.scalar_tensor_tensor(tables[:, a, :, :], tables[:, a, :, :], sc, g3, ALU.mult, ALU.mult).then_inc(gain_done, 1)
            dve.tensor_scalar(sink, sink, -1.0, None, ALU.mult).then_inc(sink_done, 1)
            dve.wait_ge(gain_done, 4)
            r = 0
            for j in range(JOBS_E, len(jobs)):
                kind, n, t = jobs[j]
                if kind == "va":
                    dve.wait_ge(proj_mm, j + 1)
                    dve.tensor_copy(va[:, t, :], banks(j % 2)).then_inc(proj_dve, 1)
                elif kind in ("k", "q"):
                    t0, A, B, R = rp[r % 2]
                    dve.wait_ge(rk_rstd, r + 1)
                    if r > CT + 1:
                        dve.wait_ge(rk_b, r - 1 - CT)
                    ss = small[:, 140 + 4 * (r % 2):144 + 4 * (r % 2)]
                    ins = dve.tensor_tensor(heads4(t0), heads4(banks(j % 2)), spread(ss, 2, AD), ALU.mult)
                    ins.then_inc(rk_t0, 1)
                    dve.wait_ge(rk_t0, r + 1)
                    if kind == "k" and t < CT:
                        dve.tensor_tensor(heads4(R), heads4(t0), spread(qk_gain[:, 1, :], 1, 4), ALU.mult).then_inc(rk_r, 1)
                    else:
                        if r > CT + 1:
                            dve.wait_ge(rk_r, r - 1)
                        dve.tensor_tensor(heads4(A), heads4(t0), spread(tables[:, 0 if kind == "q" else 1, t - CT, :], 1, 4),
                                          ALU.mult).then_inc(rk_a, 1)
                    r += 1
            dve.wait_ge(mask_in, 16)
            dve.wait_ge(sink_done, 1)
            NA = LT * AH

            def row_min(a):
                t, h = a // AH, a % AH
                nk = CTX + P * (3 if 0 < t < LT - 1 else 2)
                m = amask[:, 0:nk] if t == 0 else amask[:, CTX + 2 * P:CTX + 2 * P + nk]
                dve.wait_ge(s_mm, a + 1)
                if a >= 2:
                    dve.wait_ge(p_tr, a - 1)
                dve.tensor_tensor_reduce(out=prob[a % 2][:, 0:nk], in0=banks(2 + 2 * (a % 2), 2)[:, 0:nk], in1=m, scale=1.0,
                                         scalar=sink[:, h:h + 1], op0=ALU.add, op1=ALU.min,
                                         accum_out=small[:, 160 + h:161 + h]).then_inc(mx_done, 1)

            for a in range(NA + 2):
                if a < NA:
                    if a % GRP == 0 and a >= AH:
                        dve.wait_ge(ek_done, (a - AH) // GRP + 1)
                    row_min(a)
                if 1 <= a <= NA:
                    v = a - 1
                    t = v // AH
                    if 0 < t < LT - 1:
                        dve.wait_ge(p_tr, v + 1)
                        if v >= 2:
                            dve.wait_ge(pv_mm, v - 1)
                        dve.tensor_copy(probT[v % 2][:, 4, :], banks(7)[:, 0:P]).then_inc(pt_d, 1)
                    if v % GRP == GRP - 1:
                        G = v // GRP
                        g4 = G % AKV
                        dk = small[:, 192 + 4 * g4:196 + 4 * g4]
                        dve.wait_ge(mx_done, v + 1)
                        dve.tensor_tensor(dk, small[:, 160 + 4 * g4:164 + 4 * g4], sink[:, 4 * g4:4 * g4 + 4], ALU.subtract).then_inc(dk_done, 1)
                if a >= 2 and (a - 2) % GRP == GRP - 1:
                    v = a - 2
                    G = v // GRP
                    g4 = G % AKV
                    dk = small[:, 192 + 4 * g4:196 + 4 * g4]
                    dve.wait_ge(ek_done, G + 1)
                    do(dve.tensor_tensor(dk, dk, small[:, 176 + 4 * g4:180 + 4 * g4], ALU.add))
                    do(dve.reciprocal(dk, dk))
                    dve.wait_ge(pv_mm, v + 1)
                    if G >= 2:
                        dve.wait_ge(ot_tr, G - 1)
                    dve.tensor_tensor(heads4(ogate[G % 2]), heads4(banks(0)), spread(dk, 2, AD), ALU.mult).then_inc(on_done, 1)
            dve.wait_ge(gr_done, 3)
            for n in range(2):
                for t in range(LT):
                    q = n * LT + t
                    dve.wait_ge(oo_mm, q + 1)
                    f = ftmp[q % 2]
                    do(dve.tensor_tensor(f, banks(q), gate_o[:, NB * n:NB * (n + 1)], ALU.mult))
                    xp = x1[:, CT + t, NB * n:NB * (n + 1)]
                    dve.tensor_tensor(xp, xp, f, ALU.add).then_inc(fin_done, 1)

        @block.tensor
        def _(pe):
            mm = pe.matmul

            def arrived(n):
                pe.wait_ge(ring_full[slot_of[n]], 16 * arrivals[n])
                return ring[:, slot_of[n], :, :]

            def ready(n):
                pe.wait_ge(w_lo, sum(split[:n]) + 1)
                return ring_r[:, slot_of[n] + 2, :, :], ring_r[:, slot_of[n], :, :]

            pe.wait_ge(cst_in, 16)
            pe.wait_ge(vec_in, 16 * 9)
            pe.transpose(banks(3)[:, 0:P], vrow1, ident)
            pe.transpose(banks(3)[:, P:P + 32], vrow2, ident[0:32, 0:32]).then_inc(vec_T, 1)

            def modulation(l, b, bank):
                w = [arrived(n) for n in mod_ch[l][b]]
                for k in range(KT):
                    ins = mm(banks(bank)[0:2, :], silu_c[:, k:16:8], w[k // KH][:, k % KH, :], start=(k == 0), stop=(k == KT - 1))
                ins.then_inc(mod_mm[l], 1)

            def modulation_T(n, bank):
                pe.wait_ge(mod_row, n + 1)
                for m in range(4):
                    ins = pe.transpose(banks(bank)[:, 2 * m:2 * m + 2], mrow[0:2, P * m:P * (m + 1)], ident[0:2, 0:2])
                ins.then_inc(mod_tr, 1)

            def transpose_h(l):
                src = (xs, xn1)[l]
                pe.wait_ge(xn_done[l], TT)
                for q in range(2 * KT):
                    kt, s = q % KT, q // KT
                    t0, n = (CT, LT) if s == 0 else (0, CT)
                    if q >= 2:
                        pe.wait_ge(ht_done[l], q - 1)
                    for t in range(n):
                        ins = pe.transpose(banks(4 + q % 2)[:, P * t:P * (t + 1)], src[:, t0 + t, P * kt:P * (kt + 1)], ident)
                    ins.then_inc(ht_tr[l], 1)

            pe.wait_ge(silu_done, 1)
            for b in range(5):
                if b >= 2:
                    pe.wait_ge(mod_row, b - 1)
                if b < 4:
                    modulation(0, b, b % 2)
                if b >= 1:
                    if b >= 2:
                        pe.wait_ge(mod_add, b - 1)
                    modulation_T(b - 1, 2)
            transpose_h(0)
            pe.wait_ge(ht_done[0], 2 * KT)
            pe.wait_ge(wsm_in, 32)

            def free_bank(j):
                if j >= 2:
                    d, n = emptied(j - 2)
                    pe.wait_ge(proj_dve if d else proj_act, n)

            def token_job(j, l, ch):
                t = jobs[j][2]
                w = [arrived(n) for n in ch]
                for k in range(KT):
                    ins = mm(banks(j % 2), hT[l][:, t, k, :], w[k // KH][:, k % KH, :], start=(k == 0), stop=(k == KT - 1))
                ins.then_inc(proj_mm, 1)

            def token_parts(j, n):
                t = jobs[j][2]
                hi, lo = ready(n)
                for k in range(KT):
                    for q, (a, w) in enumerate(((h_hi, hi), (h_hi, lo), (h_lo, hi))):
                        ins = mm(banks(j % 2)[:, 0:HB], a[:, t, k, :], w[:, k, :], start=(k == 0 and q == 0), stop=(k == KT - 1 and q == 2))
                ins.then_inc(proj_mm, 1)

            def feature_parts(j, n, m, part):
                hi, lo = ready(n)
                t0, nt = (0, CT) if part == 0 else (CT, LT)
                pe.wait_ge(h_lo_done, t0 + nt)
                for k in range(KT):
                    for q, (w, a) in enumerate(((hi, h_hi), (lo, h_hi), (hi, h_lo))):
                        ins = mm(banks(j % 2)[:, 0:nt * P], w[:, k, P * m:P * (m + 1)], a[:, t0:t0 + nt, k, :],
                                 start=(k == 0 and q == 0), stop=(k == KT - 1 and q == 2))
                ins.then_inc(proj_mm, 1)

            def feature_job(j, ch, m, part):
                w = [arrived(n) for n in ch]
                t0, n = (0, CT) if part == 0 else (CT, LT)
                for k in range(KT):
                    ins = mm(banks(j % 2)[:, 0:n * P], w[k // KH][:, k % KH, P * m:P * (m + 1)], hT[0][:, t0:t0 + n, k, :],
                             start=(k == 0), stop=(k == KT - 1))
                ins.then_inc(proj_mm, 1)

            j = 0
            for t in range(TT):
                free_bank(j)
                for k in range(KT):
                    ins = mm(banks(j % 2)[:, 0:64], hT[0][:, t, k, :], w_small[:, k, :], start=(k == 0), stop=(k == KT - 1))
                ins.then_inc(proj_mm, 1)
                j += 1
            while j < JOBS_SSD:
                kind, n, t = jobs[j]
                free_bank(j)
                if kind == "xbc":
                    feature_job(j, xbc_ch[n // 4], n % 4, t)
                else:
                    token_job(j, 0, z_ch[n])
                j += 1
                if j == TT + 2:
                    pe.wait_ge(proj_dve, TT)
                    for t in range(TT):
                        b, o0 = (6, P * t) if t < 4 else (7, P * (t - 4))
                        ins = pe.transpose(banks(b)[0:32, o0:o0 + P], lr_tok[:, t, :], ident)
                    ins.then_inc(lr_tr, 1)
            pe.wait_ge(xbc_done, XB)
            for t in range(TT):
                b = 2 + 3 * (t % 2)
                if t == 0:
                    pe.wait_ge(lr_done, 1)
                if t >= 2:
                    pe.wait_ge(xs_done, t - 1)
                    pe.wait_ge(b_done, t - 1)
                for cc in range(8):
                    pe.transpose(banks(b, 2)[:, P * cc:P * (cc + 1)], xT[:, cc, P * t:P * (t + 1)], ident)
                for cc in range(2):
                    ins = pe.transpose(banks(b + 2)[:, P * cc:P * (cc + 1)], bcT[:, cc, P * t:P * (t + 1)], ident)
                ins.then_inc(xs_tr, 1)

            def ssd_ahead(u):
                s, g = u // 2, u % 2
                d, t = s % 2, ORDER[s % 2][s // 2]
                if g == 0:
                    if s >= 1:
                        pe.wait_ge(cbm_done, s)
                    r = dta[:, t, SH * d:SH * (d + 1)]
                    for q, lhsT in enumerate((incl[d], strict[d], ones)):
                        mm(banks(7)[:, 48 * d + 16 * q:48 * d + 16 * q + 16], lhsT, r, start=True, stop=True)
                    for q in range(SG):
                        ins = mm(banks(7)[:, 128 + 128 * q:256 + 128 * q], bcT[:, q, P * t:P * (t + 1)], bcT[:, 2 + q, P * t:P * (t + 1)],
                                 start=True, stop=True)
                    ins.then_inc(cb_mm, 1)
                pe.wait_ge(rd_done, u + 1)
                if u >= 1:
                    pe.wait_ge(dec_done, u)
                for q in range(2):
                    ins = mm(banks(2 + q), strict[d], RD[u % 2][:, 4 * q:4 * q + 4, :], start=True, stop=True)
                ins.then_inc(d_mm, 1)

            pe.wait_ge(dta_done, 1)
            pe.wait_ge(xs_done, TT)
            pe.wait_ge(b_done, TT)
            pe.wait_ge(S_zero, 1)
            ssd_ahead(0)
            for u in range(4 * TT):
                s, g = u // 2, u % 2
                d, t = s % 2, ORDER[s % 2][s // 2]
                if u + 1 < 4 * TT:
                    ssd_ahead(u + 1)
                if u >= 4:
                    pe.wait_ge(s_new, u - 3)
                if u >= 1:
                    pe.wait_ge(tmp_done, u)
                mm(banks(5), bcT[:, 2 + g, P * t:P * (t + 1)], S_ssd[:, d, GW * g:GW * (g + 1)], start=True, stop=True).then_inc(yo_mm, 1)
                pe.wait_ge(xw_done, u + 1)
                if u >= 1:
                    pe.wait_ge(s_new, u)
                mm(banks(6), b_tok[:, t, P * g:P * (g + 1)], xw[u % 2], start=True, stop=True).then_inc(u_mm, 1)
                pe.wait_ge(a_done, u + 1)
                for h in range(8):
                    ins = mm(banks(4)[:, SD * h:SD * (h + 1)], Edec[u % 2][:, h, :], xdt[u % 2][:, SD * h:SD * (h + 1)], start=True, stop=True)
                ins.then_inc(yd_mm, 1)

            while j < JOBS_E:
                kind, n, t = jobs[j]
                if j == JOBS_QK:
                    for tt in range(TT):
                        pe.wait_ge(yn_done, tt + 1)
                        if tt >= 2:
                            pe.wait_ge(yT_done, tt - 1)
                        else:
                            pe.wait_ge(tmp_done, 4 * TT)
                        for k in range(KT):
                            ins = pe.transpose(banks(2 + 2 * (tt % 2), 2)[:, P * k:P * (k + 1)], y[:, tt, P * k:P * (k + 1)], ident)
                        ins.then_inc(yT_tr, 1)
                free_bank(j)
                if kind == "qk":
                    feature_parts(j, qk_ch[n // 2], n % 2, t)
                else:
                    token_parts(j, (v_ch if kind == "v" else g_ch)[n])
                j += 1
            pe.wait_ge(yT_done, TT)
            pe.wait_ge(proj_act, emptied(JOBS_E - 1)[1])
            pe.wait_ge(proj_dve, emptied(JOBS_V - 1)[1])

            def gla_logits(i):
                d, t = i % 2, ORDER[i % 2][i // 2]
                if i >= 1:
                    pe.wait_ge(lg_x, i)
                for h in range(GH):
                    ins = mm(banks(1)[:, P * h:P * (h + 1)], gate_w[:, d, GK * h:GK * (h + 1)], lrT[:, P * t:P * (t + 1)], start=True, stop=True)
                ins.then_inc(lg_mm, 1)

            def gla_scores(i):
                d = i % 2
                pe.wait_ge(ki_done, i + 1)
                pe.wait_ge(qd_done, i + 1)
                if i >= 1:
                    pe.wait_ge(am_done, i)
                for h in range(GH):
                    ins = mm(banks(6)[:, P * h:P * (h + 1)], heads4(kk)[:, h, :], qdec[d][:, h, :], start=True, stop=True)
                ins.then_inc(at_mm, 1)

            def gla_keys(i):
                pe.wait_ge(ku_done, i + 1)
                if i >= 1:
                    pe.wait_ge(kut_done, i)
                for h in range(GH):
                    ins = pe.transpose(banks(7)[:, P * h:P * (h + 1)], heads4(ku)[:, h, :], ident)
                ins.then_inc(ku_tr, 1)

            o3 = banks(4, 2).rearrange("p (h e) -> p h e", h=GH)

            def gla_within(i):
                d, t = i % 2, ORDER[i % 2][i // 2]
                if i >= 1:
                    pe.wait_ge(o_added, i)
                pe.wait_ge(am_done, i + 1)
                for h in range(GH):
                    mm(o3[:, h, :], attm[d][:, h, :], vv[:, t, GV * h:GV * (h + 1)], start=(h % 2 == 0), stop=True, skip_group_check=True)

            def gla_chunk(i, a):
                d, t = i % 2, ORDER[i % 2][i // 2]
                half = a if d == 0 else 1 - a
                r0 = HALF * half
                if a == 1:
                    pe.wait_ge(gs_new, 2 * (2 * i + 1))
                elif i >= 2:
                    pe.wait_ge(gs_new, 4 * (i - 1))
                for h in range(GH):
                    ins = mm(o3[r0:r0 + HALF, h, :], qdec[d][:, h, r0:r0 + HALF], S_gla[:, d, h, :], start=False, stop=True,
                             skip_group_check=True)
                ins.then_inc(inter_mm, 1)
                pe.wait_ge(kut_done, i + 1)
                for h in range(GH):
                    hf = 2 * i + a
                    if h % 2 == 0 and 2 * hf - 1 + h // 2 > 0:
                        pe.wait_ge(gs_new, 2 * hf - 1 + h // 2)
                    ins = mm(banks(2 + h // 2)[:, GV * (h % 2):GV * (h % 2 + 1)], kutok[d][r0:r0 + HALF, h, :],
                             vv[r0:r0 + HALF, t, GV * h:GV * (h + 1)], start=True, stop=True)
                    if h % 2 == 1:
                        ins.then_inc(gu_mm, 1)

            pe.wait_ge(gw_in, 32)
            pe.wait_ge(g_zero, 2)
            gla_logits(0)
            modulation(*late_mods[0], 0)
            gla_logits(1)
            modulation_T(4, 0)
            pe.wait_ge(mod_add, 5)
            modulation(*late_mods[1], 0)
            gla_logits(2)
            gla_scores(0)
            gla_keys(0)
            for i in range(2 * TT):
                gla_within(i)
                gla_chunk(i, 0)
                if i + 1 < len(late_mods):
                    modulation_T(5 + i, 0)
                if i + 1 < 2 * TT:
                    gla_scores(i + 1)
                    gla_keys(i + 1)
                gla_chunk(i, 1)
                if i + 3 < 2 * TT:
                    gla_logits(i + 3)
                if i + 2 < len(late_mods):
                    pe.wait_ge(mod_add, 6 + i)
                    modulation(*late_mods[i + 2], 0)
            for n, t in enumerate(FIN):
                pe.wait_ge(gg_done, n + 1)
                if n >= 2:
                    pe.wait_ge(gT_done, n - 1)
                else:
                    pe.wait_ge(o_added, 2 * TT)
                    pe.wait_ge(gs_new, 8 * TT)
                for k in range(KT):
                    ins = pe.transpose(banks(2 + 2 * (n % 2), 2)[:, P * k:P * (k + 1)], og[:, t, P * k:P * (k + 1)], ident)
                ins.then_inc(gT_tr, 1)
            for q in range(3):
                l, s = (0, q) if q < 2 else (1, 0)
                if q < 2:
                    pe.wait_ge(gT_done, TT - 1 + q)
                else:
                    pe.wait_ge(gr_done, 1)
                for k in range(KT):
                    ins = mm(banks(2 + 2 * (q % 2), 2)[:, P * k:P * (k + 1)], spread(mod[l][:, 16 + k, s], 1, P), ident, start=True, stop=True)
                ins.then_inc(gr_mm, 1)
            pe.wait_ge(gr_done, 3)
            pe.wait_ge(ys_lo_done, TT)
            pe.wait_ge(gT_done, TT)
            for n in range(4):
                if n >= 2:
                    pe.wait_ge(eo_done, TT * (n - 1))
                for half, (a_hi, a_lo) in enumerate(((ys_hi, ys_lo), (yg_hi, yg_lo))):
                    hi, lo = ready(eo_ch[2 * n + half])
                    for t in range(TT):
                        for k in range(KT):
                            for q, (a, w) in enumerate(((a_hi, hi), (a_hi, lo), (a_lo, hi))):
                                ins = mm(eo_out(n, t), a[:, t, k, :], w[:, k, :], start=(half + k + q == 0 and t % 2 == 0),
                                         stop=(half == 1 and k == KT - 1 and q == 2), skip_group_check=True)
                    ins.then_inc((eo_w, eo_mm)[half], 1)
            transpose_h(1)
            pe.wait_ge(ht_done[1], 2 * KT)

            def rope_transpose(r):
                pe.wait_ge(rk_r, r + 1)
                if r >= 2:
                    pe.wait_ge(rk_done, r - 1)
                R = rp[r % 2][3]
                for h in range(4):
                    ins = pe.transpose(banks(2 + r % 2)[:, P * h:P * (h + 1)], heads4(R)[:, h, :], ident)
                ins.then_inc(rk_tr, 1)

            first = JOBS_E
            for j in range(JOBS_E, len(jobs)):
                kind, n, t = jobs[j]
                if j - 2 >= first:
                    if jobs[j - 2][0] in ("k", "q"):
                        r = ropes.index(j - 2)
                        pe.wait_ge(rk_t0, r + 1)
                    else:
                        d, m = emptied(j - 2)
                        pe.wait_ge(proj_dve if d else proj_act, m)
                token_job(j, 1, oin_ch[n])
                if j - 2 in ropes:
                    rope_transpose(ropes.index(j - 2))
            pe.wait_ge(rk_done, len(ropes))

            NA = LT * AH

            def scores(a):
                t, h = a // AH, a % AH
                kv = h // GRP
                lo, hi = max(t - 1, 0), min(t + 1, LT - 1)
                k0 = CTX + P * lo
                if a >= 2:
                    pe.wait_ge(mx_done, a - 1)
                b = banks(2 + 2 * (a % 2), 2)
                lhsT = qT[:, t, h, :]
                mm(b[:, 0:CTX], lhsT, kT[:, kv, 0:CTX], start=True, stop=True)
                ins = mm(b[:, CTX:CTX + 2 * P], lhsT, kT[:, kv, k0:k0 + 2 * P], start=True, stop=True)
                if hi - lo == 2:
                    ins = mm(b[:, CTX + 2 * P:CTX + 3 * P], lhsT, kT[:, kv, k0 + 2 * P:k0 + 3 * P], start=True, stop=True)
                ins.then_inc(s_mm, 1)

            def out_transpose(G):
                pe.wait_ge(og_done, G + 1)
                if G >= 1:
                    pe.wait_ge(ot_done, G)
                for h in range(GRP):
                    ins = pe.transpose(banks(1)[:, P * h:P * (h + 1)], heads4(ogate[G % 2])[:, h, :], ident)
                ins.then_inc(ot_tr, 1)

            scores(0)
            for a in range(NA + 1):
                if a + 1 < NA:
                    scores(a + 1)
                if a >= 1:
                    v = a - 1
                    t, h = v // AH, v % AH
                    kv = h // GRP
                    lo, hi = max(t - 1, 0), min(t + 1, LT - 1)
                    tiles = list(range(CT)) + [CT + b for b in range(lo, hi + 1)]
                    pe.wait_ge(pt_a, v + 1)
                    if len(tiles) == 5:
                        pe.wait_ge(pt_d, v + 1 - AH)
                    if v % GRP == 0 and v >= GRP:
                        pe.wait_ge(on_done, v // GRP)
                    for b, kt in enumerate(tiles):
                        ins = mm(banks(0)[:, AD * (v % GRP):AD * (v % GRP + 1)], probT[v % 2][:, b, :], va[:, kt, AD * kv:AD * (kv + 1)],
                                 start=(b == 0), stop=(b == len(tiles) - 1))
                    ins.then_inc(pv_mm, 1)
                if a < NA:
                    t = a // AH
                    nb = 5 if 0 < t < LT - 1 else 4
                    pe.wait_ge(p_done, a + 1)
                    for b in range(nb):
                        ins = pe.transpose(banks(6, 2)[:, P * b:P * (b + 1)], prob[a % 2][:, P * b:P * (b + 1)], ident)
                    ins.then_inc(p_tr, 1)
                if a >= 1 and (a - 1) % GRP == 1 and a - 1 >= GRP:
                    out_transpose((a - 1) // GRP - 1)
            out_transpose(LT * AKV - 1)
            pe.wait_ge(ot_done, LT * AKV)
            for n in range(2):
                for q, ch in enumerate(oo_ch[n]):
                    w = arrived(ch)
                    for t in range(LT):
                        for k in range(KH):
                            ins = mm(banks(n * LT + t), qT[:, t, KH * q + k, :], w[:, k, :], start=(q == 0 and k == 0), stop=(q == 3 and k == KH - 1))
                        if q == 3:
                            ins.then_inc(oo_mm, 1)
                    if q < 3:
                        ins.then_inc(oo_w, 1)


def constants():
    import numpy as np
    k = np.arange(P)
    a, b = k[:, None], k[None, :]
    same = a // HALF == b // HALF
    tiles = [a == b, a <= b, a > b, a >= b, a < b, np.ones((P, P)), same & (a <= b), same & (a >= b)]
    keep = np.ones((P, NB))
    keep[:, ::HALF] = 0
    consts = np.concatenate([np.asarray(m, np.float32) for m in tiles] + [keep.astype(np.float32)], axis=1)
    zero = np.zeros((P, P), np.float32)
    before = np.where(b >= a, 0, -NEG).astype(np.float32)
    after = np.where(b <= a, 0, -NEG).astype(np.float32)
    masks = np.concatenate([zero, zero, zero, after, zero, zero, before, zero, after], axis=1)
    grid, freqs, base = 64, AD // 4, 10000.0
    rows = LAT // grid
    row = np.repeat(np.arange(rows, dtype=np.float32), grid)
    col = np.tile(np.arange(grid, dtype=np.float32), rows)
    inv = (np.float32(1.0) / (np.float32(base) ** (np.arange(freqs, dtype=np.float32) / np.float32(freqs)))).astype(np.float32)
    ang = np.stack([row[:, None] * inv, col[:, None] * inv], axis=1).astype(np.float32)
    cos, sin = np.cos(ang), np.sin(ang)
    cc = np.stack([cos, cos], axis=2).reshape(LAT, AD)
    ss = np.stack([sin, -sin], axis=2).reshape(LAT, AD)
    return consts, masks, np.stack([cc, ss]).astype(np.float32)


_INS = ['x', 'c', 'ctx', 'c_ctx', 'e_norm', 'e_mod_w', 'e_mod_b', 'e_w_in', 'e_conv_w', 'e_conv_b', 'e_dt_bias', 'e_a_log',
        'e_d_skip', 'e_ssd_norm', 'e_gla_gate_w', 'e_gla_gate_b', 'e_gla_norm', 'e_w_out', 'o_norm', 'o_mod_w', 'o_mod_b',
        'o_w_in', 'o_q_norm', 'o_k_norm', 'o_sink', 'o_w_out']


def kernel(**inputs):
    import numpy as np
    import concourse.bacc as bacc
    from concourse.bass_utils import run_bass_kernel_spmd

    nc = bacc.Bacc("TRN2", target_bir_lowering=False, num_devices=1)
    arrays, args = {}, []
    extra = dict(zip(("consts", "masks", "rope"), constants()))
    for name in _INS + list(extra):
        a = np.ascontiguousarray(extra[name] if name in extra else inputs[name])
        arrays[f"in_{name}"] = a
        args.append(nc.dram_tensor(f"in_{name}", a.shape, mybir.dt.from_np(a.dtype), kind="ExternalInput").ap())
    args.append(nc.dram_tensor("out_x", (1, LAT, DM), mybir.dt.float32, kind="ExternalOutput").ap())
    even_odd_layers(nc, *args)
    r = run_bass_kernel_spmd(nc, [arrays], core_ids=[0])
    return r.results[0]["out_x"]
```

```python
import concourse.bass as bass
from concourse import mybir
from contextlib import ExitStack

P = 128
DM = 1024
KT = DM // P
CTX, LAT = 256, 512
TOK = CTX + LAT
TT, CT = TOK // P, CTX // P
LT = TT - CT
SH, SD, SG, SN = 16, 64, 2, 128
SW = SH * SD
GW = SW // SG
CONV_K = 5
XB = (SW + 2 * SG * SN) // P
GH, GK, GV, RANK = 4, 128, 256, 16
HALF = 64
AH, AKV, AD = 16, 4, 128
GRP = AH // AKV
NB = 512
KH = 4
HB = 256
SLOTS = 4
EPS = 1e-6
NEG = -1e30
E_Z = 0
E_XBC = E_Z + SW
E_DT = E_XBC + XB * P
E_Q = E_DT + 2 * SH
E_K = E_Q + GH * GK
E_V = E_K + GH * GK
E_G = E_V + GH * GV
E_LR = E_G + GH * GV
KVW = AKV * AD
ORDER = [list(range(TT)), list(range(CT))[::-1] + list(range(CT, TT))[::-1]]

C_ID, C_LE, C_GT, C_GE, C_LT, C_ONE, C_SCAN = [i * P for i in range(7)]
C_COLS = C_SCAN + NB
M_COLS = (CTX + 2 * P) + (CTX + 3 * P)


def even_odd_layers(nc, x, c, ctx_in, c_ctx, e_norm, e_mod_w, e_mod_b, e_w_in, e_conv_w, e_conv_b, e_dt_bias,
                    e_a_log, e_d_skip, e_ssd_norm, e_gla_gate_w, e_gla_gate_b, e_gla_norm, e_w_out, o_norm,
                    o_mod_w, o_mod_b, o_w_in, o_q_norm, o_k_norm, o_sink, o_w_out, consts, masks, rope, out):
    f32, i32 = mybir.dt.float32, mybir.dt.int32
    ALU, ACT, AX = mybir.AluOpType, mybir.ActivationFunctionType, mybir.AxisListType
    es = ExitStack()

    def sb(name, shape):
        return es.enter_context(nc.sbuf_tensor(name, shape, f32))

    def sem(name):
        return es.enter_context(nc.semaphore(name))

    def spread(ap, axis, n):
        a = ap.unsqueeze(axis)
        shape = list(a.shape)
        shape[axis] = n
        return a.broadcast_to(shape)

    with es:
        SLAB = TT * DM
        f32r = mybir.dt.float32r
        base = (nc.sbuf_base + 31) // 32 * 32
        arena = sb("arena", [P, 6 * SLAB])
        ring = sb("ring", [P, SLOTS, KH, NB])
        slab_r = [nc.alloc_sbuf_tensor_at(f"slab_parts{i}", [P, SLAB], f32r, offset=base + 4 * SLAB * i) for i in range(6)]
        ring_r = nc.alloc_sbuf_tensor_at("ring_parts", [P, SLOTS, KT, HB], f32r, offset=base + 4 * 6 * SLAB)
        cst = sb("cst", [P, C_COLS])
        ident = cst[:, C_ID:C_ID + P]
        incl = [cst[:, C_LE:C_LE + P], cst[:, C_GE:C_GE + P]]
        strict = [cst[:, C_GT:C_GT + P], cst[:, C_LT:C_LT + P]]
        ones = cst[:, C_ONE:C_ONE + P]
        scan_keep = cst[:, C_SCAN:C_SCAN + NB]
        vecs = sb("vecs", [P, 160])
        V_C, V_N, V_MB, V_CW, V_CB, V_GB, V_ON, V_OMB = 0, 16, 24, 48, 108, 120, 128, 136
        silu_c = sb("silu_c", [P, 16])
        mod = [sb("mod_e", [P, 24, 2]), sb("mod_o", [P, 24, 2])]
        small = sb("small", [P, 224])
        bc_small = sb("bc_small", [P, 96])
        dt_bias, a_log = bc_small[:, 0:32], bc_small[:, 32:64]
        d_skip, sink = bc_small[:, 64:80], bc_small[:, 80:96]
        dtv = sb("dtv", [P, TT, 32])
        dta = sb("dta", [P, TT, 32])
        gate_o = sb("gate_o", [P, DM])
        tail = sb("tail", [P, 3328])
        spare = sb("spare", [P, 1024])

        def slab(i, n=TT, w=DM):
            return arena[:, i * SLAB:i * SLAB + n * w].rearrange("p (n w) -> p n w", n=n)

        def parts(i):
            return slab_r[i][:, :].rearrange("p (t k c) -> p t k c", t=TT, k=KT)

        h_hi, h_lo = parts(1), parts(0)
        ys_hi, ys_lo = parts(2), parts(3)
        yg_hi, yg_lo = parts(5), parts(1)
        hT = [arena[:, s * SLAB:(s + 1) * SLAB].rearrange("p (t k c) -> p t k c", t=TT, k=KT) for s in (0, 2)]
        zt = [spare[:, 512 * i:512 * i + HB] for i in (0, 1)]
        xT = arena[:, 2 * SLAB:2 * SLAB + 8 * TOK].rearrange("p (c t) -> p c t", c=8)
        y = slab(2)
        xs = slab(3)
        yT_ssd = arena[:, 3 * SLAB:4 * SLAB].rearrange("p (t k c) -> p t k c", t=TT, k=KT)
        bcT = arena[:, 4 * SLAB:4 * SLAB + 4 * TOK].rearrange("p (c t) -> p c t", c=4)
        b_tok = arena[:, 4 * SLAB + 3072:4 * SLAB + 4608].rearrange("p (t n) -> p t n", t=TT)
        s4 = 4 * SLAB + 4608
        xdt = [arena[:, s4:s4 + 512], spare[:, 0:512]]
        xw = [arena[:, s4 + 512:s4 + 1024], spare[:, 512:1024]]
        ytmp = arena[:, s4 + 1024:s4 + 1536]
        s5 = 5 * SLAB
        ex_all = gate_o[:, 0:6 * TT * SH].rearrange("p (d q t h) -> p d q t h", d=2, q=3, t=TT)
        S_ssd = arena[:, s5:s5 + 2048].rearrange("p (d n) -> p d n", d=2)
        Edec = [arena[:, s5 + 2048 + 1024 * i:s5 + 3072 + 1024 * i].rearrange("p (h i) -> p h i", h=8) for i in (0, 1)]
        RD = [arena[:, s5 + 4096 + 1024 * i:s5 + 5120 + 1024 * i].rearrange("p (h i) -> p h i", h=8) for i in (0, 1)]
        RAW = TOK + 6
        raw = [arena[:, s5 + 2048 + RAW * i:s5 + 2048 + RAW * (i + 1)] for i in (0, 1)]
        cacc = [arena[:, s5 + 3600 + 772 * i:s5 + 3600 + 772 * i + TOK + 2] for i in (0, 1)]
        vrow1 = arena[:, s5:s5 + P]
        vrow2 = arena[0:32, s5 + P:s5 + 2 * P]
        junk = arena[:, 4 * SLAB:4 * SLAB + DM]
        w_small = tail[:, 0:512].rearrange("p (k n) -> p k n", k=KT)
        norm_bc = tail[:, 768:1792]
        lr_tok = tail[:, 512:704].rearrange("p (t n) -> p t n", t=TT)
        gate_w = tail[0:32, 1792:2816].rearrange("p (d n) -> p d n", d=2)
        cbm = tail[:, 2816:3328].rearrange("p (d g n) -> p d g n", d=2, g=2)
        lrT = tail[0:32, 0:TOK]
        vv = slab(5)
        s1 = SLAB
        gs = slab(2)
        qT_g = arena[:, 4 * SLAB:4 * SLAB + 4 * TOK].rearrange("p (c t) -> p c t", c=4)
        kT_g = arena[:, 4 * SLAB + 4 * TOK:5 * SLAB].rearrange("p (c t) -> p c t", c=4)
        og = slab(0)
        S_gla = arena[:, s1:s1 + 2048].rearrange("p (d h e) -> p d h e", d=2, h=GH)

        def five(i):
            return arena[:, s1 + 2048 + 512 * i:s1 + 2560 + 512 * i]

        def heads4(ap):
            return ap.rearrange("p (h n) -> p h n", h=4)

        attm = [heads4(five(0)), heads4(five(1))]
        qdec = [heads4(five(2)), heads4(five(3))]
        kutok = [heads4(five(4)), heads4(five(5))]
        gcs, gx = five(6), five(7)
        gl = tail[:, 2816:3328]
        grow, kk = spare[:, 0:512], spare[:, 512:1024]
        gshrink, ku = gate_o[:, 0:512], gate_o[:, 512:1024]
        chunk_dec = small[:, 0:16].rearrange("p (d h a) -> p d h a", d=2, h=GH)
        tile_dec = small[:, 16:24].rearrange("p (d h) -> p d h", d=2)
        first_half = (0, 1)
        mrow = tail[:, 1280:1792]
        sq_junk = dtv.rearrange("p t n -> p (t n)").bitcast(mybir.dt.bfloat16)[:, 0:GV]
        x1 = slab(0)
        gate_e = arena[:, 4 * SLAB:4 * SLAB + 2 * DM].rearrange("p (s n) -> p s n", s=2)
        etmp = [arena[:, 4 * SLAB + 2048 + HB * i:4 * SLAB + 2048 + HB * (i + 1)] for i in (0, 1)]
        junk_o = arena[:, 4 * SLAB + 3072:4 * SLAB + 3072 + DM]
        xn1 = slab(3)
        qT = arena[:, 3 * SLAB:3 * SLAB + 8192].rearrange("p (t h c) -> p t h c", t=LT, h=AH)
        tables = arena[:, 4 * SLAB + 4096:5 * SLAB].rearrange("p (a t n) -> p a t n", a=4, t=LT)
        kT = arena[:, SLAB:SLAB + AKV * TOK].rearrange("p (h t) -> p h t", h=AKV)
        va = arena[:, SLAB + 3072:2 * SLAB].rearrange("p (t n) -> p t n", t=TT)
        amask = arena[:, 0:M_COLS]
        h1_hi, h1_lo = parts(5), parts(2)
        free_a = arena[:, 4 * SLAB + 2048:4 * SLAB + 4096]
        free_b = arena[:, 2 * SLAB:2 * SLAB + 2048]
        prob = [free_a[:, 640 * i:640 * (i + 1)] for i in (0, 1)]
        probT = [free_b[:, 640 * i:640 * (i + 1)].rearrange("p (b q) -> p b q", b=5) for i in (0, 1)]
        onorm = [free_a[:, 1280:1792], free_b[:, 1280:1792]]
        gateT = [tail[:, 512 * i:512 * (i + 1)] for i in (0, 1)]
        ftmp = [spare[:, HB * i:HB * (i + 1)] for i in (0, 1)]
        TW = AH * AD
        o_lo = [slab_r[3][:, TW * t:TW * (t + 1)] for t in range(3)] + [slab_r[4][:, 0:TW]]
        o_hi = [slab_r[1][:, TW * t:TW * (t + 1)] for t in range(3)] + [slab_r[2][:, 0:TW]]
        o_lo, o_hi = ([m.rearrange("p (h c) -> p h c", h=AH) for m in o] for o in (o_lo, o_hi))
        o_lo3, o_hi3 = (slab_r[i][:, :].rearrange("p (t h c) -> p t h c", t=3, h=AH) for i in (3, 1))
        rp = [[tail[:, 2048 * b + 512 * i:2048 * b + 512 * i + HB] for i in range(4 if b == 0 else 2)] for b in (0, 1)]
        rp[1] += [spare[:, 0:HB], spare[:, 512:512 + HB]]

        def heads2(ap):
            return ap.rearrange("p (h n) -> p h n", h=2)

        qk_gain = sb("qk_gain", [P, 2, AD])

        ps = es.enter_context(nc.psum_tensor("ps", [P, 8, NB], f32))

        def banks(b, n=1):
            return ps[:, b:b + n, :].rearrange("p b n -> p (b n)")

        def eo_out(n, t):
            return ps[:, 3 * (n % 2) + t // 2, HB * (t % 2):HB * (t % 2 + 1)]

        def oo_out(n, t):
            return ps[:, 2 * n + t // 2, HB * (t % 2):HB * (t % 2 + 1)]

        chunks, slot_of, arrivals, before, split = [], [], [], [], []
        HI = {0: 2, 1: 3, 4: 5}
        owner, loads = [None] * 6, [0] * 6

        def add_chunk(src, slot, two):
            n = len(chunks)
            chunks.append(src)
            slot_of.append(slot)
            loads[slot] += 1
            arrivals.append(loads[slot])
            before.append((owner[slot], owner[HI[slot]] if two else None))
            split.append(two)
            owner[slot] = n
            if two:
                owner[HI[slot]] = n
            return n

        def plan(w, c0):
            return [add_chunk(w[0, KH * P * k:KH * P * (k + 1), c0:c0 + NB].rearrange("(j p) n -> p j n", p=P),
                              len(chunks) % SLOTS, False) for k in range(w.shape[1] // (KH * P))]

        def plan_split(w, c0, k0=0, slot=None):
            return add_chunk(w[0, P * k0:P * (k0 + KT), c0:c0 + HB].rearrange("(j p) n -> p j n", p=P),
                             sum(split) % 2 if slot is None else slot, True)

        def whole(slot):
            return ring[:, slot, :, :].rearrange("p j n -> p (j n)") if slot < SLOTS else free_a

        def part(slot):
            if slot < SLOTS:
                return ring_r[:, slot, :, :].rearrange("p j n -> p (j n)")
            return slab_r[4][:, 2048:4096] if slot == 4 else slab_r[5][:, 0:2048]

        complete = [max(i for i in range(2 * TT) if ORDER[i % 2][i // 2] == t) for t in range(TT)]
        FIN = sorted(range(TT), key=lambda t: complete[t])
        norm_at = {9: [0], 10: [1, 2], 11: [3]}
        MB = 6
        mod_ch = [[plan(e_mod_w, NB * b) for b in range(4)], []]
        xbc_ch = [plan_split(e_w_in, E_XBC + HB * b) for b in range(XB // 2)]
        z_ch = [plan_split(e_w_in, E_Z + HB * b) for b in range(4)]
        qk_ch = [plan_split(e_w_in, E_Q + HB * b) for b in range(4)]
        v_ch = [plan_split(e_w_in, E_V + HB * b) for b in range(4)]
        g_ch = [plan_split(e_w_in, E_G + HB * b) for b in range(4)]
        mod_ch[0] += [plan(e_mod_w, NB * b) for b in range(4, MB)]
        mod_ch[1] += [plan(o_mod_w, NB * b) for b in range(MB)]
        eo_ch = [plan_split(e_w_out, HB * (q // 2), KT * (q % 2)) for q in range(8)]
        turns = [0, 1, 0, 1] + [4, 0, 1] * 2 + [4, 0] + [1, 0] + [4, 1, 0] * 2
        oin_ch = [plan_split(o_w_in, HB * b, slot=turns[b]) for b in range(20)]
        oo_ch = [plan_split(o_w_out, HB * (q // 2), KT * (q % 2), slot=(4, 1, 0)[q % 3]) for q in range(8)]

        jobs = [("sm", 0, t) for t in range(TT)]
        jobs += [("xbc", cc, part) for cc in range(XB) for part in (0, 1)]
        JOBS_SSD = len(jobs)
        jobs += [("z", n, t) for n in range(4) for t in range(TT)]
        JOBS_Z = len(jobs)
        jobs += [("qk", cc, part) for cc in range(2 * GH) for part in (0, 1)]
        JOBS_QK = len(jobs)
        jobs += [("v", n, t) for n in range(4) for t in range(TT)]
        JOBS_V = len(jobs)
        jobs += [("g", n, t) for n in range(4) for t in range(TT)]
        JOBS_E = len(jobs)
        late = xbc_ch + z_ch + qk_ch + v_ch + g_ch
        first_job = {}
        for jj in range(TT, JOBS_E):
            kind, n, t = jobs[jj]
            first_job.setdefault({"xbc": xbc_ch[n // 2 % 6], "z": z_ch[n % 4], "qk": qk_ch[n // 2 % 4], "v": v_ch[n % 4],
                                  "g": g_ch[n % 4]}[kind], jj)
        DURING_SSD = XB // 2 + 1
        ready_at = {first_job[late[q - 1]] + (2 if late[q - 1] in xbc_ch + qk_ch else 3): late[q]
                    for q in range(2, len(late)) if q != DURING_SSD}
        jobs += [("k", n, t) for n in range(2) for t in range(CT)] + [("k", n, t) for n in range(2) for t in range(CT, TT)]
        jobs += [("va", 2 + n, t) for n in range(2) for t in range(TT)]
        jobs += [("q", 4 + n, t) for n in range(8) for t in range(CT, TT)]
        JOBS_Q = len(jobs)
        jobs += [("sg", m, 0) for m in range(AH)]
        UNROT = 2 * CT

        def o_chunk(jj):
            kind, n, t = jobs[jj]
            return oin_ch[12 + n // 2] if kind == "sg" else oin_ch[n]

        for jj in range(JOBS_E, len(jobs)):
            first_job.setdefault(o_chunk(jj), jj)
        after = {3: 4, 4: 2}
        ready_at.update({first_job[oin_ch[q - 1]] + after.get(q, 0): oin_ch[q] for q in range(3, 20) if q != 13})
        ready_at[JOBS_E + 10] = oin_ch[2]
        ready_at[first_job[oin_ch[19]]] = oo_ch[0]
        BY_DVE, BY_ACT = {"sm", "v", "va"}, {"xbc", "z", "qk", "g", "sg"}

        def emptied(j):
            d = jobs[j][0] in BY_DVE
            return d, sum(jobs[i][0] in (BY_DVE if d else BY_ACT) for i in range(j + 1))

        ropes = [j for j in range(len(jobs)) if jobs[j][0] in ("k", "q")]

        mod_mm = [sem("mod_mm_e"), sem("mod_mm_o")]
        proj_mm = sem("proj_mm")
        eo_mm, eo_w = sem("eo_mm"), sem("eo_w")
        oo_mm, oo_w = sem("oo_mm"), sem("oo_w")
        used = {}
        for l in (0, 1):
            for b, ch in enumerate(mod_ch[l]):
                used.update({n: (mod_mm[l], b + 1) for n in ch})
        for jj, (kind, n, t) in enumerate(jobs):
            ch = [o_chunk(jj)] if jj >= JOBS_E else {"sm": [], "xbc": [xbc_ch[n // 2 % 6]], "z": [z_ch[n % 4]], "qk": [qk_ch[n // 2 % 4]], "v": [v_ch[n % 4]],
                  "g": [g_ch[n % 4]]}[kind]
            used.update({m: (proj_mm, jj + 1) for m in ch})
        for q in range(8):
            used[eo_ch[q]] = (eo_w, q // 2 + 1) if q % 2 == 0 else (eo_mm, q // 2 + 1)
            used[oo_ch[q]] = (oo_w, q // 2 + 1) if q % 2 == 0 else (oo_mm, q // 2 + 1)
        w_hi, w_lo = sem("w_hi"), sem("w_lo")
        h_hi_done, h_lo_done, ys_hi_done, ys_lo_done, gT_hi_done = (sem(n) for n in (
            "h_hi_done", "h_lo_done", "ys_hi_done", "ys_lo_done", "gT_hi_done"))
        ring_full = [sem(f"ring_full{i}") for i in range(5)]
        cst_in, vec_in, bc_in, wsm_in, gw_in, nb_in, nb2_in = [sem(n) for n in (
            "cst_in", "vec_in", "bc_in", "wsm_in", "gw_in", "ssd_norm_in", "gla_norm_in")]
        vec2_in, cst2_in = sem("vec2_in"), sem("cst2_in")
        x_in = [sem(f"x_in{t}") for t in range(TT)]
        tab_in, mask_in, gain_in = sem("tab_in"), sem("mask_in"), sem("gain_in")
        gw_zero, conv_zero, S_zero = sem("gw_zero"), sem("conv_zero"), sem("S_zero")
        vec_T, vec_c, silu_done = sem("vec_T"), sem("vec_copied"), sem("silu_done")
        mod_done = [sem("mod_done_e"), sem("mod_done_o")]
        mod_row, mod_tr, mod_add = sem("mod_row"), sem("mod_tr"), sem("mod_add")
        late_mods = [(0, b) for b in range(4, MB)] + [(1, b) for b in range(MB)]
        rstd_in, xn_done, ht_tr, ht_done = ([sem(f"{n}{l}") for l in (0, 1)] for n in ("rstd_in", "xn_done", "ht_tr", "ht_done"))
        proj_dve, proj_act = sem("proj_dve"), sem("proj_act")
        lr_tr, lr_done = sem("lr_tr"), sem("lr_done")
        conv_done, xbc_done = sem("conv_done"), sem("xbc_done")
        xs_tr, xs_done, b_done = sem("xs_tr"), sem("xs_done"), sem("b_done")
        ex_mm = sem("ex_mm")
        dtraw, soft_in, ea_done, dta_done, y_init = (sem(n) for n in ("dtraw", "soft_in", "ea_done", "dta_done", "y_init"))
        cb_mm, d_mm, yo_mm, u_mm, yd_mm = (sem(n) for n in ("cb_mm", "d_mm", "yo_mm", "u_mm", "yd_mm"))
        ex_done, cbm_done, rd_done, dec_done, a_done = (sem(n) for n in ("ex_done", "cbm_done", "rd_done", "dec_done", "a_done"))
        xw_done, sscale, s_new, tmp_done, y_added = (sem(n) for n in ("xw_done", "s_scaled", "s_new", "tmp_done", "y_added"))
        yz_done, ssd_rstd, yn_done, yT_tr, yT_done = (sem(n) for n in ("yz_done", "ssd_rstd", "yn_done", "yT_tr", "yT_done"))
        g_zero = sem("gla_zero")
        lg_mm, lg_x, lg_sp, cs_done, e1_done, qd_done = (sem(n) for n in ("lg_mm", "lg_x", "lg_sp", "cs_done", "e1_done", "qd_done"))
        e2_done, ki_done, at_mm, am_done = (sem(n) for n in ("e2_done", "ki_done", "at_mm", "am_done"))
        ku_done, ku_tr, kut_done = (sem(n) for n in ("ku_done", "ku_tr", "kut_done"))
        ke_done, qi_done = sem("keys_to_end"), sem("queries_from_start")
        inter_mm, gu_mm, gs_new, o_added = (sem(n) for n in ("inter_mm", "gla_u_mm", "gla_s_new", "o_added"))
        g_rstd, gn_done, gg_done, gT_tr, gT_done = (sem(n) for n in ("gla_rstd", "gla_normed", "gla_gated", "gT_tr", "gT_done"))
        gr_mm, gr_done = sem("gate_row_mm"), sem("gate_row_done")
        eo_done = sem("eo_done")
        gain_done, rk_rstd, rk_t0, rk_b, rk_a, rk_r, rk_tr, rk_done = (sem(n) for n in (
            "tables_done", "rk_rstd", "rk_t0", "rk_b", "rk_a", "rk_r", "rk_tr", "rk_done"))
        sink_done = sem("sink_done")
        h1_hi_done, h1_lo_done, rk_ss, rk_out, o_hi_done, o_lo_done = (sem(n) for n in ("h1_hi_done", "h1_lo_done", "rk_squares", "rk_out", "o_hi_done", "o_lo_done"))
        s_mm, mx_done, p_done, p_tr, pt_a, pt_d, pv_mm = (sem(n) for n in ("s_mm", "mx_done", "p_done", "p_tr", "pt_act", "pt_dve", "pv_mm"))
        dk_done, ek_done, on_done, og_done, ot_tr, ot_done = (sem(n) for n in ("dk_done", "ek_done", "on_done", "og_done", "ot_tr", "ot_done"))
        fin_done, out_done = sem("fin_done"), sem("out_done")
        dve_own, act_own, pool_own = sem("dve_own"), sem("act_own"), sem("pool_own")

        def part_hi(eng, op, n):
            eng.wait_ge(ring_full[slot_of[n]], 16 * arrivals[n])
            if before[n][1] is not None:
                eng.wait_ge(*used[before[n][1]])
            elif n == oin_ch[4]:
                eng.wait_ge(proj_mm, first_job[oin_ch[3]] + CT)
            op(part(HI[slot_of[n]]), whole(slot_of[n])).then_inc(w_hi, 1)

        def part_lo(eng, n):
            eng.wait_ge(w_hi, sum(split[:n]) + 1)
            eng.tensor_tensor(part(slot_of[n]), whole(slot_of[n]), part(HI[slot_of[n]]).bitcast(f32), ALU.subtract).then_inc(w_lo, 1)

        def step(eng, own):
            n = [0]

            def do(ins):
                n[0] += 1
                ins.then_inc(own, 1)
                eng.wait_ge(own, n[0])
            return do

        block = es.enter_context(nc.Block())

        @block.sync
        def _(sp):
            def load(n):
                if before[n][0] is not None:
                    sp.wait_ge(*used[before[n][0]])
                if n == oin_ch[4]:
                    sp.wait_ge(rstd_in[1], 1)
                if n == oin_ch[14]:
                    sp.wait_ge(ot_done, LT * AKV)
                place = whole(slot_of[n]).rearrange("p (j n) -> p j n", n=HB if split[n] else NB)
                sp.dma_start(place, chunks[n]).then_inc(ring_full[slot_of[n]], 16)

            for n in range(4):
                load(n)
            sp.dma_start(cst[:, C_ID + P:C_COLS], consts[:, C_ID + P:C_COLS]).then_inc(cst2_in, 16)
            for n in range(4, eo_ch[2]):
                load(n)
            sp.wait_ge(gT_tr, TT)
            for t in range(TT):
                src = ctx_in[0, P * t:P * (t + 1), :] if t < CT else x[0, P * (t - CT):P * (t - CT + 1), :]
                sp.dma_start(x1[:, t, :], src).then_inc(x_in[t], 16)
            for n in range(eo_ch[2], oin_ch[2]):
                load(n)
            sp.wait_ge(eo_done, 4 * TT)
            for a in range(4):
                sp.dma_start(tables[:, a, :, :], rope[a // 2, :, :].rearrange("(t p) n -> p t n", p=P)).then_inc(tab_in, 16)
            for n in range(oin_ch[2], oin_ch[4]):
                load(n)
            sp.wait_ge(ht_tr[1], 2 * KT)
            sp.wait_ge(xn_done[1], TT)
            sp.dma_start(amask, masks).then_inc(mask_in, 16)
            for n in range(oin_ch[4], len(chunks)):
                load(n)
            for n in range(2):
                for t in range(LT):
                    sp.wait_ge(fin_done, (2 * n + 1) * LT + t + 1)
                    sp.dma_start(out[0, P * t:P * (t + 1), NB * n:NB * (n + 1)],
                                 x1[:, CT + t, NB * n:NB * (n + 1)]).then_inc(out_done, 16)
            sp.wait_ge(out_done, 16 * 2 * LT)

        @block.gpsimd
        def _(pool):
            do = step(pool, pool_own)
            pool.dma_start(vrow1[48:108, :], e_conv_w[0, :, :].rearrange("k (r p) -> (k r) p", p=P)).then_inc(vec2_in, 16)
            for r0, n, src in ((0, 8, o_norm[0, :]), (8, 24, o_mod_b[0, :])):
                pool.dma_start(vrow2[r0:r0 + n, :], src.rearrange("(r p) -> r p", p=P)).then_inc(vec2_in, 16)
            pool.memset(gate_w, 0.0).then_inc(gw_zero, 1)
            pool.memset(arena[:, s5 + 2048:s5 + 2048 + 2 * RAW], 0.0).then_inc(conv_zero, 1)
            pool.memset(cbm, 0.0).then_inc(conv_zero, 1)
            pool.dma_start(w_small[:, :, 0:32], e_w_in[0, :, E_DT:E_DT + 32].rearrange("(k p) n -> p k n", p=P)).then_inc(wsm_in, 16)
            pool.dma_start(w_small[:, :, 32:64], e_w_in[0, :, E_LR:E_LR + 32].rearrange("(k p) n -> p k n", p=P)).then_inc(wsm_in, 16)
            pool.wait_ge(gw_zero, 1)
            for d in range(2):
                pool.dma_start(gate_w[RANK * d:RANK * (d + 1), d, :], e_gla_gate_w[0, d, :, :]).then_inc(gw_in, 16)
            pool.dma_start(qk_gain[:, 0, :], o_q_norm[0, :].partition_broadcast(P)).then_inc(gain_in, 16)
            pool.dma_start(qk_gain[:, 1, :], o_k_norm[0, :].partition_broadcast(P)).then_inc(gain_in, 16)
            pool.wait_ge(mod_tr, 4)
            pool.dma_start(norm_bc, e_ssd_norm[0, :].partition_broadcast(P)).then_inc(nb_in, 16)
            pool.wait_ge(vec_T, 1)
            pool.memset(S_ssd, 0.0).then_inc(S_zero, 1)
            pool.wait_ge(S_zero, 1)
            pool.wait_ge(xs_tr, TT)
            pool.wait_ge(bc_in, 64)
            pool.wait_ge(dta_done, 1)
            pool.wait_ge(ex_done, 1)
            seen = set()
            for u in range(4 * TT + 1):
                if u < 4 * TT:
                    s, g = u // 2, u % 2
                    d, t = s % 2, ORDER[s % 2][s // 2]
                    dts = dtv[:, t, SH * d + 8 * g:SH * d + 8 * g + 8]
                    xg = xs[:, t, GW * g:GW * (g + 1)].rearrange("p (h e) -> p h e", h=8)
                    pool.wait_ge(xs_done, t + 1)
                    if u >= 2:
                        pool.wait_ge(yd_mm, u - 1)
                        pool.wait_ge(u_mm, u - 1)
                    do(pool.tensor_tensor(xdt[u % 2].rearrange("p (h e) -> p h e", h=8), xg, spread(dts, 2, SD), ALU.mult))
                    pool.tensor_tensor(xw[u % 2].rearrange("p (h e) -> p h e", h=8), xdt[u % 2].rearrange("p (h e) -> p h e", h=8),
                                       spread(ex_all[:, d, 1, t, 8 * g:8 * g + 8], 2, SD), ALU.mult).then_inc(xw_done, 1)
                    if (t, g) not in seen:
                        seen.add((t, g))
                        pool.tensor_tensor(y[:, t, GW * g:GW * (g + 1)].rearrange("p (h e) -> p h e", h=8), xg,
                                           spread(d_skip[:, 8 * g:8 * g + 8], 2, SD), ALU.mult).then_inc(y_init, 1)
                if u >= 1:
                    v = u - 1
                    s, g = v // 2, v % 2
                    d, t = s % 2, ORDER[s % 2][s // 2]
                    Sg = S_ssd[:, d, GW * g:GW * (g + 1)].rearrange("p (h e) -> p h e", h=8)
                    pool.wait_ge(yo_mm, v + 1)
                    if v >= 4:
                        pool.wait_ge(s_new, v - 3)
                    pool.tensor_tensor(Sg, Sg, spread(ex_all[:, d, 2, t, 8 * g:8 * g + 8], 2, SD), ALU.mult).then_inc(sscale, 1)
                    pool.wait_ge(tmp_done, v + 1)
                    pool.wait_ge(y_init, len(seen))
                    if v >= 2:
                        pool.wait_ge(y_added, v - 1)
                    yg = y[:, t, GW * g:GW * (g + 1)]
                    pool.tensor_tensor(yg, yg, ytmp, ALU.add).then_inc(y_added, 1)
            pool.wait_ge(proj_mm, JOBS_E)
            pool.memset(arena[:, s1:s1 + 2048], 0.0).then_inc(g_zero, 1)
            pool.memset(arena[:, s1 + 2048:s1 + 3072], 0.0).then_inc(g_zero, 1)
            pool.wait_ge(proj_act, emptied(JOBS_QK - 1)[1])
            pool.wait_ge(u_mm, 4 * TT)

            def keys(i):
                d, t = i % 2, ORDER[i % 2][i // 2]
                end = HALF - 1 if d == 0 else 0
                pool.wait_ge(e2_done, i + 1)
                if i >= 1:
                    pool.wait_ge(at_mm, i)
                pool.tensor_tensor(heads4(kk), kT_g[:, :, P * t:P * (t + 1)], heads4(gshrink), ALU.mult).then_inc(ki_done, 1)
                pool.wait_ge(ki_done, i + 1)
                if i >= 1:
                    pool.wait_ge(ku_tr, i)
                pool.tensor_tensor(ku.rearrange("p (h n) -> p h n", n=HALF), kk.rearrange("p (h n) -> p h n", n=HALF),
                                   spread(grow.rearrange("p (h n) -> p h n", n=HALF)[:, :, end], 2, HALF), ALU.mult).then_inc(ku_done, 1)

            def keys_to_end(i):
                d = i % 2
                a0 = first_half[d]
                pool.wait_ge(at_mm, i + 1)
                pool.wait_ge(qd_done, i + 1)
                pool.wait_ge(ku_done, i + 1)
                k0 = heads4(ku)[:, :, HALF * a0:HALF * (a0 + 1)]
                pool.tensor_tensor(k0, k0, spread(chunk_dec[:, d, :, 1 - a0], 2, HALF), ALU.mult).then_inc(ke_done, 1)

            def gate_tile(n):
                t = FIN[n]
                pool.wait_ge(proj_act, emptied(JOBS_E - 1)[1])
                pool.wait_ge(gn_done, n + 1)
                pool.tensor_tensor(og[:, t, :], og[:, t, :], gs[:, t, :], ALU.mult).then_inc(gg_done, 1)

            keys(0)
            keys_to_end(0)
            for i in range(2 * TT):
                if i + 1 < 2 * TT:
                    keys(i + 1)
                    keys_to_end(i + 1)
                if i == len(late_mods) - 1:
                    pool.wait_ge(mod_tr, 4 + len(late_mods))
                    pool.dma_start(norm_bc, e_gla_norm[0, :].partition_broadcast(P)).then_inc(nb2_in, 16)
                for n in norm_at.get(i, []):
                    gate_tile(n)
            for n in range(sum(len(v) for v in norm_at.values()), TT):
                gate_tile(n)
            for r, j in enumerate(ropes):
                kind, n, t = jobs[j]
                t0, A, B, R = rp[r % 2]
                if r < UNROT:
                    continue
                rot = r - UNROT
                a = 2 if kind == "q" else 3
                pool.wait_ge(rk_t0, r + 1)
                pool.wait_ge(gain_done, 4)
                pool.tensor_tensor(heads2(B), heads2(t0), spread(tables[:, a, t - CT, :], 1, 2), ALU.mult).then_inc(rk_b, 1)
                pool.wait_ge(rk_b, rot + 1)
                pool.wait_ge(rk_a, rot + 1)
                if r >= 2:
                    pool.wait_ge(rk_tr, r - 1)
                A4, B4, R4 = (m.rearrange("p (a s f) -> p a s f", s=2, f=32) for m in (A, B, R))
                pool.tensor_tensor(R4[:, :, 0, :], A4[:, :, 0, :], B4[:, :, 1, :], ALU.add)
                pool.tensor_tensor(R4[:, :, 1, :], A4[:, :, 1, :], B4[:, :, 0, :], ALU.add).then_inc(rk_r, 1)
            pool.wait_ge(ot_done, LT * AKV)
            for m in range(AH):
                pool.wait_ge(proj_act, emptied(JOBS_Q + m)[1])
                om = qT[:, :, m, :]
                pool.tensor_tensor(om, om, gateT[m % 2].rearrange("p (t c) -> p t c", t=LT), ALU.mult).then_inc(og_done, 1)

        @block.scalar
        def _(act):
            do = step(act, act_own)
            act.dma_start(ident, consts[:, C_ID:C_ID + P]).then_inc(cst_in, 16)
            for r0, n, src in ((0, 8, c[0, :]), (8, 8, c_ctx[:]), (16, 8, e_norm[0, :]), (24, 24, e_mod_b[0, :]),
                               (108, 12, e_conv_b[0, :]), (120, 8, e_gla_gate_b[0, :, :])):
                src = src.rearrange("(r p) -> r p", p=P) if len(src.shape) == 1 else src.rearrange("k (r p) -> (k r) p", p=P)
                act.dma_start(vrow1[r0:r0 + n, :], src).then_inc(vec_in, 16)
            for t in range(TT):
                src = ctx_in[0, P * t:P * (t + 1), :] if t < CT else x[0, P * (t - CT):P * (t - CT + 1), :]
                act.dma_start(xs[:, t, :], src).then_inc(x_in[t], 16)
            for c0, src in ((0, e_dt_bias[0, :, :].rearrange("a b -> (a b)")), (32, e_a_log[0, :, :].rearrange("a b -> (a b)")),
                            (64, e_d_skip[0, :]), (80, o_sink[0, :])):
                act.dma_start(bc_small[:, c0:c0 + src.shape[0]], src.partition_broadcast(P)).then_inc(bc_in, 16)
            act.wait_ge(vec_c, 1)
            act.activation(silu_c[:, :], banks(3)[:, 0:16], ACT.Silu).then_inc(silu_done, 1)

            def inv_rms(ss, width):
                do(act.activation(ss, ss, ACT.Copy, scale=1.0 / width, bias=EPS))
                do(act.activation(ss, ss, ACT.Ln))
                return act.activation(ss, ss, ACT.Exp, scale=-0.5)

            def token_rstd(l):
                src = (xs, x1)[l]
                ss = small[:, 96:96 + TT]
                for t in range(TT):
                    if l == 0:
                        act.wait_ge(x_in[t], 16)
                    else:
                        act.wait_ge(eo_done, 3 * TT + t + 1)
                    do(act.activation((junk, junk_o)[l], src[:, t, :], ACT.Square, accum_out=ss[:, t:t + 1]))
                inv_rms(ss, DM).then_inc(rstd_in[l], 1)

            token_rstd(0)

            def mod_rows(n, l, b, bank):
                act.wait_ge(mod_mm[l], b + 1)
                if n >= 1:
                    act.wait_ge(mod_tr, n)
                act.activation(mrow[0:2, :], banks(bank)[0:2, :], ACT.Copy).then_inc(mod_row, 1)

            for b in range(4):
                mod_rows(b, 0, b, b % 2)

            def hi_of(out_, in_):
                return act.activation(out_, in_, ACT.Copy)

            def proj_evac(j):
                kind, n, t = jobs[j]
                act.wait_ge(proj_mm, j + 1)
                bank = banks(j % 2)
                if kind == "xbc":
                    if n >= 2:
                        act.wait_ge(conv_done, n - 1)
                    if n < 2:
                        act.wait_ge(conv_zero, 2)
                    o0, w = (2, CTX) if t == 0 else (CTX + 4, LAT)
                    ins = act.activation(raw[n % 2][:, o0:o0 + w], bank[:, 0:w], ACT.Copy)
                elif kind == "z":
                    if j - 2 >= JOBS_SSD:
                        act.wait_ge(yz_done, j - 1 - JOBS_SSD)
                    ins = act.activation(zt[j % 2], bank[:, 0:HB], ACT.Silu)
                elif kind == "qk":
                    o0, w = (0, CTX) if t == 0 else (CTX, LAT)
                    dst = (qT_g if n < GH else kT_g)[:, n % GH, o0:o0 + w]
                    ins = act.activation(dst, bank[:, 0:w], ACT.Copy, scale=float(GK) ** -0.5 if n < GH else 1.0)
                elif kind == "g":
                    ins = act.activation(gs[:, t, HB * n:HB * (n + 1)], bank[:, 0:HB], ACT.Silu)
                else:
                    if n >= 2:
                        act.wait_ge(og_done, n - 1)
                    ins = act.activation(gateT[n % 2], bank, ACT.Silu)
                ins.then_inc(proj_act, 1)

            def conv_silu(cc):
                act.wait_ge(conv_done, cc + 1)
                dst = xT[:, cc, :] if cc < 8 else bcT[:, cc - 8, :]
                act.activation(dst[:, 0:CTX], cacc[cc % 2][:, 0:CTX], ACT.Silu)
                act.activation(dst[:, CTX:TOK], cacc[cc % 2][:, CTX + 2:TOK + 2], ACT.Silu).then_inc(xbc_done, 1)

            for n, t in enumerate([2, 3, 4, 5, 0, 1]):
                act.wait_ge(ht_done[0], KT if n < LT else 2 * KT)
                act.activation(h_hi[:, t, :, :], hT[0][:, t, :, :], ACT.Copy).then_inc(h_hi_done, 1)
            part_hi(act, hi_of, late[0])
            part_hi(act, hi_of, late[1])
            act.wait_ge(dtraw, TT)
            a3 = dta[:, :, :]
            do(act.activation(a3, dtv[:, :, :], ACT.Abs))
            do(act.activation(a3, a3, ACT.Exp, scale=-1.0))
            act.activation(a3, a3, ACT.Ln, bias=1.0).then_inc(soft_in, 1)
            act.wait_ge(bc_in, 64)
            act.activation(a_log, a_log, ACT.Exp).then_inc(ea_done, 1)
            j = TT
            for cc in range(XB):
                if j in ready_at:
                    part_hi(act, hi_of, ready_at[j])
                proj_evac(j)
                proj_evac(j + 1)
                j += 2
                if cc >= 1:
                    conv_silu(cc - 1)
                if cc == 3:
                    act.wait_ge(ex_mm, 1)
                    for d in range(2):
                        ins = act.activation(gate_o[:, 3 * TT * SH * d:3 * TT * SH * (d + 1)], banks(6 + d)[:, 0:3 * TT * SH], ACT.Exp)
                    ins.then_inc(ex_done, 1)
            conv_silu(XB - 1)
            for t in range(TT):
                act.wait_ge(xs_tr, t + 1)
                act.activation(xs[:, t, :], banks(2 + 3 * (t % 2), 2), ACT.Copy).then_inc(xs_done, 1)
            for u in range(4 * TT):
                s, g = u // 2, u % 2
                if u == 14:
                    part_hi(act, hi_of, late[DURING_SSD])
                act.wait_ge(d_mm, u + 1)
                if u >= 2:
                    act.wait_ge(yd_mm, u - 1)
                act.activation(Edec[u % 2].rearrange("p h i -> p (h i)"), banks(2, 2), ACT.Exp).then_inc(dec_done, 1)
            act.wait_ge(xw_done, 4 * TT)
            act.wait_ge(u_mm, 4 * TT)
            act.wait_ge(yd_mm, 4 * TT)
            ss = small[:, 104:104 + 2 * TT]

            def ssd_squares(t):
                act.wait_ge(yz_done, 3 * TT + t + 1)
                for g in range(SG):
                    do(act.activation(junk[:, 0:GW], y[:, t, GW * g:GW * (g + 1)], ACT.Square, accum_out=ss[:, 2 * t + g:2 * t + g + 1]))

            while j < JOBS_Z:
                if j in ready_at:
                    part_hi(act, hi_of, ready_at[j])
                proj_evac(j)
                if j - (JOBS_Z - TT) >= 1:
                    ssd_squares(j - (JOBS_Z - TT) - 1)
                j += 1
            ssd_squares(TT - 1)
            inv_rms(ss, GW).then_inc(ssd_rstd, 1)
            while j < JOBS_QK:
                if j in ready_at:
                    part_hi(act, hi_of, ready_at[j])
                proj_evac(j)
                j += 1

            def out_T(dst, tr, done):
                for t in range(TT):
                    act.wait_ge(tr, t + 1)
                    act.activation(dst[:, t, :, :].rearrange("p k c -> p (k c)"), banks(2 + 2 * (t % 2), 2), ACT.Copy).then_inc(done, 1)

            out_T(yT_ssd, yT_tr, yT_done)
            while j < JOBS_E:
                if j in ready_at:
                    part_hi(act, hi_of, ready_at[j])
                if jobs[j][0] == "g":
                    proj_evac(j)
                j += 1
            act.preload_act_table_set("natural_log_exp_and_others")
            act.wait_ge(a_done, 4 * TT)
            act.wait_ge(yd_mm, 4 * TT)
            act.wait_ge(u_mm, 4 * TT)
            act.wait_ge(yn_done, TT)

            def soft(i):
                act.wait_ge(lg_x, i + 1)
                if i >= 1:
                    act.wait_ge(cs_done, i)
                do(act.activation(gl, gx, ACT.Abs))
                do(act.activation(gl, gl, ACT.Exp, scale=-1.0))
                act.activation(gl, gl, ACT.Ln, bias=1.0).then_inc(lg_sp, 1)

            def exps(i):
                act.wait_ge(cs_done, i + 1)
                if i >= 1:
                    act.wait_ge(qd_done, i)
                    act.wait_ge(ku_done, i)
                act.activation(grow, gcs, ACT.Exp, scale=1.0 / 16).then_inc(e1_done, 1)
                act.activation(gshrink, gcs, ACT.Exp, scale=-1.0 / 16).then_inc(e2_done, 1)

            def key_rows(i):
                act.wait_ge(ku_tr, i + 1)
                if i >= 2:
                    act.wait_ge(gu_mm, 2 * (i - 1))
                act.activation(kutok[i % 2].rearrange("p h n -> p (h n)"), banks(7), ACT.Copy).then_inc(kut_done, 1)

            def tile_rstd(n):
                t = FIN[n]
                ss = small[:, 116 + GH * t:116 + GH * (t + 1)]
                act.wait_ge(o_added, complete[t] + 1)
                for h in range(GH):
                    do(act.activation(sq_junk, og[:, t, GV * h:GV * (h + 1)], ACT.Square, accum_out=ss[:, h:h + 1]))
                inv_rms(ss, GV).then_inc(g_rstd, 1)

            soft(0)
            mod_rows(4, *late_mods[0], 0)
            exps(0)
            soft(1)
            key_rows(0)
            exps(1)
            for i in range(2 * TT):
                if i + 1 < len(late_mods):
                    mod_rows(5 + i, *late_mods[i + 1], 0)
                if i + 2 < 2 * TT:
                    soft(i + 2)
                if i + 1 < 2 * TT:
                    key_rows(i + 1)
                if i + 2 < 2 * TT:
                    exps(i + 2)
                for n in range(TT):
                    if complete[FIN[n]] == i - 1:
                        tile_rstd(n)
                if i in (8, 9):
                    part_hi(act, hi_of, eo_ch[i - 8])
            tile_rstd(TT - 1)
            for n, t in enumerate(FIN):
                act.wait_ge(gg_done, n + 1)
                act.activation(ys_hi[:, t, :, :], yT_ssd[:, t, :, :], ACT.Copy).then_inc(ys_hi_done, 1)
                act.wait_ge(gT_tr, n + 1)
                act.activation(yg_hi[:, t, :, :].rearrange("p k c -> p (k c)"), banks(2 + 2 * (n % 2), 2), ACT.Copy).then_inc(gT_hi_done, 1)
            for q in range(3):
                act.wait_ge(gr_mm, q + 1)
                dst = gate_e[:, q, :] if q < 2 else gate_o[:, :]
                act.activation(dst, banks(2 + 2 * (q % 2), 2), ACT.Copy).then_inc(gr_done, 1)
            for q in range(2, 8):
                part_hi(act, hi_of, eo_ch[q])
            part_hi(act, hi_of, oin_ch[0])
            token_rstd(1)
            part_hi(act, hi_of, oin_ch[1])

            for q in range(2 * KT):
                kt, st = q % KT, q // KT
                t0, n = (CT, LT) if st == 0 else (0, CT)
                act.wait_ge(ht_done[1], q + 1)
                act.activation(h1_hi[:, t0:t0 + n, kt, :], hT[1][:, t0:t0 + n, kt, :], ACT.Copy).then_inc(h1_hi_done, 1)

            def rope_rstd(r):
                ss = small[:, 140 + 2 * (r % 2):142 + 2 * (r % 2)]
                act.wait_ge(rk_ss, r + 1)
                do(act.activation(ss, ss, ACT.Ln))
                act.activation(ss, ss, ACT.Exp, scale=-0.5).then_inc(rk_rstd, 1)

            def rope_T(r):
                kind, n, t = jobs[ropes[r]]
                act.wait_ge(rk_tr, r + 1)
                src = heads2(banks(2 + r % 2)[:, 0:HB])
                if kind == "k":
                    dst = kT[:, 2 * n:2 * n + 2, P * t:P * (t + 1)]
                else:
                    dst = qT[:, t - CT, 2 * (n - 4):2 * (n - 3), :]
                act.activation(dst, src, ACT.Copy).then_inc(rk_done, 1)

            act.wait_ge(ht_tr[1], 2 * KT)
            r = 0
            for j in range(JOBS_E, JOBS_Q + 2):
                if j < JOBS_Q and jobs[j][0] in ("k", "q"):
                    rope_rstd(r)
                    r += 1
                if j - 2 in ropes:
                    rope_T(ropes.index(j - 2))
                if j in ready_at and j < JOBS_Q:
                    part_hi(act, hi_of, ready_at[j])
            def probs(a):
                t, h = a // AH, a % AH
                nk = CTX + P * (3 if 0 < t < LT - 1 else 2)
                act.wait_ge(mx_done, a + 1)
                if h % GRP == 0 and t >= 1:
                    act.wait_ge(on_done, a // GRP - AKV + 1)
                act.activation(prob[a % 2][:, 0:nk], prob[a % 2][:, 0:nk], ACT.Exp, scale=-1.0, bias=small[:, 160 + h:161 + h],
                               accum_out=small[:, 176 + h:177 + h]).then_inc(p_done, 1)

            def probs_T(a):
                act.wait_ge(p_tr, a + 1)
                if a >= 2:
                    act.wait_ge(pv_mm, a - 1)
                act.activation(probT[a % 2][:, 0:4, :].rearrange("p b q -> p (b q)"), banks(6), ACT.Copy).then_inc(pt_a, 1)

            NA = LT * AH
            for a in range(NA + 1):
                if a == GRP:
                    part_hi(act, hi_of, oin_ch[13])
                if a < NA:
                    probs(a)
                if a >= 1:
                    v = a - 1
                    probs_T(v)
                    if v % GRP == GRP - 1:
                        G = v // GRP
                        g4 = G % AKV
                        act.wait_ge(dk_done, G + 1)
                        act.activation(small[:, 192 + 4 * g4:196 + 4 * g4], small[:, 192 + 4 * g4:196 + 4 * g4], ACT.Exp).then_inc(ek_done, 1)
                    if v % GRP == 1 and v >= GRP:
                        G = v // GRP - 1
                        act.wait_ge(ot_tr, G + 1)
                        act.activation(qT[:, G // AKV, 4 * (G % AKV):4 * (G % AKV) + 4, :].rearrange("p h c -> p (h c)"), banks(1), ACT.Copy).then_inc(ot_done, 1)
            G = LT * AKV - 1
            act.wait_ge(ot_tr, G + 1)
            act.activation(qT[:, G // AKV, 4 * (G % AKV):4 * (G % AKV) + 4, :].rearrange("p h c -> p (h c)"), banks(1), ACT.Copy).then_inc(ot_done, 1)
            for m in range(AH + 1):
                j = JOBS_Q + m
                if m < AH:
                    proj_evac(j)
                if j in ready_at:
                    part_hi(act, hi_of, ready_at[j])
                if m >= 1:
                    act.wait_ge(og_done, m)
                    act.activation(o_hi3[:, :, m - 1, :], qT[:, 0:3, m - 1, :], ACT.Copy)
                    act.activation(o_hi[3][:, m - 1, :], qT[:, 3, m - 1, :], ACT.Copy).then_inc(o_hi_done, 1)
            for q in range(1, 8):
                part_hi(act, hi_of, oo_ch[q])

        @block.vector
        def _(dve):
            do = step(dve, dve_own)
            dve.wait_ge(vec_T, 1)
            dve.tensor_copy(vecs[:, :], banks(3)[:, 0:160]).then_inc(vec_c, 1)
            dve.wait_ge(vec_c, 1)

            def mod_block(n, l, b, bank):
                mb = vecs[:, (V_MB, V_OMB)[l] + 4 * b:(V_MB, V_OMB)[l] + 4 * b + 4]
                dve.wait_ge(mod_tr, n + 1)
                dve.tensor_tensor(mod[l][:, 4 * b:4 * b + 4, :], banks(bank)[:, 0:8].rearrange("p (m s) -> p m s", s=2),
                                  spread(mb, 2, 2), ALU.add).then_inc(mod_add, 1)

            def scale_gain(l, n):
                g = vecs[:, (V_N, V_ON)[l]:(V_N, V_ON)[l] + KT]
                dve.wait_ge(mod_add, n)
                dve.scalar_tensor_tensor(mod[l][:, 8:16, :], mod[l][:, 8:16, :], 1.0, spread(g, 2, 2), ALU.add, ALU.mult).then_inc(mod_done[l], 1)

            def h1_rest(q):
                kt, st = q % KT, q // KT
                t0, n = (CT, LT) if st == 0 else (0, CT)
                dve.wait_ge(h1_hi_done, q + 1)
                dve.tensor_tensor(h1_lo[:, t0:t0 + n, kt, :], hT[1][:, t0:t0 + n, kt, :], h1_hi[:, t0:t0 + n, kt, :].bitcast(f32),
                                  ALU.subtract).then_inc(h1_lo_done, 1)

            def normalise(l):
                dve.wait_ge(rstd_in[l], 1)
                src, dst = ((xs, xs), (x1, xn1))[l]
                for t in [2, 3, 4, 5, 0, 1]:
                    dve.tensor_scalar(dst[:, t, :], src[:, t, :], small[:, 96 + t:97 + t], None, ALU.mult).then_inc(xn_done[l], 1)
                dve.wait_ge(mod_done[l], 1)
                for q in range(2 * KT):
                    kt, s = q % KT, q // KT
                    t0, n = (CT, LT) if s == 0 else (0, CT)
                    dve.wait_ge(ht_tr[l], q + 1)
                    dve.tensor_scalar(hT[l][:, t0:t0 + n, kt, :], banks(4 + q % 2)[:, 0:n * P].rearrange("p (t c) -> p t c", t=n),
                                      mod[l][:, 8 + kt, s:s + 1], mod[l][:, kt, s:s + 1], ALU.mult, ALU.add).then_inc(ht_done[l], 1)
                    if l == 1 and q >= 1:
                        h1_rest(q - 1)
                if l == 1:
                    h1_rest(2 * KT - 1)

            for b in range(4):
                mod_block(b, 0, b, 2)
            scale_gain(0, 4)
            normalise(0)

            dve.wait_ge(bc_in, 64)
            for t in range(TT):
                dve.wait_ge(proj_mm, t + 1)
                dve.tensor_tensor(dtv[:, t, :], banks(t % 2)[:, 0:32], dt_bias, ALU.add).then_inc(dtraw, 1)
                dve.tensor_copy(lr_tok[:, t, :], banks(t % 2)[:, 32:64]).then_inc(proj_dve, 1)
                dve.wait_ge(h_hi_done, TT)
                dve.tensor_tensor(h_lo[:, t, :, :], hT[0][:, t, :, :], h_hi[:, t, :, :].bitcast(f32), ALU.subtract).then_inc(h_lo_done, 1)
                if t in (3, 5):
                    part_lo(dve, late[(t - 3) // 2])
            dve.wait_ge(soft_in, 1)
            dve.wait_ge(dtraw, TT)
            do(dve.scalar_tensor_tensor(dtv[:, :, :], dtv[:, :, :], 0.0, dta[:, :, :], ALU.max, ALU.add))
            dve.wait_ge(ea_done, 1)
            dve.scalar_tensor_tensor(dta[:, :, :], dtv[:, :, :], -1.0, spread(a_log, 1, TT), ALU.mult, ALU.mult).then_inc(dta_done, 1)
            dve.wait_ge(lr_tr, 1)
            dve.tensor_copy(lrT[:, 0:NB], banks(6)[0:32, :])
            dve.tensor_copy(lrT[:, NB:TOK], banks(7)[0:32, 0:TOK - NB]).then_inc(lr_done, 1)
            dve.wait_ge(cst2_in, 16)
            for cc in range(XB):
                if TT + 2 * cc in ready_at:
                    part_lo(dve, ready_at[TT + 2 * cc])
                dve.wait_ge(proj_act, 2 * cc + 2)
                if cc >= 2:
                    dve.wait_ge(xbc_done, cc - 1)
                acc = cacc[cc % 2]
                for k in range(CONV_K):
                    w = vecs[:, V_CW + XB * k + cc:V_CW + XB * k + cc + 1]
                    src = raw[cc % 2][:, k:k + TOK + 2]
                    if k == 0:
                        do(dve.tensor_scalar(acc, src, w, vecs[:, V_CB + cc:V_CB + cc + 1], ALU.mult, ALU.add))
                    elif k < CONV_K - 1:
                        do(dve.scalar_tensor_tensor(acc, src, w, acc, ALU.mult, ALU.add))
                    else:
                        dve.scalar_tensor_tensor(acc, src, w, acc, ALU.mult, ALU.add).then_inc(conv_done, 1)
            for t in range(TT):
                dve.wait_ge(xs_tr, t + 1)
                dve.tensor_copy(b_tok[:, t, :], banks(4 + 3 * (t % 2))[:, 0:2 * P]).then_inc(b_done, 1)
            dve.wait_ge(dta_done, 1)

            def decay_rhs(u):
                s, g = u // 2, u % 2
                d, t = s % 2, ORDER[s % 2][s // 2]
                if u >= 2:
                    dve.wait_ge(d_mm, u - 1)
                dve.tensor_tensor(RD[u % 2], spread(dta[:, t, SH * d + 8 * g:SH * d + 8 * g + 8], 2, P), spread(incl[d], 1, 8),
                                  ALU.mult).then_inc(rd_done, 1)

            def mask_cb(s):
                dve.wait_ge(cb_mm, s + 1)
                if s >= 2:
                    dve.wait_ge(a_done, 2 * (s - 1))
                dve.copy_predicated(cbm[:, s % 2, :, :], spread(incl[s % 2].bitcast(i32), 1, 2),
                                    banks(7)[:, 128:384].rearrange("p (g n) -> p g n", g=2)).then_inc(cbm_done, 1)

            dve.wait_ge(conv_zero, 2)
            decay_rhs(0)
            decay_rhs(1)

            def masked_decays(u):
                s, g = u // 2, u % 2
                dve.wait_ge(dec_done, u + 1)
                dve.wait_ge(cbm_done, s + 1)
                dve.tensor_tensor(Edec[u % 2], Edec[u % 2], spread(cbm[:, s % 2, g, :], 1, 8), ALU.mult).then_inc(a_done, 1)

            mask_cb(0)
            masked_decays(0)
            dve.wait_ge(ex_done, 1)
            for u in range(4 * TT):
                s, g = u // 2, u % 2
                d, t = s % 2, ORDER[s % 2][s // 2]
                if u == 15:
                    part_lo(dve, late[DURING_SSD])
                if u + 2 < 4 * TT:
                    decay_rhs(u + 2)
                if g == 1 and s + 1 < 2 * TT:
                    mask_cb(s + 1)
                if u + 1 < 4 * TT:
                    masked_decays(u + 1)
                dve.wait_ge(yo_mm, u + 1)
                if u >= 1:
                    dve.wait_ge(y_added, u)
                do(dve.tensor_tensor(ytmp.rearrange("p (h e) -> p h e", h=8), banks(5).rearrange("p (h e) -> p h e", h=8),
                                     spread(ex_all[:, d, 0, t, 8 * g:8 * g + 8], 2, SD), ALU.mult))
                dve.wait_ge(yd_mm, u + 1)
                dve.tensor_tensor(ytmp, ytmp, banks(4), ALU.add).then_inc(tmp_done, 1)
                dve.wait_ge(u_mm, u + 1)
                dve.wait_ge(sscale, u + 1)
                Sg = S_ssd[:, d, GW * g:GW * (g + 1)]
                dve.tensor_tensor(Sg, Sg, banks(6), ALU.add).then_inc(s_new, 1)
            dve.wait_ge(y_added, 4 * TT)
            for j in range(JOBS_SSD, JOBS_Z):
                n, t = jobs[j][1:]
                if j in ready_at:
                    part_lo(dve, ready_at[j])
                dve.wait_ge(proj_act, emptied(j)[1])
                yn = y[:, t, HB * n:HB * (n + 1)]
                dve.tensor_tensor(yn, yn, zt[j % 2], ALU.mult).then_inc(yz_done, 1)
            dve.wait_ge(ssd_rstd, 1)
            dve.wait_ge(nb_in, 16)
            dve.wait_ge(yz_done, 4 * TT)
            for t in range(TT):
                for g in range(SG):
                    yg = y[:, t, GW * g:GW * (g + 1)]
                    ins = dve.scalar_tensor_tensor(yg, yg, small[:, 104 + 2 * t + g:105 + 2 * t + g], norm_bc[:, GW * g:GW * (g + 1)],
                                                   ALU.mult, ALU.mult)
                ins.then_inc(yn_done, 1)
            for j in range(JOBS_Z, JOBS_E):
                kind, n, t = jobs[j]
                if j in ready_at:
                    part_lo(dve, ready_at[j])
                if kind == "v":
                    dve.wait_ge(proj_mm, j + 1)
                    dve.tensor_copy(vv[:, t, HB * n:HB * (n + 1)], banks(j % 2)[:, 0:HB]).then_inc(proj_dve, 1)

            def log_gates(i):
                d = i % 2
                dve.wait_ge(lg_mm, i + 1)
                if i >= 1:
                    dve.wait_ge(cs_done, i)
                dve.tensor_tensor(heads4(gx), heads4(banks(1)), spread(vecs[:, V_GB + 4 * d:V_GB + 4 * d + 4], 2, P), ALU.add).then_inc(lg_x, 1)

            def decays(i):
                d = i % 2
                dve.wait_ge(lg_sp, i + 1)
                dve.wait_ge(lg_x, i + 1)
                do(dve.scalar_tensor_tensor(gx, gx, 0.0, gl, ALU.min, ALU.subtract))
                if i >= 1:
                    dve.wait_ge(e2_done, i)
                o_, i_ = (gcs, gx) if d == 0 else (gcs[:, ::-1], gx[:, ::-1])
                dve.tensor_tensor_scan(o_, scan_keep, i_, 0.0, ALU.mult, ALU.add).then_inc(cs_done, 1)

            def dec_queries(i):
                d, t = i % 2, ORDER[i % 2][i // 2]
                end = HALF - 1 if d == 0 else 0
                dve.wait_ge(e1_done, i + 1)
                if i >= 2:
                    dve.wait_ge(inter_mm, i - 1)
                    dve.wait_ge(gs_new, 2 * (i - 1))
                    dve.wait_ge(ke_done, i - 1)
                do(dve.tensor_copy(chunk_dec[:, d, :, :], grow.rearrange("p (h a n) -> p h a n", h=GH, n=HALF)[:, :, :, end]))
                dve.tensor_tensor(tile_dec[:, d, :], chunk_dec[:, d, :, 0], chunk_dec[:, d, :, 1], ALU.mult)
                dve.tensor_tensor(qdec[d], qT_g[:, :, P * t:P * (t + 1)], heads4(grow), ALU.mult).then_inc(qd_done, 1)

            def mask_att(i):
                d = i % 2
                dve.wait_ge(at_mm, i + 1)
                if i >= 2:
                    dve.wait_ge(inter_mm, i - 1)
                dve.copy_predicated(attm[d], spread(incl[d].bitcast(i32), 1, 4), heads4(banks(6))).then_inc(am_done, 1)
                a0 = first_half[d]
                dve.wait_ge(qd_done, i + 1)
                q1 = qdec[d][:, :, HALF * (1 - a0):HALF * (2 - a0)]
                dve.tensor_tensor(q1, q1, spread(chunk_dec[:, d, :, a0], 2, HALF), ALU.mult).then_inc(qi_done, 1)

            def states(i):
                d = i % 2
                dve.wait_ge(inter_mm, i + 1)
                dve.wait_ge(qd_done, i + 1)
                for h in range(GH):
                    if h % 2 == 0:
                        dve.wait_ge(gu_mm, 2 * i + h // 2 + 1)
                    Sh = S_gla[:, d, h, :]
                    ins = dve.scalar_tensor_tensor(Sh, Sh, tile_dec[:, d, h:h + 1],
                                                   banks(2 + h // 2)[:, GV * (h % 2):GV * (h % 2 + 1)], ALU.mult, ALU.add)
                    if h % 2 == 1:
                        ins.then_inc(gs_new, 1)

            dve.wait_ge(g_zero, 2)
            dve.wait_ge(xw_done, 4 * TT)
            dve.wait_ge(u_mm, 4 * TT)
            dve.wait_ge(proj_act, emptied(JOBS_QK - 1)[1])

            def norm_tile(n):
                t = FIN[n]
                dve.wait_ge(nb2_in, 16)
                dve.wait_ge(g_rstd, n + 1)
                for h in range(GH):
                    oh = og[:, t, GV * h:GV * (h + 1)]
                    ins = dve.scalar_tensor_tensor(oh, oh, small[:, 116 + GH * t + h:117 + GH * t + h], norm_bc[:, GV * h:GV * (h + 1)],
                                                   ALU.mult, ALU.mult)
                ins.then_inc(gn_done, 1)

            log_gates(0)
            decays(0)
            log_gates(1)
            dec_queries(0)
            mod_block(4, *late_mods[0], 0)
            decays(1)
            mask_att(0)
            seen = set()
            for i in range(2 * TT):
                t = ORDER[i % 2][i // 2]
                if i + 2 < 2 * TT:
                    log_gates(i + 2)
                if i + 1 < 2 * TT:
                    dec_queries(i + 1)
                if i + 2 < 2 * TT:
                    decays(i + 2)
                if i + 1 < len(late_mods):
                    mod_block(5 + i, *late_mods[i + 1], 0)
                if i + 1 < 2 * TT:
                    mask_att(i + 1)
                dve.wait_ge(inter_mm, i + 1)
                if t in seen:
                    dve.wait_ge(o_added, i)
                    dve.tensor_tensor(og[:, t, :], og[:, t, :], banks(4, 2), ALU.add).then_inc(o_added, 1)
                else:
                    dve.tensor_copy(og[:, t, :], banks(4, 2)).then_inc(o_added, 1)
                seen.add(t)
                states(i)
                if i + 1 == len(late_mods):
                    scale_gain(1, 4 + len(late_mods))
                for n in norm_at.get(i, []):
                    norm_tile(n)
                if i in (9, 10):
                    part_lo(dve, eo_ch[i - 9])
            for n in range(sum(len(v) for v in norm_at.values()), TT):
                norm_tile(n)
            for n, t in enumerate(FIN):
                dve.wait_ge(ys_hi_done, n + 1)
                dve.tensor_tensor(ys_lo[:, t, :, :], yT_ssd[:, t, :, :], ys_hi[:, t, :, :].bitcast(f32), ALU.subtract).then_inc(ys_lo_done, 1)
                dve.wait_ge(gT_hi_done, n + 1)
                dve.tensor_tensor(yg_lo[:, t, :, :].rearrange("p k c -> p (k c)"), banks(2 + 2 * (n % 2), 2),
                                  yg_hi[:, t, :, :].rearrange("p k c -> p (k c)").bitcast(f32), ALU.subtract).then_inc(gT_done, 1)
            part_lo(dve, eo_ch[2])
            dve.wait_ge(gr_done, 2)
            for n in range(4):
                dve.wait_ge(eo_mm, n + 1)
                for t in range(TT):
                    e = etmp[t % 2]
                    do(dve.tensor_tensor(e, eo_out(n, t), gate_e[:, 1 if t < CT else 0, HB * n:HB * (n + 1)], ALU.mult))
                    if n == 0:
                        dve.wait_ge(x_in[t], 32)
                    xp = x1[:, t, HB * n:HB * (n + 1)]
                    dve.tensor_tensor(xp, xp, e, ALU.add).then_inc(eo_done, 1)
                if n < 3:
                    part_lo(dve, eo_ch[2 * n + 3])
                if n < 2:
                    part_lo(dve, eo_ch[2 * n + 4])
                if n == 2:
                    part_lo(dve, oin_ch[0])
            dve.wait_ge(eo_done, 4 * TT)
            normalise(1)
            part_lo(dve, oin_ch[1])
            dve.wait_ge(tab_in, 64)
            dve.wait_ge(gain_in, 32)
            for a in range(4):
                qk = a % 2
                g3 = spread(qk_gain[:, qk, :], 1, LT)
                sc = -float(AD) ** -0.5 if qk == 0 else 1.0
                dve.scalar_tensor_tensor(tables[:, a, :, :], tables[:, a, :, :], sc, g3, ALU.mult, ALU.mult).then_inc(gain_done, 1)
            dve.tensor_scalar(sink, sink, -1.0, None, ALU.mult).then_inc(sink_done, 1)
            dve.wait_ge(gain_done, 4)

            def squares(r, j):
                t0 = rp[r % 2][0]
                ss = small[:, 140 + 2 * (r % 2):142 + 2 * (r % 2)]
                dve.wait_ge(proj_mm, j + 1)
                if r > UNROT + 1:
                    dve.wait_ge(rk_b, r - 1 - UNROT)
                    dve.wait_ge(rk_a, r - 1 - UNROT)
                elif r >= 2:
                    dve.wait_ge(rk_r, min(r - 1, UNROT))
                dve.tensor_copy(t0, banks(j % 2)[:, 0:HB]).then_inc(rk_out, 1)
                dve.wait_ge(rk_out, r + 1)
                for h in range(2):
                    t0h = heads2(t0)[:, h, :]
                    ins = dve.tensor_tensor_reduce(out=vecs[:, 0:AD], in0=t0h, in1=t0h, scale=1.0 / AD, scalar=EPS,
                                                   op0=ALU.mult, op1=ALU.add, accum_out=ss[:, h:h + 1])
                    if h == 0:
                        do(ins)
                ins.then_inc(rk_ss, 1)

            def normed(r, j):
                kind, n, t = jobs[j]
                t0, A, B, R = rp[r % 2]
                ss = small[:, 140 + 2 * (r % 2):142 + 2 * (r % 2)]
                dve.wait_ge(rk_rstd, r + 1)
                dve.tensor_tensor(heads2(t0), heads2(t0), spread(ss, 2, AD), ALU.mult).then_inc(rk_t0, 1)
                dve.wait_ge(rk_t0, r + 1)
                if r < UNROT:
                    if r >= 2:
                        dve.wait_ge(rk_tr, r - 1)
                    dve.tensor_tensor(heads2(R), heads2(t0), spread(qk_gain[:, 1, :], 1, 2), ALU.mult).then_inc(rk_r, 1)
                else:
                    if r > UNROT + 1:
                        dve.wait_ge(rk_r, r - 1)
                    dve.tensor_tensor(heads2(A), heads2(t0), spread(tables[:, 0 if kind == "q" else 1, t - CT, :], 1, 2),
                                      ALU.mult).then_inc(rk_a, 1)

            for j in range(JOBS_E, JOBS_Q + 1):
                if j in ropes:
                    squares(ropes.index(j), j)
                elif j < JOBS_Q:
                    n, t = jobs[j][1:]
                    dve.wait_ge(proj_mm, j + 1)
                    dve.tensor_copy(va[:, t, HB * (n - 2):HB * (n - 1)], banks(j % 2)[:, 0:HB]).then_inc(proj_dve, 1)
                if j - 1 in ropes:
                    normed(ropes.index(j - 1), j - 1)
                if j - 1 in ready_at and j - 1 >= JOBS_E:
                    part_lo(dve, ready_at[j - 1])
            dve.wait_ge(mask_in, 16)
            dve.wait_ge(sink_done, 1)
            NA = LT * AH

            def row_min(a):
                t, h = a // AH, a % AH
                nk = CTX + P * (3 if 0 < t < LT - 1 else 2)
                m = amask[:, 0:nk] if t == 0 else amask[:, CTX + 2 * P:CTX + 2 * P + nk]
                dve.wait_ge(s_mm, a + 1)
                if a >= 2:
                    dve.wait_ge(p_tr, a - 1)
                dve.tensor_tensor_reduce(out=prob[a % 2][:, 0:nk], in0=banks(2 + 2 * (a % 2), 2)[:, 0:nk], in1=m, scale=1.0,
                                         scalar=sink[:, h:h + 1], op0=ALU.add, op1=ALU.min,
                                         accum_out=small[:, 160 + h:161 + h]).then_inc(mx_done, 1)

            for a in range(NA + 2):
                if a == GRP + 1:
                    part_lo(dve, oin_ch[13])
                if a < NA:
                    if a % GRP == 0 and a >= AH:
                        dve.wait_ge(ek_done, (a - AH) // GRP + 1)
                    row_min(a)
                if 1 <= a <= NA:
                    v = a - 1
                    t = v // AH
                    if 0 < t < LT - 1:
                        dve.wait_ge(p_tr, v + 1)
                        if v >= 2:
                            dve.wait_ge(pv_mm, v - 1)
                        dve.tensor_copy(probT[v % 2][:, 4, :], banks(7)[:, 0:P]).then_inc(pt_d, 1)
                    if v % GRP == GRP - 1:
                        G = v // GRP
                        g4 = G % AKV
                        dk = small[:, 192 + 4 * g4:196 + 4 * g4]
                        dve.wait_ge(mx_done, v + 1)
                        dve.tensor_tensor(dk, small[:, 160 + 4 * g4:164 + 4 * g4], sink[:, 4 * g4:4 * g4 + 4], ALU.subtract).then_inc(dk_done, 1)
                if a >= 2 and (a - 2) % GRP == GRP - 1:
                    v = a - 2
                    G = v // GRP
                    g4 = G % AKV
                    dk = small[:, 192 + 4 * g4:196 + 4 * g4]
                    dve.wait_ge(ek_done, G + 1)
                    do(dve.tensor_tensor(dk, dk, small[:, 176 + 4 * g4:180 + 4 * g4], ALU.add))
                    do(dve.reciprocal(dk, dk))
                    dve.wait_ge(pv_mm, v + 1)
                    if G >= 2:
                        dve.wait_ge(ot_tr, G - 1)
                    dve.tensor_tensor(heads4(onorm[G % 2]), heads4(banks(0)), spread(dk, 2, AD), ALU.mult).then_inc(on_done, 1)
            for m in range(AH):
                if JOBS_Q + m in ready_at:
                    part_lo(dve, ready_at[JOBS_Q + m])
                dve.wait_ge(o_hi_done, m + 1)
                dve.tensor_tensor(o_lo3[:, :, m, :], qT[:, 0:3, m, :], o_hi3[:, :, m, :].bitcast(f32), ALU.subtract)
                dve.tensor_tensor(o_lo[3][:, m, :], qT[:, 3, m, :], o_hi[3][:, m, :].bitcast(f32), ALU.subtract).then_inc(o_lo_done, 1)
            part_lo(dve, oo_ch[1])
            part_lo(dve, oo_ch[2])
            dve.wait_ge(gr_done, 3)
            for n in range(4):
                dve.wait_ge(oo_mm, n + 1)
                for t in range(LT):
                    f = ftmp[t % 2]
                    do(dve.tensor_tensor(f, oo_out(n, t), gate_o[:, HB * n:HB * (n + 1)], ALU.mult))
                    xp = x1[:, CT + t, HB * n:HB * (n + 1)]
                    dve.tensor_tensor(xp, xp, f, ALU.add).then_inc(fin_done, 1)
                if n < 3:
                    part_lo(dve, oo_ch[2 * n + 3])
                if n < 2:
                    part_lo(dve, oo_ch[2 * n + 4])

        @block.tensor
        def _(pe):
            mm = pe.matmul

            def arrived(n):
                pe.wait_ge(ring_full[slot_of[n]], 16 * arrivals[n])
                return ring[:, slot_of[n], :, :]

            def ready(n):
                pe.wait_ge(w_lo, sum(split[:n]) + 1)
                return [part(m).rearrange("p (k n) -> p k n", n=HB) for m in (HI[slot_of[n]], slot_of[n])]

            pe.wait_ge(cst_in, 16)
            pe.wait_ge(vec_in, 16 * 6)
            pe.wait_ge(vec2_in, 16 * 3)
            pe.transpose(banks(3)[:, 0:P], vrow1, ident)
            pe.transpose(banks(3)[:, P:P + 32], vrow2, ident[0:32, 0:32]).then_inc(vec_T, 1)

            def modulation(l, b, bank):
                w = [arrived(n) for n in mod_ch[l][b]]
                for k in range(KT):
                    ins = mm(banks(bank)[0:2, :], silu_c[:, k:16:8], w[k // KH][:, k % KH, :], start=(k == 0), stop=(k == KT - 1))
                ins.then_inc(mod_mm[l], 1)

            def modulation_T(n, bank):
                pe.wait_ge(mod_row, n + 1)
                for m in range(4):
                    ins = pe.transpose(banks(bank)[:, 2 * m:2 * m + 2], mrow[0:2, P * m:P * (m + 1)], ident[0:2, 0:2])
                ins.then_inc(mod_tr, 1)

            def transpose_h(l):
                src = (xs, xn1)[l]
                for q in range(2 * KT):
                    kt, s = q % KT, q // KT
                    pe.wait_ge(xn_done[l], LT if s == 0 else TT)
                    t0, n = (CT, LT) if s == 0 else (0, CT)
                    if q >= 2:
                        pe.wait_ge(ht_done[l], q - 1)
                    for t in range(n):
                        ins = pe.transpose(banks(4 + q % 2)[:, P * t:P * (t + 1)], src[:, t0 + t, P * kt:P * (kt + 1)], ident)
                    ins.then_inc(ht_tr[l], 1)

            pe.wait_ge(silu_done, 1)
            for b in range(5):
                if b >= 2:
                    pe.wait_ge(mod_row, b - 1)
                if b < 4:
                    modulation(0, b, b % 2)
                if b >= 1:
                    if b >= 2:
                        pe.wait_ge(mod_add, b - 1)
                    modulation_T(b - 1, 2)
            transpose_h(0)
            pe.wait_ge(ht_done[0], 2 * KT)
            pe.wait_ge(wsm_in, 32)

            def free_bank(j):
                if j >= 2:
                    d, n = emptied(j - 2)
                    pe.wait_ge(proj_dve if d else proj_act, n)

            def token_parts(j, n, h_hi=h_hi, h_lo=h_lo):
                t = jobs[j][2]
                hi, lo = ready(n)
                for k in range(KT):
                    for q, (a, w) in enumerate(((h_hi, hi), (h_hi, lo), (h_lo, hi))):
                        ins = mm(banks(j % 2)[:, 0:HB], a[:, t, k, :], w[:, k, :], start=(k == 0 and q == 0), stop=(k == KT - 1 and q == 2))
                ins.then_inc(proj_mm, 1)

            def feature_parts(j, n, m, part, h_hi=h_hi, h_lo=h_lo):
                hi, lo = ready(n)
                t0, nt = (0, CT) if part == 0 else (CT, LT)
                pe.wait_ge(h_lo_done, t0 + nt)
                for k in range(KT):
                    for q, (w, a) in enumerate(((hi, h_hi), (lo, h_hi), (hi, h_lo))):
                        ins = mm(banks(j % 2)[:, 0:nt * P], w[:, k, P * m:P * (m + 1)], a[:, t0:t0 + nt, k, :],
                                 start=(k == 0 and q == 0), stop=(k == KT - 1 and q == 2))
                ins.then_inc(proj_mm, 1)

            j = 0
            for t in range(TT):
                free_bank(j)
                for k in range(KT):
                    ins = mm(banks(j % 2)[:, 0:64], hT[0][:, t, k, :], w_small[:, k, :], start=(k == 0), stop=(k == KT - 1))
                ins.then_inc(proj_mm, 1)
                j += 1
            while j < JOBS_SSD:
                kind, n, t = jobs[j]
                if j == TT + 6:
                    pe.wait_ge(cst2_in, 16)
                    pe.wait_ge(dta_done, 1)
                    pe.wait_ge(lr_done, 1)
                    for d in range(2):
                        for q, lhsT in enumerate((incl[d], strict[d], ones)):
                            ins = mm(banks(6 + d)[:, TT * SH * q:TT * SH * (q + 1)], lhsT, dta[:, :, SH * d:SH * (d + 1)], start=True, stop=True)
                    ins.then_inc(ex_mm, 1)
                free_bank(j)
                feature_parts(j, xbc_ch[n // 2], n % 2, t)
                j += 1
                if j == TT + 2:
                    pe.wait_ge(proj_dve, TT)
                    for t in range(TT):
                        b, o0 = (6, P * t) if t < 4 else (7, P * (t - 4))
                        ins = pe.transpose(banks(b)[0:32, o0:o0 + P], lr_tok[:, t, :], ident)
                    ins.then_inc(lr_tr, 1)
            pe.wait_ge(xbc_done, XB)
            for t in range(TT):
                b = 2 + 3 * (t % 2)
                if t == 1:
                    pe.wait_ge(ex_done, 1)
                if t >= 2:
                    pe.wait_ge(xs_done, t - 1)
                    pe.wait_ge(b_done, t - 1)
                for cc in range(8):
                    pe.transpose(banks(b, 2)[:, P * cc:P * (cc + 1)], xT[:, cc, P * t:P * (t + 1)], ident)
                for cc in range(2):
                    ins = pe.transpose(banks(b + 2)[:, P * cc:P * (cc + 1)], bcT[:, cc, P * t:P * (t + 1)], ident)
                ins.then_inc(xs_tr, 1)

            def ssd_ahead(u):
                s, g = u // 2, u % 2
                d, t = s % 2, ORDER[s % 2][s // 2]
                if g == 0:
                    if s >= 1:
                        pe.wait_ge(cbm_done, s)
                    for q in range(SG):
                        ins = mm(banks(7)[:, 128 + 128 * q:256 + 128 * q], bcT[:, q, P * t:P * (t + 1)], bcT[:, 2 + q, P * t:P * (t + 1)],
                                 start=True, stop=True)
                    ins.then_inc(cb_mm, 1)
                pe.wait_ge(rd_done, u + 1)
                if u >= 1:
                    pe.wait_ge(dec_done, u)
                for q in range(2):
                    ins = mm(banks(2 + q), strict[d], RD[u % 2][:, 4 * q:4 * q + 4, :], start=True, stop=True)
                ins.then_inc(d_mm, 1)

            pe.wait_ge(dta_done, 1)
            pe.wait_ge(xs_done, TT)
            pe.wait_ge(b_done, TT)
            pe.wait_ge(S_zero, 1)
            ssd_ahead(0)
            ssd_ahead(1)
            for u in range(4 * TT):
                s, g = u // 2, u % 2
                d, t = s % 2, ORDER[s % 2][s // 2]
                if u >= 4:
                    pe.wait_ge(s_new, u - 3)
                if u >= 1:
                    pe.wait_ge(tmp_done, u)
                mm(banks(5), bcT[:, 2 + g, P * t:P * (t + 1)], S_ssd[:, d, GW * g:GW * (g + 1)], start=True, stop=True).then_inc(yo_mm, 1)
                pe.wait_ge(xw_done, u + 1)
                if u >= 1:
                    pe.wait_ge(s_new, u)
                mm(banks(6), b_tok[:, t, P * g:P * (g + 1)], xw[u % 2], start=True, stop=True).then_inc(u_mm, 1)
                pe.wait_ge(a_done, u + 1)
                for h in range(8):
                    ins = mm(banks(4)[:, SD * h:SD * (h + 1)], Edec[u % 2][:, h, :], xdt[u % 2][:, SD * h:SD * (h + 1)], start=True, stop=True)
                ins.then_inc(yd_mm, 1)
                if u + 2 < 4 * TT:
                    ssd_ahead(u + 2)

            while j < JOBS_E:
                kind, n, t = jobs[j]
                if j == JOBS_QK:
                    for tt in range(TT):
                        pe.wait_ge(yn_done, tt + 1)
                        if tt >= 2:
                            pe.wait_ge(yT_done, tt - 1)
                        else:
                            pe.wait_ge(tmp_done, 4 * TT)
                        for k in range(KT):
                            ins = pe.transpose(banks(2 + 2 * (tt % 2), 2)[:, P * k:P * (k + 1)], y[:, tt, P * k:P * (k + 1)], ident)
                        ins.then_inc(yT_tr, 1)
                free_bank(j)
                if kind == "qk":
                    feature_parts(j, qk_ch[n // 2], n % 2, t)
                else:
                    token_parts(j, {"z": z_ch, "v": v_ch, "g": g_ch}[kind][n])
                j += 1
            pe.wait_ge(yT_done, TT)
            pe.wait_ge(proj_act, emptied(JOBS_E - 1)[1])
            pe.wait_ge(proj_dve, emptied(JOBS_V - 1)[1])

            def gla_logits(i):
                d, t = i % 2, ORDER[i % 2][i // 2]
                if i >= 1:
                    pe.wait_ge(lg_x, i)
                for h in range(GH):
                    ins = mm(banks(1)[:, P * h:P * (h + 1)], gate_w[:, d, GK * h:GK * (h + 1)], lrT[:, P * t:P * (t + 1)], start=True, stop=True)
                ins.then_inc(lg_mm, 1)

            def gla_scores(i):
                d = i % 2
                pe.wait_ge(ki_done, i + 1)
                pe.wait_ge(qd_done, i + 1)
                if i >= 1:
                    pe.wait_ge(am_done, i)
                for h in range(GH):
                    mm(banks(6)[:, P * h:P * (h + 1)], heads4(kk)[:, h, :], qdec[d][:, h, :], start=True, stop=True)
                pe.wait_ge(ku_done, i + 1)
                a0 = first_half[d]
                j0, i0 = HALF * a0, HALF * (1 - a0)
                for h in range(GH):
                    ins = mm(banks(6)[j0:j0 + HALF, P * h + i0:P * h + i0 + HALF], heads4(ku)[:, h, j0:j0 + HALF],
                             qdec[d][:, h, i0:i0 + HALF], start=True, stop=True)
                ins.then_inc(at_mm, 1)

            def gla_keys(i):
                pe.wait_ge(ke_done, i + 1)
                if i >= 1:
                    pe.wait_ge(kut_done, i)
                for h in range(GH):
                    ins = pe.transpose(banks(7)[:, P * h:P * (h + 1)], heads4(ku)[:, h, :], ident)
                ins.then_inc(ku_tr, 1)

            o3 = banks(4, 2).rearrange("p (h e) -> p h e", h=GH)

            def gla_within(i):
                d, t = i % 2, ORDER[i % 2][i // 2]
                if i >= 1:
                    pe.wait_ge(o_added, i)
                pe.wait_ge(am_done, i + 1)
                for h in range(GH):
                    mm(o3[:, h, :], attm[d][:, h, :], vv[:, t, GV * h:GV * (h + 1)], start=(h % 2 == 0), stop=True, skip_group_check=True)

            def gla_before(i):
                d = i % 2
                pe.wait_ge(qi_done, i + 1)
                if i >= 2:
                    pe.wait_ge(gs_new, 2 * (i - 1))
                for h in range(GH):
                    ins = mm(o3[:, h, :], qdec[d][:, h, :], S_gla[:, d, h, :], start=False, stop=True, skip_group_check=True)
                ins.then_inc(inter_mm, 1)

            def gla_state(i):
                d, t = i % 2, ORDER[i % 2][i // 2]
                pe.wait_ge(kut_done, i + 1)
                for h in range(GH):
                    if h % 2 == 0 and i >= 1:
                        pe.wait_ge(gs_new, 2 * i - 1 + h // 2)
                    ins = mm(banks(2 + h // 2)[:, GV * (h % 2):GV * (h % 2 + 1)], kutok[d][:, h, :], vv[:, t, GV * h:GV * (h + 1)],
                             start=True, stop=True)
                    if h % 2 == 1:
                        ins.then_inc(gu_mm, 1)

            pe.wait_ge(gw_in, 32)
            pe.wait_ge(g_zero, 2)
            gla_logits(0)
            modulation(*late_mods[0], 0)
            gla_logits(1)
            modulation_T(4, 0)
            pe.wait_ge(mod_add, 5)
            modulation(*late_mods[1], 0)
            gla_logits(2)
            gla_scores(0)
            gla_keys(0)
            for i in range(2 * TT):
                gla_within(i)
                gla_before(i)
                if i + 1 < len(late_mods):
                    modulation_T(5 + i, 0)
                if i + 1 < 2 * TT:
                    gla_scores(i + 1)
                gla_state(i)
                if i + 1 < 2 * TT:
                    gla_keys(i + 1)
                if i + 3 < 2 * TT:
                    gla_logits(i + 3)
                if i + 2 < len(late_mods):
                    pe.wait_ge(mod_add, 6 + i)
                    modulation(*late_mods[i + 2], 0)
            for n, t in enumerate(FIN):
                pe.wait_ge(gg_done, n + 1)
                if n >= 2:
                    pe.wait_ge(gT_done, n - 1)
                else:
                    pe.wait_ge(o_added, 2 * TT)
                    pe.wait_ge(gs_new, 4 * TT)
                for k in range(KT):
                    ins = pe.transpose(banks(2 + 2 * (n % 2), 2)[:, P * k:P * (k + 1)], og[:, t, P * k:P * (k + 1)], ident)
                ins.then_inc(gT_tr, 1)
            for q in range(3):
                l, s = (0, q) if q < 2 else (1, 0)
                if q < 2:
                    pe.wait_ge(gT_done, TT - 1 + q)
                else:
                    pe.wait_ge(gr_done, 1)
                for k in range(KT):
                    ins = mm(banks(2 + 2 * (q % 2), 2)[:, P * k:P * (k + 1)], spread(mod[l][:, 16 + k, s], 1, P), ident, start=True, stop=True)
                ins.then_inc(gr_mm, 1)
            pe.wait_ge(gr_done, 3)
            pe.wait_ge(ys_lo_done, TT)
            pe.wait_ge(gT_done, TT)
            for n in range(4):
                if n >= 2:
                    pe.wait_ge(eo_done, TT * (n - 1))
                for half, (a_hi, a_lo) in enumerate(((ys_hi, ys_lo), (yg_hi, yg_lo))):
                    hi, lo = ready(eo_ch[2 * n + half])
                    for t in range(TT):
                        for k in range(KT):
                            for q, (a, w) in enumerate(((a_hi, hi), (a_hi, lo), (a_lo, hi))):
                                ins = mm(eo_out(n, t), a[:, t, k, :], w[:, k, :], start=(half + k + q == 0 and t % 2 == 0),
                                         stop=(half == 1 and k == KT - 1 and q == 2), skip_group_check=True)
                    ins.then_inc((eo_w, eo_mm)[half], 1)
            transpose_h(1)
            pe.wait_ge(h1_lo_done, 2 * KT)

            def rope_transpose(r):
                pe.wait_ge(rk_r, r + 1)
                if r >= 2:
                    pe.wait_ge(rk_done, r - 1)
                R = rp[r % 2][3]
                for h in range(2):
                    ins = pe.transpose(banks(2 + r % 2)[:, P * h:P * (h + 1)], heads2(R)[:, h, :], ident)
                ins.then_inc(rk_tr, 1)

            first = JOBS_E
            for j in range(JOBS_E, JOBS_Q + 2):
                if j < JOBS_Q:
                    kind, n, t = jobs[j]
                    if j - 2 >= first:
                        if jobs[j - 2][0] in ("k", "q"):
                            pe.wait_ge(rk_out, ropes.index(j - 2) + 1)
                        else:
                            pe.wait_ge(proj_dve, emptied(j - 2)[1])
                    token_parts(j, oin_ch[n], h1_hi, h1_lo)
                if j - 2 in ropes:
                    rope_transpose(ropes.index(j - 2))
            pe.wait_ge(rk_done, len(ropes))

            NA = LT * AH

            def scores(a):
                t, h = a // AH, a % AH
                kv = h // GRP
                lo, hi = max(t - 1, 0), min(t + 1, LT - 1)
                k0 = CTX + P * lo
                if a >= 2:
                    pe.wait_ge(mx_done, a - 1)
                b = banks(2 + 2 * (a % 2), 2)
                lhsT = qT[:, t, h, :]
                mm(b[:, 0:CTX], lhsT, kT[:, kv, 0:CTX], start=True, stop=True)
                ins = mm(b[:, CTX:CTX + 2 * P], lhsT, kT[:, kv, k0:k0 + 2 * P], start=True, stop=True)
                if hi - lo == 2:
                    ins = mm(b[:, CTX + 2 * P:CTX + 3 * P], lhsT, kT[:, kv, k0 + 2 * P:k0 + 3 * P], start=True, stop=True)
                ins.then_inc(s_mm, 1)

            def out_transpose(G):
                pe.wait_ge(on_done, G + 1)
                if G >= 1:
                    pe.wait_ge(ot_done, G)
                for h in range(GRP):
                    ins = pe.transpose(banks(1)[:, P * h:P * (h + 1)], heads4(onorm[G % 2])[:, h, :], ident)
                ins.then_inc(ot_tr, 1)

            scores(0)
            for a in range(NA + 1):
                if a + 1 < NA:
                    scores(a + 1)
                if a >= 1:
                    v = a - 1
                    t, h = v // AH, v % AH
                    kv = h // GRP
                    lo, hi = max(t - 1, 0), min(t + 1, LT - 1)
                    tiles = list(range(CT)) + [CT + b for b in range(lo, hi + 1)]
                    pe.wait_ge(pt_a, v + 1)
                    if len(tiles) == 5:
                        pe.wait_ge(pt_d, v + 1 - AH)
                    if v % GRP == 0 and v >= GRP:
                        pe.wait_ge(on_done, v // GRP)
                    for b, kt in enumerate(tiles):
                        ins = mm(banks(0)[:, AD * (v % GRP):AD * (v % GRP + 1)], probT[v % 2][:, b, :], va[:, kt, AD * kv:AD * (kv + 1)],
                                 start=(b == 0), stop=(b == len(tiles) - 1))
                    ins.then_inc(pv_mm, 1)
                if a < NA:
                    t = a // AH
                    nb = 5 if 0 < t < LT - 1 else 4
                    pe.wait_ge(p_done, a + 1)
                    for b in range(nb):
                        ins = pe.transpose(banks(6, 2)[:, P * b:P * (b + 1)], prob[a % 2][:, P * b:P * (b + 1)], ident)
                    ins.then_inc(p_tr, 1)
                if a >= 1 and (a - 1) % GRP == 1 and a - 1 >= GRP:
                    out_transpose((a - 1) // GRP - 1)
            out_transpose(LT * AKV - 1)
            for m in range(AH):
                if m < 2:
                    pe.wait_ge(on_done, LT * AKV)
                    pe.wait_ge(ot_done, LT * AKV)
                else:
                    pe.wait_ge(proj_act, emptied(JOBS_Q + m - 2)[1])
                feature_parts(JOBS_Q + m, oin_ch[12 + m // 2], m % 2, 1, h1_hi, h1_lo)
            pe.wait_ge(proj_act, emptied(len(jobs) - 1)[1])
            pe.wait_ge(pt_a, NA)
            pe.wait_ge(mx_done, NA)
            for n in range(4):
                for half in range(2):
                    hi, lo = ready(oo_ch[2 * n + half])
                    for t in range(LT):
                        for k in range(KT):
                            m = KT * half + k
                            if n == 0 and t == 0:
                                pe.wait_ge(o_lo_done, m + 1)
                            for q, (a, w) in enumerate(((o_hi, hi), (o_hi, lo), (o_lo, hi))):
                                ins = mm(oo_out(n, t), a[t][:, m, :], w[:, k, :], start=(m + q == 0 and t % 2 == 0),
                                         stop=(m == 2 * KT - 1 and q == 2), skip_group_check=True)
                    ins.then_inc((oo_w, oo_mm)[half], 1)


def constants():
    import numpy as np
    k = np.arange(P)
    a, b = k[:, None], k[None, :]
    tiles = [a == b, a <= b, a > b, a >= b, a < b, np.ones((P, P))]
    keep = np.ones((P, NB))
    keep[:, ::HALF] = 0
    consts = np.concatenate([np.asarray(m, np.float32) for m in tiles] + [keep.astype(np.float32)], axis=1)
    zero = np.zeros((P, P), np.float32)
    before = np.where(b >= a, 0, -NEG).astype(np.float32)
    after = np.where(b <= a, 0, -NEG).astype(np.float32)
    masks = np.concatenate([zero, zero, zero, after, zero, zero, before, zero, after], axis=1)
    grid, freqs, base = 64, AD // 4, 10000.0
    rows = LAT // grid
    row = np.repeat(np.arange(rows, dtype=np.float32), grid)
    col = np.tile(np.arange(grid, dtype=np.float32), rows)
    inv = (np.float32(1.0) / (np.float32(base) ** (np.arange(freqs, dtype=np.float32) / np.float32(freqs)))).astype(np.float32)
    ang = np.stack([row[:, None] * inv, col[:, None] * inv], axis=1).astype(np.float32)
    cos, sin = np.cos(ang), np.sin(ang)
    cc = np.stack([cos, cos], axis=2).reshape(LAT, AD)
    ss = np.stack([sin, -sin], axis=2).reshape(LAT, AD)
    return consts, masks, np.stack([cc, ss]).astype(np.float32)


_INS = ['x', 'c', 'ctx', 'c_ctx', 'e_norm', 'e_mod_w', 'e_mod_b', 'e_w_in', 'e_conv_w', 'e_conv_b', 'e_dt_bias', 'e_a_log',
        'e_d_skip', 'e_ssd_norm', 'e_gla_gate_w', 'e_gla_gate_b', 'e_gla_norm', 'e_w_out', 'o_norm', 'o_mod_w', 'o_mod_b',
        'o_w_in', 'o_q_norm', 'o_k_norm', 'o_sink', 'o_w_out']


def kernel(**inputs):
    import numpy as np
    import concourse.bacc as bacc
    from concourse.bass_utils import run_bass_kernel_spmd

    nc = bacc.Bacc("TRN2", target_bir_lowering=False, num_devices=1)
    arrays, args = {}, []
    extra = dict(zip(("consts", "masks", "rope"), constants()))
    for name in _INS + list(extra):
        a = np.ascontiguousarray(extra[name] if name in extra else inputs[name])
        arrays[f"in_{name}"] = a
        args.append(nc.dram_tensor(f"in_{name}", a.shape, mybir.dt.from_np(a.dtype), kind="ExternalInput").ap())
    args.append(nc.dram_tensor("out_x", (1, LAT, DM), mybir.dt.float32, kind="ExternalOutput").ap())
    even_odd_layers(nc, *args)
    r = run_bass_kernel_spmd(nc, [arrays], core_ids=[0])
    return r.results[0]["out_x"]
```
